# Optimizing a Trainium2 kernel written in Bass

```python
import math
import jax, jax.numpy as jnp
from jax import lax
import numpy as np

D_MODEL = 2048
BATCH = 1
SEQ = 256
DEPTH = 1

MIX_WIDTH = D_MODEL
RWKV_WIDTH = MIX_WIDTH // 2
RWKV_HEAD_DIM = 64
RWKV_HEADS = RWKV_WIDTH // RWKV_HEAD_DIM
DECAY_LORA = max(32, int(round(1.8 * RWKV_WIDTH ** 0.5 / 32)) * 32)
AAA_LORA = max(32, int(round(1.8 * RWKV_WIDTH ** 0.5 / 32)) * 32)
GATE_LORA = max(32, int(round(0.6 * RWKV_WIDTH ** 0.8 / 32)) * 32)
RWKV_COLS = 3 * RWKV_WIDTH + DECAY_LORA + AAA_LORA + GATE_LORA
DIFF_WIDTH = MIX_WIDTH - RWKV_WIDTH
DIFF_HEAD_DIM = 64
DIFF_V_DIM = 2 * DIFF_HEAD_DIM
DIFF_HEADS = DIFF_WIDTH // DIFF_V_DIM
DIFF_COLS = 3 * DIFF_WIDTH
IN_COLS = RWKV_COLS + DIFF_COLS
D_FF = 4 * D_MODEL
ROPE_THETA = 10000.0
Q_BLOCK = 128
LN_EPS = 1e-5
RWKV_GN_EPS = 64e-5
SUBLN_EPS = 1e-5
DEEPNORM_ALPHA = (2 * DEPTH) ** 0.25
DEEPNORM_BETA = (8 * DEPTH) ** -0.25

kernel_name = "hymba_rwkv7_diffattn_deepnorm"

def _layer_norm(x, gain, bias):
    xf = x.astype(jnp.float32)
    mean = xf.mean(-1, keepdims=True)
    var = jnp.square(xf - mean).mean(-1, keepdims=True)
    return ((xf - mean) * lax.rsqrt(var + LN_EPS) * gain + bias).astype(x.dtype)

def _token_shift(p):
    return jnp.pad(p, ((0, 0), (1, 0), (0, 0)))[:, :-1]

def _rwkv7_mixer(proj, mu, w0, w_up, a0, a_up, g_up, k_k, k_a, r_k, gn_gain, gn_bias):
    B, S, _ = proj.shape
    H, N = RWKV_HEADS, RWKV_HEAD_DIM
    p = proj.astype(jnp.float32)
    mixed = p + (_token_shift(p) - p) * mu
    splits = [RWKV_WIDTH, 2 * RWKV_WIDTH, 3 * RWKV_WIDTH,
              3 * RWKV_WIDTH + DECAY_LORA, 3 * RWKV_WIDTH + DECAY_LORA + AAA_LORA]
    r, k, v, w_d, a_d, g_d = jnp.split(mixed, splits, axis=-1)
    w = -jax.nn.softplus(-(w0 + jnp.tanh(w_d) @ w_up)) - 0.5
    decay = jnp.exp(-jnp.exp(w))
    a = jax.nn.sigmoid(a0 + a_d @ a_up)
    g = jax.nn.sigmoid(g_d) @ g_up
    heads = lambda t: t.reshape(B, S, H, N)
    kk = heads(k * k_k)
    kk = kk / jnp.maximum(jnp.sqrt(jnp.sum(jnp.square(kk), -1, keepdims=True)), 1e-12)
    k = k * (1.0 + (a - 1.0) * k_a)
    r_h, k_h, v_h, w_h, a_h = heads(r), heads(k), heads(v), heads(decay), heads(a)

    def step(state, inp):
        r_t, w_t, k_t, v_t, kk_t, a_t = inp
        sa = jnp.einsum('bhij,bhj->bhi', state, -kk_t)
        state = (state * w_t[..., None, :]
                 + sa[..., :, None] * (kk_t * a_t)[..., None, :]
                 + v_t[..., :, None] * k_t[..., None, :])
        return state, jnp.einsum('bhij,bhj->bhi', state, r_t)

    xs = tuple(jnp.moveaxis(t, 1, 0) for t in (r_h, w_h, k_h, v_h, kk, a_h))
    _, y = lax.scan(step, jnp.zeros((B, H, N, N), jnp.float32), xs)
    y = jnp.moveaxis(y, 0, 1)
    mean = y.mean(-1, keepdims=True)
    var = jnp.square(y - mean).mean(-1, keepdims=True)
    y = ((y - mean) * lax.rsqrt(var + RWKV_GN_EPS)).reshape(B, S, RWKV_WIDTH) * gn_gain + gn_bias
    bonus = (jnp.sum(r_h * k_h * r_k, -1, keepdims=True) * v_h).reshape(B, S, RWKV_WIDTH)
    return ((y + bonus) * g).astype(proj.dtype)

def _rotary_tables(positions):
    inv_freq = ROPE_THETA ** (-jnp.arange(0, DIFF_HEAD_DIM, 2, dtype=jnp.float32) / DIFF_HEAD_DIM)
    ang = positions.astype(jnp.float32)[..., None] * inv_freq
    return jnp.cos(ang)[:, :, None, None, :], jnp.sin(ang)[:, :, None, None, :]

def _apply_rotary(t, cos, sin):
    t1, t2 = jnp.split(t.astype(jnp.float32), 2, axis=-1)
    return jnp.concatenate([t1 * cos - t2 * sin, t2 * cos + t1 * sin], -1)

def _diff_attention(proj, cos, sin, lq1, lk1, lq2, lk2, subln_gain, lambda_init):
    B, S, _ = proj.shape
    H, d = DIFF_HEADS, DIFF_HEAD_DIM
    q, k, v = jnp.split(proj, [DIFF_WIDTH, 2 * DIFF_WIDTH], axis=-1)
    q = _apply_rotary(q.reshape(B, S, H, 2, d), cos, sin).transpose(0, 2, 3, 1, 4)
    k = _apply_rotary(k.reshape(B, S, H, 2, d), cos, sin).transpose(0, 2, 3, 1, 4)
    v = v.reshape(B, S, H, DIFF_V_DIM).transpose(0, 2, 1, 3).astype(jnp.float32)
    lam = (jnp.exp(jnp.sum(lq1.astype(jnp.float32) * lk1))
           - jnp.exp(jnp.sum(lq2.astype(jnp.float32) * lk2)) + lambda_init)
    scale = d ** -0.5
    key_pos = jnp.arange(S)

    def query_block(i):
        start = i * Q_BLOCK
        qb = lax.dynamic_slice_in_dim(q, start, Q_BLOCK, axis=3)
        s = jnp.einsum('bhcqd,bhckd->bhcqk', qb, k) * scale
        q_pos = start + jnp.arange(Q_BLOCK)
        s = jnp.where(key_pos[None, :] <= q_pos[:, None], s, -1e30)
        p = jax.nn.softmax(s, axis=-1)
        attn = p[:, :, 0] - lam * p[:, :, 1]
        return jnp.einsum('bhqk,bhkd->bhqd', attn, v)

    out = lax.map(query_block, jnp.arange(S // Q_BLOCK))
    out = out.transpose(1, 0, 3, 2, 4).reshape(B, S, H, DIFF_V_DIM)
    out = out * lax.rsqrt(jnp.square(out).mean(-1, keepdims=True) + SUBLN_EPS) * subln_gain
    out = out * (1.0 - lambda_init)
    return out.reshape(B, S, DIFF_WIDTH).astype(proj.dtype)

def setup_inputs(seed: int = 0) -> dict:
    key = jax.random.key(seed)
    ks = jax.random.split(key, 26)
    L = DEPTH

    def nrm(k, shape, scale):
        return jax.random.normal(k, shape, jnp.float32) * scale

    col_scale = np.ones((IN_COLS,), np.float32)
    col_scale[2 * RWKV_WIDTH:3 * RWKV_WIDTH] = DEEPNORM_BETA
    col_scale[RWKV_COLS + 2 * DIFF_WIDTH:] = DEEPNORM_BETA
    x = nrm(ks[0], (BATCH, SEQ, D_MODEL), 1.0)
    positions = jnp.tile(jnp.arange(SEQ, dtype=jnp.int32)[None, :], (BATCH, 1))
    w_in = nrm(ks[1], (L, D_MODEL, IN_COLS), D_MODEL ** -0.5) * jnp.asarray(col_scale)
    mu_shift = jax.random.uniform(ks[2], (L, RWKV_COLS), jnp.float32)
    rwkv_w0 = jax.random.uniform(ks[3], (L, RWKV_WIDTH), jnp.float32, -6.5, -1.5)
    rwkv_w_up = nrm(ks[4], (L, DECAY_LORA, RWKV_WIDTH), 0.5 * DECAY_LORA ** -0.5)
    rwkv_a0 = nrm(ks[5], (L, RWKV_WIDTH), 0.5)
    rwkv_a_up = nrm(ks[6], (L, AAA_LORA, RWKV_WIDTH), AAA_LORA ** -0.5)
    rwkv_g_up = nrm(ks[7], (L, GATE_LORA, RWKV_WIDTH), GATE_LORA ** -0.5)
    rwkv_k_k = 0.85 + nrm(ks[8], (L, RWKV_WIDTH), 0.05)
    rwkv_k_a = 1.0 + nrm(ks[9], (L, RWKV_WIDTH), 0.05)
    rwkv_r_k = nrm(ks[10], (L, RWKV_HEADS, RWKV_HEAD_DIM), 0.1)
    rwkv_gn_gain = 1.0 + nrm(ks[11], (L, RWKV_WIDTH), 0.05)
    rwkv_gn_bias = nrm(ks[12], (L, RWKV_WIDTH), 0.02)
    diff_lambda_q1 = nrm(ks[13], (L, DIFF_HEAD_DIM), 0.1)
    diff_lambda_k1 = nrm(ks[14], (L, DIFF_HEAD_DIM), 0.1)
    diff_lambda_q2 = nrm(ks[15], (L, DIFF_HEAD_DIM), 0.1)
    diff_lambda_k2 = nrm(ks[16], (L, DIFF_HEAD_DIM), 0.1)
    diff_subln_gain = 1.0 + nrm(ks[17], (L, DIFF_V_DIM), 0.05)
    w_out = nrm(ks[18], (L, MIX_WIDTH, D_MODEL), MIX_WIDTH ** -0.5 * DEEPNORM_BETA)
    ln1_gain = 1.0 + nrm(ks[19], (L, D_MODEL), 0.05)
    ln1_bias = nrm(ks[20], (L, D_MODEL), 0.02)
    w_ff1 = nrm(ks[21], (L, D_MODEL, D_FF), D_MODEL ** -0.5 * DEEPNORM_BETA)
    w_ff2 = nrm(ks[22], (L, D_FF, D_MODEL), D_FF ** -0.5 * DEEPNORM_BETA)
    ln2_gain = 1.0 + nrm(ks[23], (L, D_MODEL), 0.05)
    ln2_bias = nrm(ks[24], (L, D_MODEL), 0.02)
    return {
        'x': x, 'positions': positions, 'w_in': w_in, 'mu_shift': mu_shift,
        'rwkv_w0': rwkv_w0, 'rwkv_w_up': rwkv_w_up, 'rwkv_a0': rwkv_a0, 'rwkv_a_up': rwkv_a_up,
        'rwkv_g_up': rwkv_g_up, 'rwkv_k_k': rwkv_k_k, 'rwkv_k_a': rwkv_k_a, 'rwkv_r_k': rwkv_r_k,
        'rwkv_gn_gain': rwkv_gn_gain, 'rwkv_gn_bias': rwkv_gn_bias,
        'diff_lambda_q1': diff_lambda_q1, 'diff_lambda_k1': diff_lambda_k1,
        'diff_lambda_q2': diff_lambda_q2, 'diff_lambda_k2': diff_lambda_k2,
        'diff_subln_gain': diff_subln_gain, 'w_out': w_out,
        'ln1_gain': ln1_gain, 'ln1_bias': ln1_bias, 'w_ff1': w_ff1, 'w_ff2': w_ff2,
        'ln2_gain': ln2_gain, 'ln2_bias': ln2_bias,
    }

def reference(x, positions, w_in, mu_shift, rwkv_w0, rwkv_w_up, rwkv_a0, rwkv_a_up,
              rwkv_g_up, rwkv_k_k, rwkv_k_a, rwkv_r_k, rwkv_gn_gain, rwkv_gn_bias,
              diff_lambda_q1, diff_lambda_k1, diff_lambda_q2, diff_lambda_k2,
              diff_subln_gain, w_out, ln1_gain, ln1_bias, w_ff1, w_ff2, ln2_gain, ln2_bias):
    cos, sin = _rotary_tables(positions)
    for l in range(DEPTH):
        lambda_init = 0.8 - 0.6 * math.exp(-0.3 * l)
        proj = x @ w_in[l]
        y_rwkv = _rwkv7_mixer(proj[..., :RWKV_COLS], mu_shift[l], rwkv_w0[l], rwkv_w_up[l],
                              rwkv_a0[l], rwkv_a_up[l], rwkv_g_up[l], rwkv_k_k[l], rwkv_k_a[l],
                              rwkv_r_k[l], rwkv_gn_gain[l], rwkv_gn_bias[l])
        y_diff = _diff_attention(proj[..., RWKV_COLS:], cos, sin, diff_lambda_q1[l],
                                 diff_lambda_k1[l], diff_lambda_q2[l], diff_lambda_k2[l],
                                 diff_subln_gain[l], lambda_init)
        mix = jnp.concatenate([y_rwkv, y_diff], axis=-1) @ w_out[l]
        x = _layer_norm(DEEPNORM_ALPHA * x + mix, ln1_gain[l], ln1_bias[l])
        h = jnp.square(jax.nn.relu(x @ w_ff1[l])) @ w_ff2[l]
        x = _layer_norm(DEEPNORM_ALPHA * x + h, ln2_gain[l], ln2_bias[l])
    return x


_drawn_inputs = setup_inputs


def setup_inputs(seed=0):
    import zlib

    import numpy as np

    out = dict(_drawn_inputs(seed))
    spreads = {}
    factors = {'rwkv_w_up': 8.0,
     'rwkv_k_k': 29.387,
     'rwkv_k_a': 5.435,
     'rwkv_gn_gain': 6.133,
     'rwkv_gn_bias': 28.647,
     'diff_lambda_q1': 3.738,
     'diff_lambda_k1': 5.661,
     'diff_lambda_q2': 3.682,
     'diff_lambda_k2': 5.097,
     'diff_subln_gain': 4.336,
     'ln1_bias': 2.854,
     'ln2_bias': 2.838}
    for name, (base, spread) in spreads.items():
        noise = np.random.default_rng([zlib.crc32(name.encode()), seed]).standard_normal(out[name].shape)
        drawn = base * np.exp(spread * noise) if base else spread * noise
        out[name] = __import__('jax').numpy.asarray(drawn.astype(out[name].dtype))
    for name, factor in factors.items():
        out[name] = (out[name] * factor).astype(out[name].dtype)
    return out
```

```python
import math
from contextlib import ExitStack

import numpy as np

import concourse.bass as bass
from concourse import mybir

ALU = mybir.AluOpType
ACT = mybir.ActivationFunctionType
F32 = mybir.dt.float32
F32R = mybir.dt.float32r
I32 = mybir.dt.int32
AX_X = mybir.AxisListType.X

P = 128
D = 2048
S = 256
TT_ = S // P
DFF = 4 * D
RW = D // 2
HD = 64
NB = RW // P
DH = 8
KT = D // P
C = 64
NC = S // C
LORA_W, LORA_A, LORA_G = 64, 64, 160
RCOLS = 3 * RW + LORA_W + LORA_A + LORA_G
ALPHA = 2.0 ** 0.25
LAMBDA_INIT = 0.8 - 0.6 * math.exp(-0.3 * 0)
LN_EPS, GN_EPS, SUB_EPS = 1e-5, 64e-5, 1e-5
DECAY = math.exp(-0.5)
NEG = -1e30
UNITS = 32

SLAB = 2048
G_LORA, N_LORA = 0, 3
G_KRV = G_LORA + N_LORA
N_KRV = 12
G_QK = G_KRV + 2 * N_KRV
N_QK = 8
G_VD = G_QK + 2 * N_QK
G_OUT = G_VD + 8
G_FF1 = G_OUT + KT
N_FF1 = DFF // 256
G_FF2 = G_FF1 + 2 * N_FF1
G_END = G_FF2 + DFF // P
NST, NHL = 4, 2

V_MU, V_KK, V_KA, V_RK, V_A0, V_GG, V_GB, V_SG, V_INVF, V_SIGN, V_GNEPS, V_SUBEPS, V_LNEPS = (
    0, 27, 35, 43, 51, 59, 67, 75, 76, 77, 78, 79, 80)
V_IN = 81
V_OMMU, V_OMKA, V_G08 = 81, 108, 116
V_ALL = 120

C_SU, C_IU, C_SL, C_ID, C_BD, C_ONE = 0, 128, 256, 384, 512, 640
C_SMALL = 768
C_LEV, C_M1T = 768, 768 + 6 * 128
C_ATT = C_M1T + 128
C_ALL = C_ATT + 384


def shape_constants():
    p, q = np.arange(P)[:, None], np.arange(P)[None, :]
    same = p // C == q // C
    out = np.zeros((P, C_ALL), np.float32)
    out[:, C_SU:C_SU + P] = same & (p < q)
    out[:, C_IU:C_IU + P] = same & (p <= q)
    out[:, C_SL:C_SL + P] = same & (q < p)
    out[:, C_ID:C_ID + P] = p == q
    out[:, C_BD:C_BD + P] = same
    out[:, C_ONE:C_ONE + P] = 1.0
    for n in range(6):
        m = 1 << n
        lev = (p // (2 * m) == q // (2 * m)) & (p // m % 2 == 1) & (q // m % 2 == 0)
        out[:, C_LEV + n * P:C_LEV + (n + 1) * P] = lev
        if n == 0:
            out[:, C_M1T:C_M1T + P] = lev.T
    causal = np.where(q > p, NEG, 0.0)
    out[:, C_ATT:C_ATT + P] = causal
    out[:, C_ATT + 2 * P:C_ATT + 3 * P] = causal
    return out


def build(nc, t):
    ctx = ExitStack()
    with ctx:
        BASE, SL_BYTES = 16512, 8192
        SMALL = BASE + 25 * SL_BYTES

        def at(name, slot, shape, dtype=F32, byte=0):
            return nc.alloc_sbuf_tensor_at(name, shape, dtype, offset=BASE + slot * SL_BYTES + byte)

        def small(name, col, shape, dtype=F32):
            return nc.alloc_sbuf_tensor_at(name, shape, dtype, offset=SMALL + 4 * col)

        def sem(name):
            return ctx.enter_context(nc.semaphore(name))

        stage = [at(f"stage{i}", i, [P, SLAB]) for i in range(NST)]
        whi = [at(f"whi{i}", 4 + i, [P, SLAB], F32R) for i in range(NHL)]
        wlo = [at(f"wlo{i}", 6 + i, [P, SLAB], F32R) for i in range(NHL)]
        acthi = at("acthi", 8, [P, KT, S], F32R)
        actlo = at("actlo", 10, [P, KT, S], F32R)
        wup = at("wup", 12, [65, RW])
        aup = at("aup", 12, [P, RW], byte=4096)
        sig = at("sig", 13, [P, TT_, RW])
        kr = at("kr", 14, [P, NB, TT_, 2, P])
        e2 = at("e2", 16, [P, NB, S])
        bt = at("bt", 17, [P, NB, S])
        krv = at("krv", 18, [P, 3 * NB, S])
        ki = at("ki", 21, [P, NB, S])
        qk = at("qk", 22, [P, 2 * DH, S])
        xstage = at("xstage", 22, [P, KT, S])
        vd = at("vd", 24, [P, TT_, RW])
        cosb = at("cosb", 24, [P, S])
        sinb = at("sinb", 24, [P, S], byte=1024)
        angt = [at(f"angt{i}", 24, [P, S], byte=2048 + 1024 * i) for i in range(3)]
        posi = at("posi", 24, [P, S], I32, byte=5120)
        rot = [at(f"rot{i}", 12, [P, 2, S], byte=2048 * i) for i in range(2)]
        sqt = at("sqt", 13, [P, 2, S])
        inv = at("inv", 13, [P, 2, S], byte=2048)
        rkt_ = at("rkt_", 13, [P, 2, S], byte=4096)
        yt = at("yt", 12, [P, KT, S])
        amask = at("amask", 8, [P, 3 * P])
        sm = [at(f"sm{i}", 8, [P, 2, 3 * P], byte=2048 + 3072 * i) for i in range(2)]
        pr = [at(f"pr{i}", 9, [P, 2, 3 * P], byte=3072 * i) for i in range(2)]
        att = at("att", 9, [P, 3 * P], byte=6144)
        lamv = at("lamv", 10, [P, 4, HD])
        lamt = at("lamt", 10, [P, 2, HD], byte=1024)
        attT = at("attT", 10, [P, 3 * P], byte=2048)
        osq = at("osq", 10, [P, 2, S], byte=4096)
        oinv = at("oinv", 10, [P, 2, S], byte=6144)
        AT = at("AT", 8, [P, 16, P])
        TM = at("TM", 9, [P, 16, P])
        XM = at("XM", 10, [P, 16, P])
        levc = at("levc", 11, [P, 7, P])
        TTm = at("TTm", 22, [P, UNITS, P])
        kbt = [at(f"kbt{i}", 8, [P, 8, P], byte=4096 * i) for i in range(2)]
        vtm = at("vtm", 9, [P, NB, TT_, P])
        btm = at("btm", 10, [P, NB, TT_, P])
        ktm = at("ktm", 24, [P, NB, TT_, P])
        z1 = at("z1", 16, [P, NB, TT_, P])
        um = at("um", 18, [P, NB, TT_, P])
        st = [None, at("st1", 8, [P, NB, P]), at("st2", 8, [P, NB, P], byte=4096), at("st3", 11, [P, NB, P])]
        gm = [at("gm0", 20, [P, NB, P]), at("gm1", 20, [P, NB, P], byte=4096), at("gm2", 11, [P, NB, P], byte=4096)]
        rbt = [at(f"rbt{i}", 22, [P, 8, P], byte=4096 * i) for i in range(2)]
        rkt = [at(f"rkt{i}", 23, [P, 8, P], byte=4096 * i) for i in range(2)]
        yf = at("yf", 16, [P, NB, S])
        gup = at("gup", 10, [P, 2, RW])
        gsq = [at(f"gsq{i}", 24, [P, 2, S], byte=2048 * i) for i in range(2)]
        ginv = [at(f"ginv{i}", 24, [P, 2, S], byte=4096 + 2048 * i) for i in range(2)]
        xres = at("xres", 22, [P, TT_, D])
        gain1 = at("gain1", 14, [P, D])
        bias1 = at("bias1", 15, [P, D])
        hid = at("hid", 14, [P, DFF // P, S])
        gain2 = at("gain2", 12, [P, D])
        bias2 = at("bias2", 13, [P, D])
        cst = small("cst", 0, [P, C_SMALL])
        vec = small("vec", 768, [P, V_ALL])
        wt = small("wt", 888, [65, S])
        wa = small("wa", 888 + 256, [P, S])
        sg = [small(f"sg{i}", 888 + 512 + 256 * i, [P, S]) for i in range(2)]
        shi = [small(f"shi{i}", 888 + 256 * i, [P, S], F32R) for i in range(2)]
        slo = [small(f"slo{i}", 888 + 512 + 256 * i, [P, S], F32R) for i in range(2)]
        gam = small("gam", 1912, [P, NB, NC])
        mx = small("mx", 1944, [P, 2, 4])
        nmx = small("nmx", 1952, [P, 2, 4])
        sums = small("sums", 1960, [P, 2, 4])
        coef = small("coef", 1968, [P, 2, 4])
        lam = small("lam", 1976, [P, 4])
        stats = small("stats", 1984, [P, 4, 6])
        moments = small("moments", 2008, [P, 4])
        mv, rstd = moments[:, 0:2], moments[:, 2:3]

        ps = ctx.enter_context(nc.psum_tensor("ps", [P, 8, 512], F32))

        s_stage = [sem(f"stage_loaded{i}") for i in range(NST)]
        s_hi, s_lo, s_used = sem("hi_ready"), sem("lo_ready"), sem("slab_used")
        s_free, s_mix = sem("acc_free"), sem("mix_scaled")
        s_x = [sem(f"x_loaded{i}") for i in range(4)]
        s_xhi, s_xlo = sem("act_hi_ready"), sem("act_lo_ready")
        s_cst, s_pos, s_attc, s_levc, s_gup = (
            sem("consts_loaded"), sem("positions_loaded"), sem("attention_consts_loaded"),
            sem("level_masks_loaded"), sem("gate_up_loaded"))
        s_ln1c, s_ln2c, s_xres, s_out = (
            sem("ln1_vectors_loaded"), sem("ln2_vectors_loaded"), sem("x_reloaded"), sem("output_stored"))
        s_vec, s_lup = sem("vectors_ready"), sem("lora_weights_loaded")
        s_lora, s_z, s_sig = sem("lora_activated"), sem("decay_logits"), sem("decay_sigmoid")
        s_item, s_itemd, s_gam = sem("rate_or_cumsum"), sem("rate_or_cumsum_done"), sem("chunk_decay_kept")
        s_ang, s_sin, s_tab = sem("angle_step"), sem("sines_ready"), sem("rotary_tables_ready")
        s_rotc, s_rotm, s_rotd = sem("rot_copied"), sem("rot_multiplied"), sem("rotary_done")
        s_sq, s_ss, s_nrm = sem("kk_squares"), sem("kk_sums"), sem("kk_norms")
        s_ew = sem("elementwise_step")
        s_rk, s_bon, s_kk, s_pl = sem("bonus_terms"), sem("bonus_sums"), sem("kk_ready"), sem("pool_step")
        s_vdc = sem("v_copied")
        s_lamd = sem("lambda_step")
        s_lame = sem("lambda_exps")
        s_sc, s_smd, s_exp, s_at, s_atc, s_o, s_oc = (
            sem("scores_ready"), sem("masked_scores_ready"), sem("probs_ready"), sem("attention_transposed"),
            sem("attention_T_copied"), sem("head_out"), sem("head_out_copied"))
        s_attn, s_attd = sem("attention_ready"), sem("attention_step")
        s_osq, s_oss, s_ord, s_yd, s_ydn = (
            sem("out_squares"), sem("out_sums"), sem("out_roots"), sem("diff_step"), sem("diff_out_ready"))
        s_ini, s_inia, s_init, s_init0 = (
            sem("chunk_products"), sem("chunk_masked"), sem("first_level_ready"), sem("first_level_masked"))
        s_px, s_xm, s_ptx, s_upd = sem("level_x"), sem("level_x_masked"), sem("level_products"), sem("level_done")
        s_tr, s_trc = sem("transposed"), sem("transposed_copied")
        s_kb, s_kbm, s_z1p, s_z1 = sem("kb_products"), sem("kb_masked"), sem("z1_products"), sem("z1_ready")
        s_gm = sem("state_decay_masks")
        s_ks, s_zc, s_u, s_uc, s_sp, s_stm, s_st = (
            sem("state_term"), sem("z_ready"), sem("u_products"), sem("u_ready"), sem("state_products"),
            sem("state_sum"), sem("state_ready"))
        s_rb, s_rbm, s_y, s_yc = sem("read_products"), sem("read_masked"), sem("y_products"), sem("y_copied")
        s_mean, s_cen, s_gsq, s_var, s_sd, s_gn, s_gate, s_yg = (
            sem("gn_means"), sem("gn_centred"), sem("gn_squares"), sem("gn_vars"), sem("gn_roots"),
            sem("gn_step"), sem("gate_ready"), sem("rwkv_out_ready"))
        s_ahi, s_alo = sem("moving_hi_ready"), sem("moving_lo_ready")
        s_ln, s_std, s_lnd, s_lnk = sem("ln_moments"), sem("ln_roots"), sem("ln_done"), sem("ln_chain")
        s_xt, s_x1h, s_x1l = sem("x1_transposed"), sem("x1_hi"), sem("x1_lo")
        s_relu, s_ff = sem("relu_ready"), sem("hidden_ready")

        block = ctx.enter_context(nc.Block())

        def col(v, n=0):
            return vec[:, v + n:v + n + 1]

        def vcol(v, blk):
            return vec[:, bass.ds(blk + v, 1)]

        def over(ap, n):
            return ap.unsqueeze(1).broadcast_to([ap.shape[0], n, ap.shape[1]])

        def f(ap):
            return ap.bitcast(F32)

        SU, IU, ID = cst[:, C_SU:C_SU + P], cst[:, C_IU:C_IU + P], cst[:, C_ID:C_ID + P]
        BD, ONE = cst[:, C_BD:C_BD + P], cst[:, C_ONE:C_ONE + P]
        M1, M1T = levc[:, 0, :], levc[:, 6, :]

        def banks(a, n=2, lo=0, hi=512):
            return ps[:, a:a + n, lo:hi]

        def units(g):
            return [(hp * 4 + b2 * 2 + a, hp, 2 * g + b2, a) for hp in range(2) for b2 in range(2) for a in range(TT_)]

        def unit(b, hp, a):
            return (b // 2) * 8 + hp * 4 + (b % 2) * 2 + a

        def hr(hp):
            return slice(HD * hp, HD * hp + HD)

        def tok(a):
            return slice(P * a, P * a + P)

        @block.sync
        def _(sp):
            sp.dma_start(cst[:, :], t["consts"][:, 0:C_SMALL]).then_inc(s_cst, 16)
            sp.dma_start(vec[:, 0:V_IN], t["vecs"]).then_inc(s_cst, 16)
            for j in range(4):
                sp.dma_start(xstage[:, 4 * j:4 * j + 4, :], t["xT"][:, 4 * j:4 * j + 4, :]).then_inc(s_x[j], 16)

            def slab(n, k, src):
                if not (isinstance(n, int) and n < NST):
                    sp.wait_ge(s_lo, n - (NST - 1))
                sp.dma_start(stage[k % NST][:, :], src).then_inc(s_stage[k % NST], 16)

            def slabs(base, first, last, src):
                with sp.Fori(first, last) as i:
                    for k in range(4):
                        slab(i * 4 + (base + k), base + k, src[bass.ds(i * 4 + k, 1), :, :])

            for g in range(4):
                slab(g, g, t["w_in"][g])
                if g == 1:
                    sp.dma_start(wup[:, :], t["w_up"]).then_inc(s_lup, 16)
                    sp.dma_start(aup[64:128, :], t["a_up"]).then_inc(s_lup, 16)
                    sp.dma_start(posi[:, :], t["positions"].partition_broadcast(P)).then_inc(s_pos, 16)
            slabs(4, 0, (G_OUT - 4) // 4, t["w_in"][4:, :, :])
            for g in range(G_OUT // 4 * 4, G_OUT):
                slab(g, g, t["w_in"][g])
            sp.wait_ge(s_used, G_OUT)
            sp.dma_start(amask[:, :], t["consts"][:, C_ATT:C_ATT + 3 * P]).then_inc(s_attc, 16)
            for j in range(4):
                sp.dma_start(lamv[:, j, :], t["lam"][j:j + 1, :].partition_broadcast(P)).then_inc(s_attc, 16)
            sp.dma_start(levc[:, :, :], t["consts"][:, C_LEV:C_LEV + 7 * P].rearrange("p (l q) -> p l q", l=7)
                         ).then_inc(s_levc, 16)
            for g in range(G_OUT, G_OUT + 4):
                slab(g, g, t["w_out"][g - G_OUT])
            sp.wait_ge(s_sp, 2 * (NC - 1))
            sp.dma_start(gup[:, :, :], t["g_up"]).then_inc(s_gup, 16)
            sp.wait_ge(s_y, 4)
            sp.dma_start(xres[:, :, :], t["x"].rearrange("(a p) d -> p a d", p=P)).then_inc(s_xres, 16)
            sp.dma_start(gain1[:, :], t["ln1_gain"].partition_broadcast(P)).then_inc(s_ln1c, 16)
            sp.dma_start(bias1[:, :], t["ln1_bias"].partition_broadcast(P)).then_inc(s_ln1c, 16)
            slabs(G_OUT + 4, 0, KT // 4 - 1, t["w_out"][4:, :, :])
            slabs(G_FF1, 0, N_FF1 // 2, t["w_ff1"])
            sp.dma_start(gain2[:, :], t["ln2_gain"].partition_broadcast(P)).then_inc(s_ln2c, 16)
            sp.dma_start(bias2[:, :], t["ln2_bias"].partition_broadcast(P)).then_inc(s_ln2c, 16)
            slabs(G_FF2, 0, DFF // P // 4, t["w_ff2"])
            for a in range(TT_):
                sp.wait_ge(s_lnd, TT_ + a + 1)
                sp.dma_start(t["out"][a * P:(a + 1) * P, :], xres[:, a, :]).then_inc(s_out, 16)
            sp.wait_ge(s_out, 16 * TT_)

        @block.tensor
        def _(pe):
            def mm(out, lhsT, rhs, start=True, stop=True):
                return pe.matmul(out, lhsT, rhs, start=start, stop=stop, skip_group_check=True)

            def halves_ready(g):
                pe.wait_ge(s_hi, g + 1)
                pe.wait_ge(s_lo, g + 1)

            def chunk(b0, g, k0, width=256, slabs=2):
                kts = SLAB // width
                for s in range(slabs):
                    w = (k0 + s) % NHL
                    halves_ready(g + s)
                    for j in range(kts):
                        k = s * kts + j
                        for fb in range(width // P):
                            acc = ps[:, b0 + fb, 0:S]
                            cols = slice(j * width + fb * P, j * width + fb * P + P)
                            mm(acc, whi[w][:, cols], acthi[:, k, :], start=(k == 0), stop=False)
                            mm(acc, whi[w][:, cols], actlo[:, k, :], start=False, stop=False)
                            last = mm(acc, wlo[w][:, cols], acthi[:, k, :], start=False, stop=(k == KT - 1))
                    last.then_inc(s_used, 1)

            def rows(g, k0, n, first, last_):
                w, h = k0 % NHL, n % 2
                halves_ready(g)
                for a in range(TT_):
                    for q in range(4):
                        acc = ps[:, 4 * a + q, :]
                        cols = slice(512 * q, 512 * q + 512)
                        mm(acc, shi[h][:, tok(a)], whi[w][:, cols], start=first, stop=False)
                        mm(acc, slo[h][:, tok(a)], whi[w][:, cols], start=False, stop=False)
                        last = mm(acc, shi[h][:, tok(a)], wlo[w][:, cols], start=False, stop=last_)
                last.then_inc(s_used, 1)

            pe.wait_ge(s_xlo, 4)
            chunk(0, 0, 0)
            chunk(2, 2, 2, width=128, slabs=1)
            pe.wait_ge(s_cst, 32)
            pe.wait_ge(s_lup, 32)
            pe.wait_ge(s_lora, 1)
            pe.wait_ge(s_vec, 1)
            for a in range(TT_):
                for q in range(2):
                    mm(ps[:, 4 + 2 * a + q, :], wt[:, tok(a)], wup[:, 512 * q:512 * q + 512]).then_inc(s_z, 1)
            for n in range(2 * NB):
                b, bk = n % NB, 4 + n % 4
                if n < 4:
                    pe.wait_ge(s_sig, n + 1)
                else:
                    pe.wait_ge(s_itemd, n - 3)
                if n < NB:
                    mm(ps[:, bk, 0:S], aup[64:128, P * b:P * b + P], wa[64:128, :]).then_inc(s_item, 1)
                else:
                    for a in range(TT_):
                        last = mm(ps[:, bk, 256 * a:256 * a + 256], sig[:, a, P * b:P * b + P],
                                  cst[:, C_SU:C_SU + 2 * P])
                    last.then_inc(s_item, 1)
            with pe.Fori(0, N_KRV // 2) as i:
                for k in range(2):
                    pe.wait_ge(s_free, i * 2 + (k + 1))
                    chunk(2 * k, i * 4 + (G_KRV + 2 * k), G_KRV + 2 * k)
            with pe.Fori(0, N_QK // 2) as i:
                for k in range(2):
                    pe.wait_ge(s_free, i * 2 + (N_KRV + k + 1))
                    chunk(2 * k, i * 4 + (G_QK + 2 * k), G_QK + 2 * k)
                    pe.wait_ge(s_sq, i * 2 + (k + 1))
                    mm(ps[:, 4 + k, 0:S], BD, sqt[:, k, :]).then_inc(s_ss, 1)
                    pe.wait_ge(s_rk, i * 2 + (k + 1))
                    mm(ps[:, 6 + k, 0:S], BD, rkt_[:, k, :]).then_inc(s_bon, 1)
            for m in range(2):
                pe.wait_ge(s_free, 2 + N_KRV + N_QK - 1 + m)
                for s in range(4):
                    g = G_VD + 4 * m + s
                    halves_ready(g)
                    w = g % NHL
                    for j in range(4):
                        k = 4 * s + j
                        for a in range(TT_):
                            acc = ps[:, 2 * m + a, :]
                            cols = slice(512 * j, 512 * j + 512)
                            mm(acc, acthi[:, k, tok(a)], whi[w][:, cols], start=(k == 0), stop=False)
                            mm(acc, actlo[:, k, tok(a)], whi[w][:, cols], start=False, stop=False)
                            last = mm(acc, acthi[:, k, tok(a)], wlo[w][:, cols], start=False, stop=(k == KT - 1))
                    last.then_inc(s_used, 1)

            def scores(h):
                if h >= 2:
                    pe.wait_ge(s_smd, h - 1)
                for c in range(2):
                    for a in range(TT_):
                        o = (0, P)[a]
                        last = mm(ps[:, 2 * (h % 2) + c, o:o + P * (a + 1)], qk[hr(c), h, tok(a)],
                                  qk[hr(c), DH + h, 0:P * (a + 1)])
                last.then_inc(s_sc, 1)

            pe.wait_ge(s_rotd, N_QK)
            pe.wait_ge(s_vdc, 4)
            scores(0)
            for h in range(DH):
                if h + 1 < DH:
                    scores(h + 1)
                pe.wait_ge(s_attn, h + 1)
                for j in range(3):
                    last = pe.transpose(ps[:, 4 + h % 2, P * j:P * j + P], att[:, P * j:P * j + P], ID)
                last.then_inc(s_at, 1)
                pe.wait_ge(s_atc, h + 1)
                if h >= 2:
                    pe.wait_ge(s_oc, h - 1)
                mm(ps[:, 6 + h % 2, 0:S], vd[:, 0, P * h:P * h + P], attT[:, 0:S], stop=False)
                mm(ps[:, 6 + h % 2, P:S], vd[:, 1, P * h:P * h + P], attT[:, S:3 * P], start=False).then_inc(s_o, 1)
            for h in range(DH):
                pe.wait_ge(s_osq, h + 1)
                if h >= 4:
                    pe.wait_ge(s_ord, h - 3)
                mm(ps[:, h % 4, 0:S], ONE, osq[:, h % 2, :]).then_inc(s_oss, 1)

            pe.wait_ge(s_pl, 4 * NB)
            pe.wait_ge(s_ord, DH)
            for half in range(2):
                for gp in range(2):
                    g = 2 * half + gp
                    if half:
                        pe.wait_ge(s_upd, 10 * half - 1 + gp)
                    for ul, hp, b, a in units(g):
                        o = P * (ul % 4)
                        mm(ps[:, 4 * gp + hp, o:o + P], kr[hr(hp), b, a, 0, :], bt[hr(hp), b, tok(a)])
                        last = mm(ps[:, 4 * gp + 2 + hp, o:o + P], bt[hr(hp), b, tok(a)], kr[hr(hp), b, a, 0, :])
                    last.then_inc(s_ini, 1)
                for lev in range(1, 6):
                    for gp in range(2):
                        g, n = 2 * half + gp, (half * 5 + lev - 1) * 2 + gp
                        if lev == 1:
                            pe.wait_ge(s_init, g + 1)
                            pe.wait_ge(s_inia, 2 * g + 2)
                        else:
                            pe.wait_ge(s_upd, n - 1)
                        for ul, hp, b, a in units(g):
                            o, u = P * (ul % 4), 8 * gp + ul
                            last = mm(ps[:, 4 * gp + hp, o:o + P], AT[:, u, :], TM[:, u, :])
                        last.then_inc(s_px, 1)
                    for gp in range(2):
                        g, n = 2 * half + gp, (half * 5 + lev - 1) * 2 + gp
                        pe.wait_ge(s_xm, n + 1)
                        for ul, hp, b, a in units(g):
                            o, u = P * (ul % 4), 8 * gp + ul
                            if lev < 5:
                                mm(ps[:, 4 * gp + hp, o:o + P], TTm[:, 8 * g + ul, :], XM[:, u, :])
                            last = mm(ps[:, 4 * gp + 2 + hp, o:o + P], XM[:, u, :], TTm[:, 8 * g + ul, :])
                        last.then_inc(s_ptx, 1)
            pe.wait_ge(s_upd, 20)
            for n in range(12):
                src = [lambda b: krv[:, 2 * NB + b, :], lambda b: bt[:, b, :], lambda b: ki[:, b, :]][n // 4]
                if n >= 8:
                    pe.wait_ge(s_trc, n - 7)
                for b2 in range(2):
                    for a in range(TT_):
                        o = P * (2 * b2 + a)
                        last = pe.transpose(ps[:, n % 8, o:o + P], src(2 * (n % 4) + b2)[:, tok(a)], ID)
                last.then_inc(s_tr, 1)
            def kb(g):
                if g >= 2:
                    pe.wait_ge(s_kbm, g - 1)
                for ul, hp, b, a in units(g):
                    o = P * (ul % 4)
                    last = mm(ps[:, 4 * (g % 2) + hp, o:o + P], ki[hr(hp), b, tok(a)], kr[hr(hp), b, a, 0, :])
                last.then_inc(s_kb, 1)

            pe.wait_ge(s_trc, 12)
            kb(0)
            for g in range(4):
                if g + 1 < 4:
                    kb(g + 1)
                pe.wait_ge(s_kbm, g + 1)
                if g >= 2:
                    pe.wait_ge(s_z1, g - 1)
                for ul, hp, b, a in units(g):
                    o = P * (2 * (b % 2) + a) + HD * hp
                    last = mm(ps[:, 4 * (g % 2) + 2, o:o + HD], kbt[g % 2][:, ul, :], vtm[:, b, a, hr(hp)])
                last.then_inc(s_z1p, 1)
            pe.wait_ge(s_z1, 4)
            for c in range(NC):
                a, cb = c // 2, C * (c % 2)
                rw = slice(cb, cb + C)
                if c:
                    for G in range(2):
                        pe.wait_ge(s_st, 2 * (c - 1) + G + 1)
                        for j in range(4):
                            b = 4 * G + j
                            last = mm(ps[rw, 3 * G, P * j:P * j + P], kr[:, b, a, 0, rw], st[c][:, b, :])
                        last.then_inc(s_ks, 1)
                for G in range(2):
                    if c:
                        pe.wait_ge(s_zc, 2 * (c - 1) + G + 1)
                    if c:
                        pe.wait_ge(s_uc, 2 * (c - 1) + G + 1)
                    for j in range(4):
                        b = 4 * G + j
                        for hp in range(2):
                            last = mm(ps[rw, 3 * G + 1, P * j + HD * hp:P * j + HD * hp + HD],
                                      TTm[:, unit(b, hp, a), rw], z1[:, b, a, hr(hp)])
                    last.then_inc(s_u, 1)
                if c == NC - 1:
                    break
                for G in range(2):
                    pe.wait_ge(s_uc, 2 * c + G + 1)
                    for j in range(4):
                        b = 4 * G + j
                        o = ps[:, 3 * G + 2, P * j:P * j + P]
                        mm(o, ktm[rw, b, a, :], vtm[rw, b, a, :], stop=False)
                        last = mm(o, btm[rw, b, a, :], um[rw, b, a, :], start=False)
                    last.then_inc(s_sp, 1)
            def read(g):
                if g:
                    pe.wait_ge(s_rbm, g)
                for ul, hp, b, a in units(g):
                    o = P * (ul % 4)
                    mm(ps[:, hp, o:o + P], bt[hr(hp), b, tok(a)], kr[hr(hp), b, a, 1, :])
                    last = mm(ps[:, 2 + hp, o:o + P], ki[hr(hp), b, tok(a)], kr[hr(hp), b, a, 1, :])
                last.then_inc(s_rb, 1)

            pe.wait_ge(s_uc, 2 * NC)
            read(0)
            for g in range(4):
                if g + 1 < 4:
                    read(g + 1)
                pe.wait_ge(s_rbm, g + 1)
                if g >= 2:
                    pe.wait_ge(s_yc, g - 1)
                for b2 in range(2):
                    b = 2 * g + b2
                    for a in range(TT_):
                        o = P * (2 * b2 + a)
                        for hp in range(2):
                            out = ps[hr(hp), 4 + g % 2, o:o + P]
                            ul = hp * 4 + b2 * 2 + a
                            mm(out, vtm[:, b, a, hr(hp)], rkt[g % 2][:, ul, :], stop=False)
                            last = mm(out, um[:, b, a, hr(hp)], rbt[g % 2][:, ul, :], start=False)
                        for cc in range(2):
                            c = 2 * a + cc
                            if c:
                                last = mm(ps[:, 4 + g % 2, o + C * cc:o + C * cc + C], st[c][:, b, :],
                                          kr[:, b, a, 1, C * cc:C * cc + C], start=False)
                last.then_inc(s_y, 1)
            pe.wait_ge(s_gup, 16)
            for g in range(4):
                pe.wait_ge(s_yc, g + 1)
                if g >= 2:
                    pe.wait_ge(s_cen, g - 1)
                mm(ps[:, g % 2, :], BD, yf[:, 2 * g:2 * g + 2, :]).then_inc(s_mean, 1)
                if g >= 1:
                    if g >= 3:
                        pe.wait_ge(s_yg, g - 2)
                    for j in range(2):
                        b = 2 * (g - 1) + j
                        for q in range(2):
                            last = mm(ps[:, 4 + g % 2, S * j:S * j + S], gup[:, q, P * b:P * b + P], sg[q][:, :],
                                      start=(q == 0), stop=(q == 1))
                    last.then_inc(s_gate, 1)
                pe.wait_ge(s_gsq, g + 1)
                if g >= 2:
                    pe.wait_ge(s_sd, g - 1)
                mm(ps[:, 2 + g % 2, :], BD, gsq[g % 2][:, :, :]).then_inc(s_var, 1)
            pe.wait_ge(s_yg, 2)
            for j in range(2):
                b = 6 + j
                for q in range(2):
                    last = mm(ps[:, 4, S * j:S * j + S], gup[:, q, P * b:P * b + P], sg[q][:, :],
                              start=(q == 0), stop=(q == 1))
            last.then_inc(s_gate, 1)

            pe.wait_ge(s_yg, 4)
            pe.wait_ge(s_ydn, DH)
            for n in range(4):
                pe.wait_ge(s_ahi, n + 1)
                pe.wait_ge(s_alo, n + 1)
                rows(G_OUT + n, G_OUT + n, n, n == 0, False)
            with pe.Fori(1, KT // 4 - 1) as i:
                for k in range(4):
                    pe.wait_ge(s_ahi, i * 4 + (k + 1))
                    pe.wait_ge(s_alo, i * 4 + (k + 1))
                    rows(i * 4 + (G_OUT + k), G_OUT + k, k, False, False)
            for n in range(KT - 4, KT):
                pe.wait_ge(s_ahi, n + 1)
                pe.wait_ge(s_alo, n + 1)
                rows(G_OUT + n, G_OUT + n, n, False, n == KT - 1)
            for n in range(8):
                a, j = n // 4, n % 4
                pe.wait_ge(s_lnd, a + 1)
                for q in range(4):
                    k = 4 * j + q
                    last = pe.transpose(ps[:, n, P * q:P * q + P], xres[:, a, P * k:P * k + P], ID)
                last.then_inc(s_xt, 1)
            pe.wait_ge(s_x1l, 8)
            for k in range(2):
                chunk(2 * k, G_FF1 + 2 * k, G_FF1 + 2 * k)
            with pe.Fori(1, N_FF1 // 2) as i:
                for k in range(2):
                    pe.wait_ge(s_ff, i * 2 + (k - 1))
                    chunk(2 * k, i * 4 + (G_FF1 + 2 * k), G_FF1 + 2 * k)
            pe.wait_ge(s_ff, N_FF1)
            NF = DFF // P
            for n in range(4):
                pe.wait_ge(s_ahi, KT + n + 1)
                pe.wait_ge(s_alo, KT + n + 1)
                rows(G_FF2 + n, G_FF2 + n, n, n == 0, False)
            with pe.Fori(1, NF // 4 - 1) as i:
                for k in range(4):
                    pe.wait_ge(s_ahi, i * 4 + (KT + k + 1))
                    pe.wait_ge(s_alo, i * 4 + (KT + k + 1))
                    rows(i * 4 + (G_FF2 + k), G_FF2 + k, k, False, False)
            for n in range(NF - 4, NF):
                pe.wait_ge(s_ahi, KT + n + 1)
                pe.wait_ge(s_alo, KT + n + 1)
                rows(G_FF2 + n, G_FF2 + n, n, False, n == NF - 1)

        @block.scalar
        def _(act):
            def A(out, in_, func, **kw):
                return act.activation(out, in_, func, **kw)

            def hi(g, k0):
                act.wait_ge(s_stage[k0 % NST], (g - k0) * 4 + 16 * (k0 // NST + 1))
                if not (isinstance(g, int) and g < 2):
                    act.wait_ge(s_used, g - 1)
                A(whi[k0 % NHL][:, :], stage[k0 % NST][:, :], ACT.Copy).then_inc(s_hi, 1)

            def split(src, g, n, h):
                act.wait_ge(s_used, g - 1)
                A(shi[h][:, :], src, ACT.Copy).then_inc(s_ahi, 1)

            for j in range(4):
                act.wait_ge(s_x[j], 16)
                A(acthi[:, 4 * j:4 * j + 4, :], xstage[:, 4 * j:4 * j + 4, :], ACT.Copy).then_inc(s_xhi, 1)
                if j == 1:
                    hi(0, 0)
            hi(1, 1)
            hi(2, 2)
            act.wait_ge(s_vec, 1)
            act.wait_ge(s_used, 2)
            A(wa[:, :], ps[:, 0, 0:S], ACT.Copy, scale=col(V_OMMU, 24))
            A(sg[0][:, :], ps[:, 1, 0:S], ACT.Copy, scale=col(V_OMMU, 25)).then_inc(s_mix, 1)
            hi(3, 3)
            act.wait_ge(s_free, 1)
            A(wt[0:64, :], wa[0:64, :], ACT.Tanh).then_inc(s_lora, 1)
            act.wait_ge(s_used, 3)
            A(sg[1][:, :], ps[:, 2, 0:S], ACT.Copy, scale=col(V_OMMU, 26)).then_inc(s_mix, 1)
            A(sg[0][:, :], sg[0][:, :], ACT.Sigmoid).then_inc(s_lora, 1)
            act.wait_ge(s_free, 2)
            A(sg[1][:, :], sg[1][:, :], ACT.Sigmoid).then_inc(s_lora, 1)
            for n in range(4):
                act.wait_ge(s_z, n + 1)
                A(sig[:, n // 2, 512 * (n % 2):512 * (n % 2) + 512], ps[:, 4 + n, :], ACT.Sigmoid).then_inc(s_sig, 1)
            for n in range(2 * NB):
                b, bk = n % NB, 4 + n % 4
                act.wait_ge(s_item, n + 1)
                if n < NB:
                    A(bt[:, b, :], ps[:, bk, 0:S], ACT.Sigmoid, bias=col(V_A0, b)).then_inc(s_itemd, 1)
                else:
                    A(kr[:, b, :, :, :].rearrange("p a e q -> p (a e q)"), ps[:, bk, :], ACT.Exp, scale=-DECAY)
                    A(e2[:, b, :].rearrange("p (a q) -> p a q", a=TT_),
                      ps[:, bk, :].rearrange("p (a e q) -> p a e q", a=TT_, e=2)[:, :, 1, :],
                      ACT.Exp, scale=DECAY).then_inc(s_itemd, 1)
            act.wait_ge(s_ang, 9)
            A(sinb[:, :], angt[0][:, :], ACT.Sin).then_inc(s_sin, 1)
            A(cosb[:, :], angt[2][:, :], ACT.Sin).then_inc(s_sin, 1)
            with act.Fori(0, N_KRV // 2) as i:
                for k in range(2):
                    k0 = G_KRV + 2 * k
                    hi(i * 4 + (k0 + 1), k0 + 1)
                    hi(i * 4 + (k0 + 2), k0 + 2)
                    act.wait_ge(s_used, i * 4 + (k0 + 2))
                    for fb in range(2):
                        blk = i * 4 + (2 * k + fb)
                        last = A(krv[:, bass.ds(blk, 1), :].squeeze(1), ps[:, 2 * k + fb, 0:S], ACT.Copy,
                                 scale=vcol(V_OMMU, blk))
                    last.then_inc(s_mix, 1)
            with act.Fori(0, N_QK // 2) as i:
                for k in range(2):
                    k0 = G_QK + 2 * k
                    b = i * 2 + k
                    hi(i * 4 + (k0 + 1), k0 + 1)
                    act.wait_ge(s_free, 2 + N_KRV)
                    A(sqt[:, k, :], krv[:, bass.ds(b, 1), :].squeeze(1), ACT.Square, scale=vcol(V_KK, b)
                      ).then_inc(s_sq, 1)
                    hi(i * 4 + (k0 + 2), k0 + 2)
                    act.wait_ge(s_used, i * 4 + (k0 + 2))
                    for j in range(4):
                        o, s = 32 * j, 32 * (j ^ 1)
                        last = A(rot[k][o:o + 32, :, :], ps[s:s + 32, 2 * k:2 * k + 2, 0:S], ACT.Copy)
                    last.then_inc(s_rotc, 1)
                    act.wait_ge(s_ss, b + 1)
                    A(inv[:, k, :], ps[:, 4 + k, 0:S], ACT.Sqrt).then_inc(s_nrm, 1)
            for m in range(2):
                g = G_VD + 4 * m
                for s in range(1, 5):
                    hi(g + s, g + s)
                act.wait_ge(s_used, g + 4)
                act.wait_ge(s_rotd, N_QK)
                for a in range(TT_):
                    A(vd[:, a, 512 * m:512 * m + 512], ps[:, 2 * m + a, :], ACT.Copy).then_inc(s_vdc, 1)
            act.wait_ge(s_lamd, 2)
            A(lam[:, 0:2], lam[:, 0:2], ACT.Exp).then_inc(s_lame, 1)

            def exps(h):
                act.wait_ge(s_smd, h + 1)
                for c in range(2):
                    for a in range(TT_):
                        o = (0, P)[a]
                        last = A(pr[h % 2][:, c, o:o + P * (a + 1)], sm[h % 2][:, c, o:o + P * (a + 1)], ACT.Exp,
                                 scale=HD ** -0.5, bias=nmx[:, h % 2, 2 * c + a:2 * c + a + 1],
                                 accum_out=sums[:, h % 2, 2 * c + a:2 * c + a + 1])
                last.then_inc(s_exp, 1)

            exps(0)
            for h in range(DH):
                if h + 1 < DH:
                    if h >= 1:
                        act.wait_ge(s_attn, h)
                    exps(h + 1)
                act.wait_ge(s_at, h + 1)
                if h:
                    act.wait_ge(s_o, h)
                A(attT[:, :], ps[:, 4 + h % 2, 0:3 * P], ACT.Copy).then_inc(s_atc, 1)
                act.wait_ge(s_o, h + 1)
                A(yt[:, NB + h, :], ps[:, 6 + h % 2, 0:S], ACT.Copy).then_inc(s_oc, 1)
            for h in range(DH):
                act.wait_ge(s_oc, h + 1)
                if h >= 2:
                    act.wait_ge(s_oss, h - 1)
                A(osq[:, h % 2, :], yt[:, NB + h, :], ACT.Square).then_inc(s_osq, 1)
                act.wait_ge(s_oss, h + 1)
                if h >= 2:
                    act.wait_ge(s_ydn, h - 1)
                A(oinv[:, h % 2, :], ps[:, h % 4, 0:S], ACT.Sqrt, scale=1.0 / P, bias=col(V_SUBEPS)).then_inc(s_ord, 1)
            for n in range(12):
                act.wait_ge(s_tr, n + 1)
                dst = (vtm, btm, ktm)[n // 4]
                j = n % 4
                A(dst[:, 2 * j:2 * j + 2, :, :].rearrange("p b a q -> p (b a q)"), ps[:, n % 8, :], ACT.Copy
                  ).then_inc(s_trc, 1)
            for g in range(4):
                act.wait_ge(s_z1p, g + 1)
                A(z1[:, 2 * g:2 * g + 2, :, :].rearrange("p b a q -> p (b a q)"), ps[:, 4 * (g % 2) + 2, :], ACT.Copy
                  ).then_inc(s_z1, 1)
            for c in range(NC):
                a, cb = c // 2, C * (c % 2)
                for G in range(2):
                    act.wait_ge(s_u, 2 * c + G + 1)
                    A(um[cb:cb + C, 4 * G:4 * G + 4, a, :],
                      ps[cb:cb + C, 3 * G + 1, :].rearrange("p (b q) -> p b q", b=4), ACT.Copy).then_inc(s_uc, 1)
            for g in range(4):
                act.wait_ge(s_y, g + 1)
                A(yf[:, 2 * g:2 * g + 2, :].rearrange("p b q -> p (b q)"), ps[:, 4 + g % 2, :], ACT.Copy
                  ).then_inc(s_yc, 1)
            for g in range(4):
                act.wait_ge(s_cen, g + 1)
                if g >= 2:
                    act.wait_ge(s_var, g - 1)
                A(gsq[g % 2][:, :, :], yf[:, 2 * g:2 * g + 2, :], ACT.Square).then_inc(s_gsq, 1)
                act.wait_ge(s_var, g + 1)
                if g >= 2:
                    act.wait_ge(s_yg, g - 1)
                A(ginv[g % 2][:, :, :].rearrange("p b q -> p (b q)"), ps[:, 2 + g % 2, :], ACT.Sqrt, scale=1.0 / HD,
                  bias=col(V_GNEPS)).then_inc(s_sd, 1)
            act.wait_ge(s_yg, 4)
            act.wait_ge(s_gate, 4)
            act.wait_ge(s_ydn, DH)
            A(shi[0][:, :], yt[:, 0, :], ACT.Copy).then_inc(s_ahi, 1)
            with act.Fori(0, KT // 4 - 1) as i:
                for k in range(4):
                    hi(i * 4 + (G_OUT + k + 1), G_OUT + k + 1)
                    split(yt[:, bass.ds(i * 4 + (k + 1), 1), :].squeeze(1), i * 4 + (G_OUT + k + 1), None, (k + 1) % 2)
            for k in range(KT - 4, KT):
                hi(G_OUT + k + 1, G_OUT + k + 1)
                if k + 1 < KT:
                    split(yt[:, k + 1, :], G_OUT + k + 1, None, (k + 1) % 2)

            def roots(n):
                act.wait_ge(s_ln, n + 1)
                A(rstd[:, :], mv[:, 1:2], ACT.Sqrt, bias=col(V_LNEPS)).then_inc(s_std, 1)

            roots(0)
            roots(1)
            for n in range(8):
                act.wait_ge(s_xt, n + 1)
                a, j = n // 4, n % 4
                A(acthi[:, 4 * j:4 * j + 4, tok(a)], ps[:, n, :].rearrange("p (k q) -> p k q", k=4), ACT.Copy
                  ).then_inc(s_x1h, 1)
            with act.Fori(0, N_FF1 // 2) as i:
                for k in range(2):
                    k0 = G_FF1 + 2 * k
                    hi(i * 4 + (k0 + 1), k0 + 1)
                    hi(i * 4 + (k0 + 2), k0 + 2)
                    act.wait_ge(s_used, i * 4 + (k0 + 2))
                    A(hid[:, bass.ds(i * 4 + 2 * k, 2), :], ps[:, 2 * k:2 * k + 2, 0:S], ACT.Relu).then_inc(s_relu, 1)
            act.wait_ge(s_ff, 1)
            A(shi[0][:, :], hid[:, 0, :], ACT.Copy).then_inc(s_ahi, 1)
            NF = DFF // P
            act.wait_ge(s_ff, N_FF1)
            with act.Fori(0, NF // 4 - 1) as i:
                for k in range(4):
                    hi(i * 4 + (G_FF2 + k + 1), G_FF2 + k + 1)
                    split(hid[:, bass.ds(i * 4 + (k + 1), 1), :].squeeze(1), i * 4 + (G_FF2 + k + 1), None, (k + 1) % 2)
            for k in range(NF - 4, NF - 1):
                hi(G_FF2 + k + 1, G_FF2 + k + 1)
                split(hid[:, k + 1, :], G_FF2 + k + 1, None, (k + 1) % 2)
            roots(2)
            roots(3)

        @block.vector
        def _(dve):
            TTn, TS, STT = dve.tensor_tensor, dve.tensor_scalar, dve.scalar_tensor_tensor

            def lo(g, k0):
                dve.wait_ge(s_hi, g + 1)
                if not (isinstance(g, int) and g < 2):
                    dve.wait_ge(s_used, g - 1)
                TTn(wlo[k0 % NHL][:, :], stage[k0 % NST][:, :], f(whi[k0 % NHL][:, :]), ALU.subtract
                    ).then_inc(s_lo, 1)

            def mix(out, acc, mu):
                return STT(out[:, 1:S], acc[:, 0:S - 1], mu, out[:, 1:S], ALU.mult, ALU.add)

            dve.wait_ge(s_cst, 32)
            dve.memset(wt[64:65, :], 1.0)
            TS(vec[:, V_OMMU:V_OMMU + 27], vec[:, V_MU:V_MU + 27], -1.0, 1.0, ALU.mult, ALU.add)
            TS(vec[:, V_OMKA:V_OMKA + 8], vec[:, V_KA:V_KA + 8], -1.0, 1.0, ALU.mult, ALU.add)
            TS(vec[:, V_G08:V_G08 + 1], vec[:, V_SG:V_SG + 1], 1.0 - LAMBDA_INIT, None, ALU.mult).then_inc(s_vec, 1)
            for j in range(4):
                dve.wait_ge(s_xhi, j + 1)
                TTn(actlo[:, 4 * j:4 * j + 4, :], xstage[:, 4 * j:4 * j + 4, :], f(acthi[:, 4 * j:4 * j + 4, :]),
                    ALU.subtract).then_inc(s_xlo, 1)
            for g in range(3):
                lo(g, g)
            dve.wait_ge(s_mix, 1)
            mix(wa, ps[:, 0, :], col(V_MU, 24))
            mix(sg[0], ps[:, 1, :], col(V_MU, 25)).then_inc(s_free, 1)
            lo(3, 3)
            dve.wait_ge(s_mix, 2)
            mix(sg[1], ps[:, 2, :], col(V_MU, 26)).then_inc(s_free, 1)
            dve.wait_ge(s_pos, 16)
            MAGIC = 1.5 * 2 ** 23
            n = 0

            def ang(ins):
                nonlocal n
                n += 1
                ins.then_inc(s_ang, 1)
                dve.wait_ge(s_ang, n)

            ang(dve.tensor_copy(angt[0][:, :], posi[:, :]))
            ang(TS(angt[0][:, :], angt[0][:, :], col(V_INVF), None, ALU.mult))
            ang(TS(angt[1][:, :], angt[0][:, :], 1.0 / (2.0 * math.pi), MAGIC, ALU.mult, ALU.add))
            ang(TS(angt[1][:, :], angt[1][:, :], MAGIC, None, ALU.subtract))
            for part in (6.28125, 2029.0 / 2 ** 20, 2.0 * math.pi - 6.28125 - 2029.0 / 2 ** 20):
                ang(STT(angt[0][:, :], angt[1][:, :], -part, angt[0][:, :], ALU.mult, ALU.add))
            ang(TS(angt[0][:, :], angt[0][:, :], 3.1415925, -3.1415925, ALU.min, ALU.max))
            dve.wait_ge(s_ang, 8)
            STT(angt[2][:, :], angt[0][:, :], -1.0, angt[0][:, :], ALU.mult, ALU.max).then_inc(s_tab, 1)
            dve.wait_ge(s_tab, 1)
            TS(angt[2][:, :], angt[2][:, :], -1.0, math.pi / 2, ALU.mult, ALU.add).then_inc(s_ang, 1)
            dve.wait_ge(s_sin, 1)
            TS(sinb[:, :], sinb[:, :], col(V_SIGN), None, ALU.mult).then_inc(s_tab, 1)
            dve.wait_ge(s_itemd, 16)
            dve.tensor_copy(gam[:, :, :].rearrange("p b c -> p (b c)").rearrange("p (m c) -> p m c", c=2),
                            kr[:, :, :, 1, C - 1::C].rearrange("p b a c -> p (b a) c")).then_inc(s_gam, 1)
            with dve.Fori(0, N_KRV // 2) as i:
                for k in range(2):
                    k0 = G_KRV + 2 * k
                    lo(i * 4 + (k0 + 1), k0 + 1)
                    lo(i * 4 + (k0 + 2), k0 + 2)
                    dve.wait_ge(s_mix, i * 2 + (k + 3))
                    for fb in range(2):
                        blk = i * 4 + (2 * k + fb)
                        out = krv[:, bass.ds(blk, 1), 1:S].squeeze(1)
                        last = STT(out, ps[:, 2 * k + fb, 0:S - 1], vcol(V_MU, blk), out, ALU.mult, ALU.add)
                    last.then_inc(s_free, 1)
            dve.wait_ge(s_tab, 2)
            dve.wait_ge(s_sin, 2)
            dve.wait_ge(s_gam, 1)
            dve.wait_ge(s_free, 2 + N_KRV)
            with dve.Fori(0, N_QK // 2) as i:
                for k in range(2):
                    k0 = G_QK + 2 * k
                    b = i * 2 + k

                    def at_b(x, o=0):
                        return x[:, bass.ds(b + o, 1), :].squeeze(1)

                    K, R, V = at_b(krv), at_b(krv, NB), at_b(krv, 2 * NB)
                    lo(i * 4 + (k0 + 1), k0 + 1)
                    E = i * 10 + 5 * k
                    TS(at_b(ki), at_b(bt), vcol(V_KA, b), vcol(V_OMKA, b), ALU.mult, ALU.add).then_inc(s_ew, 1)
                    dve.wait_ge(s_ew, E + 1)
                    TTn(at_b(ki), K, at_b(ki), ALU.mult).then_inc(s_ew, 1)
                    dve.wait_ge(s_ew, E + 2)
                    STT(rkt_[:, k, :], R, vcol(V_RK, b), at_b(ki), ALU.mult, ALU.mult).then_inc(s_rk, 1)
                    rt = kr[:, bass.ds(b, 1), :, 1, :].squeeze(1)
                    TTn(rt, rt, R.rearrange("p (a q) -> p a q", a=TT_), ALU.mult).then_inc(s_ew, 1)
                    lo(i * 4 + (k0 + 2), k0 + 2)
                    dve.wait_ge(s_rotc, b + 1)
                    TTn(rot[k][:, :, :], rot[k][:, :, :], over(sinb[:, :], 2), ALU.mult).then_inc(s_rotm, 1)
                    out = qk[:, bass.ds(b * 2, 2), :]
                    TTn(out, ps[:, 2 * k:2 * k + 2, 0:S], over(cosb[:, :], 2), ALU.mult).then_inc(s_free, 1)
                    dve.wait_ge(s_rotm, b + 1)
                    dve.wait_ge(s_free, b + (2 + N_KRV + 1))
                    TTn(out, out, rot[k][:, :, :], ALU.add).then_inc(s_rotd, 1)
                    dve.wait_ge(s_nrm, b + 1)
                    TS(inv[:, k, :], inv[:, k, :], 1e-12, None, ALU.max).then_inc(s_ew, 1)
                    dve.wait_ge(s_ew, E + 4)
                    dve.reciprocal(inv[:, k, :], inv[:, k, :]).then_inc(s_ew, 1)
                    dve.wait_ge(s_ew, E + 5)
                    STT(K, K, vcol(V_KK, b), inv[:, k, :], ALU.mult, ALU.mult).then_inc(s_kk, 1)
                    dve.wait_ge(s_bon, b + 1)
                    TTn(R, V, ps[:, 6 + k, 0:S], ALU.mult).then_inc(s_kk, 1)
            for g in range(G_VD + 1, G_OUT + 1):
                lo(g, g)
            dve.wait_ge(s_attc, 80)
            for j in range(2):
                dve.tensor_tensor_reduce(lamt[:, j, :], lamv[:, 2 * j, :], lamv[:, 2 * j + 1, :], 1.0, 0.0,
                                         ALU.mult, ALU.add, lam[:, j:j + 1]).then_inc(s_lamd, 1)
            dve.wait_ge(s_lame, 1)
            TTn(lam[:, 2:3], lam[:, 1:2], lam[:, 0:1], ALU.subtract).then_inc(s_lamd, 1)
            dve.wait_ge(s_lamd, 3)
            TS(lam[:, 3:4], lam[:, 2:3], LAMBDA_INIT, None, ALU.subtract).then_inc(s_lamd, 1)
            dve.wait_ge(s_lamd, 4)

            def masked(h):
                dve.wait_ge(s_sc, h + 1)
                if h >= 2:
                    dve.wait_ge(s_exp, h - 1)
                for c in range(2):
                    for a in range(TT_):
                        o = (0, P)[a]
                        last = dve.tensor_tensor_reduce(
                            sm[h % 2][:, c, o:o + P * (a + 1)], ps[:, 2 * (h % 2) + c, o:o + P * (a + 1)],
                            amask[:, o:o + P * (a + 1)], 1.0, -3e38, ALU.add, ALU.max,
                            mx[:, h % 2, 2 * c + a:2 * c + a + 1])
                last.then_inc(s_attd, 1)
                dve.wait_ge(s_attd, 5 * h + 1 if h < 1 else MS[h])
                TS(nmx[:, h % 2, :], mx[:, h % 2, :], -HD ** -0.5, None, ALU.mult).then_inc(s_smd, 1)

            MS, step = {0: 1}, 1
            masked(0)
            for h in range(DH):
                if h + 1 < DH:
                    step += 1
                    MS[h + 1] = step
                    masked(h + 1)
                dve.wait_ge(s_exp, h + 1)
                q = h % 2
                dve.reciprocal(coef[:, q, :], sums[:, q, :]).then_inc(s_attd, 1)
                step += 1
                dve.wait_ge(s_attd, step)
                TS(coef[:, q, 2:4], coef[:, q, 2:4], lam[:, 3:4], None, ALU.mult).then_inc(s_attd, 1)
                if h:
                    dve.wait_ge(s_at, h)
                for a in range(TT_):
                    o = (0, P)[a]
                    last = TS(att[:, o:o + P * (a + 1)], pr[q][:, 0, o:o + P * (a + 1)], coef[:, q, a:a + 1], None,
                              ALU.mult)
                last.then_inc(s_attd, 1)
                step += 2
                dve.wait_ge(s_attd, step)
                for a in range(TT_):
                    o = (0, P)[a]
                    last = STT(att[:, o:o + P * (a + 1)], pr[q][:, 1, o:o + P * (a + 1)],
                               coef[:, q, 2 + a:3 + a], att[:, o:o + P * (a + 1)], ALU.mult, ALU.add)
                last.then_inc(s_attn, 1)
            for h in range(DH):
                dve.wait_ge(s_ord, h + 1)
                dve.reciprocal(oinv[:, h % 2, :], oinv[:, h % 2, :]).then_inc(s_yd, 1)
                dve.wait_ge(s_yd, h + 1)
                STT(yt[:, NB + h, :], yt[:, NB + h, :], col(V_G08), oinv[:, h % 2, :], ALU.mult, ALU.mult
                    ).then_inc(s_ydn, 1)
            dve.wait_ge(s_levc, 16)
            for half in range(2):
                for gp in range(2):
                    g = 2 * half + gp
                    u = slice(8 * gp, 8 * gp + 8)
                    dve.wait_ge(s_ini, g + 1)
                    ab = banks(4 * gp).rearrange("p h (u q) -> p (h u) q", q=P)
                    bb = banks(4 * gp + 2).rearrange("p h (u q) -> p (h u) q", q=P)
                    STT(TM[:, u, :], ab, -1.0, over(M1, 8), ALU.mult, ALU.mult).then_inc(s_inia, 1)
                    TTn(AT[:, u, :], bb, over(SU, 8), ALU.mult).then_inc(s_inia, 1)
                for lev in range(1, 6):
                    for gp in range(2):
                        n = (half * 5 + lev - 1) * 2 + gp
                        dve.wait_ge(s_px, n + 1)
                        TTn(XM[:, 8 * gp:8 * gp + 8, :], banks(4 * gp).rearrange("p h (u q) -> p (h u) q", q=P),
                            over(levc[:, lev, :], 8), ALU.mult).then_inc(s_xm, 1)
                    for gp in range(2):
                        g, n = 2 * half + gp, (half * 5 + lev - 1) * 2 + gp
                        dve.wait_ge(s_ptx, n + 1)
                        tm, tt = TM[:, 8 * gp:8 * gp + 8, :], TTm[:, 8 * g:8 * g + 8, :]
                        ab = banks(4 * gp).rearrange("p h (u q) -> p (h u) q", q=P)
                        bb = banks(4 * gp + 2).rearrange("p h (u q) -> p (h u) q", q=P)
                        if lev < 5:
                            TTn(tm, tm, ab, ALU.subtract)
                            TTn(tt, tt, bb, ALU.subtract).then_inc(s_upd, 1)
                        else:
                            TTn(tt, bb, tt, ALU.subtract).then_inc(s_upd, 1)
            for g in range(4):
                dve.wait_ge(s_kb, g + 1)
                if g >= 2:
                    dve.wait_ge(s_z1p, g - 1)
                TTn(kbt[g % 2][:, :, :], banks(4 * (g % 2)).rearrange("p h (u q) -> p (h u) q", q=P), over(SU, 8),
                    ALU.mult).then_inc(s_kbm, 1)
            dve.wait_ge(s_gm, 3)
            dve.wait_ge(s_z1, 4)
            for c in range(NC):
                a, cb = c // 2, C * (c % 2)
                if c:
                    for G in range(2):
                        dve.wait_ge(s_ks, 2 * (c - 1) + G + 1)
                        z = z1[cb:cb + C, 4 * G:4 * G + 4, a, :]
                        TTn(z, ps[cb:cb + C, 3 * G, :].rearrange("p (b q) -> p b q", b=4), z, ALU.add
                            ).then_inc(s_zc, 1)
                if c == NC - 1:
                    break
                for G in range(2):
                    dve.wait_ge(s_sp, 2 * c + G + 1)
                    bs = slice(4 * G, 4 * G + 4)
                    pp = ps[:, 3 * G + 2, :].rearrange("p (b q) -> p b q", b=4)
                    if c == 0:
                        TTn(st[1][:, bs, :], pp, gm[0][:, bs, :], ALU.mult).then_inc(s_st, 1)
                    else:
                        TTn(st[c + 1][:, bs, :], pp, st[c][:, bs, :], ALU.add).then_inc(s_stm, 1)
                        dve.wait_ge(s_stm, 2 * (c - 1) + G + 1)
                        TTn(st[c + 1][:, bs, :], st[c + 1][:, bs, :], gm[c][:, bs, :], ALU.mult).then_inc(s_st, 1)
            dve.wait_ge(s_uc, 2 * NC)
            for g in range(4):
                dve.wait_ge(s_rb, g + 1)
                if g >= 2:
                    dve.wait_ge(s_y, g - 1)
                TTn(rbt[g % 2][:, :, :], banks(0).rearrange("p h (u q) -> p (h u) q", q=P), over(IU, 8), ALU.mult)
                TTn(rkt[g % 2][:, :, :], banks(2).rearrange("p h (u q) -> p (h u) q", q=P), over(IU, 8), ALU.mult
                    ).then_inc(s_rbm, 1)
            for g in range(4):
                y = yf[:, 2 * g:2 * g + 2, :]
                y512 = y.rearrange("p b q -> p (b q)")
                dve.wait_ge(s_mean, g + 1)
                STT(y512, ps[:, g % 2, :], -1.0 / HD, y512, ALU.mult, ALU.add).then_inc(s_cen, 1)
                dve.wait_ge(s_sd, g + 1)
                dve.reciprocal(ginv[g % 2][:, :, :], ginv[g % 2][:, :, :]).then_inc(s_gn, 1)
                dve.wait_ge(s_gn, 4 * g + 1)
                TTn(y, y, ginv[g % 2][:, :, :], ALU.mult).then_inc(s_gn, 1)
                dve.wait_ge(s_gn, 4 * g + 2)
                for j in range(2):
                    b = 2 * g + j
                    last = TS(yf[:, b, :], yf[:, b, :], col(V_GG, b), col(V_GB, b), ALU.mult, ALU.add)
                last.then_inc(s_gn, 1)
                dve.wait_ge(s_gn, 4 * g + 3)
                TTn(y, y, krv[:, NB + 2 * g:NB + 2 * g + 2, :], ALU.add).then_inc(s_gn, 1)
                dve.wait_ge(s_gn, 4 * g + 4)
                dve.wait_ge(s_gate, g + 1)
                TTn(yt[:, 2 * g:2 * g + 2, :].rearrange("p b q -> p (b q)"), ps[:, 4 + (g + 1) % 2, :], y512,
                    ALU.mult).then_inc(s_yg, 1)

            def split(src, n, h, used):
                dve.wait_ge(s_ahi, n + 1)
                if used is not None:
                    dve.wait_ge(s_used, used)
                TTn(slo[h][:, :], src, f(shi[h][:, :]), ALU.subtract).then_inc(s_alo, 1)

            split(yt[:, 0, :], 0, 0, None)
            with dve.Fori(0, KT // 4 - 1) as i:
                for k in range(4):
                    lo(i * 4 + (G_OUT + k + 1), G_OUT + k + 1)
                    split(yt[:, bass.ds(i * 4 + (k + 1), 1), :].squeeze(1), i * 4 + (k + 1), (k + 1) % 2,
                          i * 4 + (G_OUT + k))
            for k in range(KT - 4, KT):
                lo(G_OUT + k + 1, G_OUT + k + 1)
                if k + 1 < KT:
                    split(yt[:, k + 1, :], k + 1, (k + 1) % 2, G_OUT + k)

            chain = 0

            def layer_norm(n, gain, bias):
                nonlocal chain

                def link(ins):
                    nonlocal chain
                    chain += 1
                    ins.then_inc(s_lnk, 1)
                    dve.wait_ge(s_lnk, chain)

                for a in range(TT_):
                    for q in range(4):
                        x = xres[:, a, 512 * q:512 * q + 512]
                        last = STT(x, x, ALPHA, ps[:, 4 * a + q, :], ALU.mult, ALU.add)
                    link(last)
                for a in range(TT_):
                    for q in range(4):
                        last = dve.bn_stats(stats[:, q, :], xres[:, a, 512 * q:512 * q + 512])
                    link(last)
                    dve.bn_aggr(mv[:, :], stats[:, :, :]).then_inc(s_ln, 1)
                    dve.wait_ge(s_std, 2 * n + a + 1)
                    link(dve.reciprocal(rstd[:, :], rstd[:, :]))
                    x = xres[:, a, :]
                    link(TS(x, x, mv[:, 0:1], rstd[:, 0:1], ALU.subtract, ALU.mult))
                    link(TTn(x, x, gain[:, :], ALU.mult))
                    TTn(x, x, bias[:, :], ALU.add).then_inc(s_lnd, 1)

            dve.wait_ge(s_used, G_FF1)
            dve.wait_ge(s_xres, 16)
            dve.wait_ge(s_ln1c, 32)
            layer_norm(0, gain1, bias1)
            for n in range(8):
                dve.wait_ge(s_x1h, n + 1)
                a, j = n // 4, n % 4
                TTn(actlo[:, 4 * j:4 * j + 4, tok(a)], ps[:, n, :].rearrange("p (k q) -> p k q", k=4),
                    f(acthi[:, 4 * j:4 * j + 4, tok(a)]), ALU.subtract).then_inc(s_x1l, 1)
            with dve.Fori(0, N_FF1 // 2) as i:
                for k in range(2):
                    k0 = G_FF1 + 2 * k
                    lo(i * 4 + (k0 + 1), k0 + 1)
                    lo(i * 4 + (k0 + 2), k0 + 2)
                    dve.wait_ge(s_relu, i * 2 + (k + 1))
                    h2 = hid[:, bass.ds(i * 4 + 2 * k, 2), :]
                    TTn(h2, ps[:, 2 * k:2 * k + 2, 0:S], h2, ALU.mult).then_inc(s_ff, 1)
            NF = DFF // P
            split(hid[:, 0, :], KT, 0, None)
            with dve.Fori(0, NF // 4 - 1) as i:
                for k in range(4):
                    lo(i * 4 + (G_FF2 + k + 1), G_FF2 + k + 1)
                    split(hid[:, bass.ds(i * 4 + (k + 1), 1), :].squeeze(1), i * 4 + (KT + k + 1), (k + 1) % 2,
                          i * 4 + (G_FF2 + k))
            for k in range(NF - 4, NF - 1):
                lo(G_FF2 + k + 1, G_FF2 + k + 1)
                split(hid[:, k + 1, :], KT + k + 1, (k + 1) % 2, G_FF2 + k)
            dve.wait_ge(s_used, G_END)
            dve.wait_ge(s_ln2c, 32)
            layer_norm(1, gain2, bias2)

        @block.gpsimd
        def _(pool):
            PT = pool.tensor_tensor
            with pool.Fori(0, NB) as b:
                def at_b(x):
                    return x[:, bass.ds(b, 1), :].squeeze(1)

                kk, bb, kb_, e = at_b(krv), at_b(bt), at_b(ki), at_b(e2)
                kt = kr[:, bass.ds(b, 1), :, 0, :].squeeze(1)
                pool.wait_ge(s_kk, b * 2 + 1)
                PT(kt, kt, kk.rearrange("p (a q) -> p a q", a=TT_), ALU.mult).then_inc(s_pl, 1)
                PT(bb, bb, kk, ALU.mult).then_inc(s_pl, 1)
                pool.wait_ge(s_pl, b * 4 + 2)
                PT(bb, bb, e, ALU.mult).then_inc(s_pl, 1)
                PT(kb_, kb_, e, ALU.mult).then_inc(s_pl, 1)
            pool.wait_ge(s_levc, 16)
            for g in range(4):
                u, ug = slice(8 * (g % 2), 8 * (g % 2) + 8), slice(8 * g, 8 * g + 8)
                pool.wait_ge(s_inia, 2 * g + 2)
                PT(TM[:, u, :], TM[:, u, :], over(ID, 8), ALU.add)
                PT(TTm[:, ug, :], AT[:, u, :], over(M1T, 8), ALU.mult).then_inc(s_init0, 1)
                pool.wait_ge(s_init0, g + 1)
                PT(TTm[:, ug, :], over(ID, 8), TTm[:, ug, :], ALU.subtract).then_inc(s_init, 1)
            for c in range(3):
                if c == 0:
                    pool.wait_ge(s_tr, 4)
                if c == 2:
                    pool.wait_ge(s_upd, 20)
                PT(gm[c][:, :, :], over(BD, NB), gam[:, :, c:c + 1].broadcast_to([P, NB, P]), ALU.mult
                   ).then_inc(s_gm, 1)


OUT_SHAPE = (1, S, D)


def layout(inputs):
    a = {k: np.asarray(v) for k, v in inputs.items()}
    w_in = a["w_in"][0]

    def cut(w, c0, width, slabs):
        piece = w[:, c0:c0 + width].reshape(slabs, KT // slabs, P, width)
        return piece.transpose(0, 2, 1, 3).reshape(slabs, P, -1)

    slabs = [cut(w_in, 3 * RW, 256, 2), cut(w_in, RCOLS - P, P, 1)]
    for base in (RW, 0, 2 * RW):
        slabs += [cut(w_in, base + 256 * j, 256, 2) for j in range(RW // 256)]
    slabs += [cut(w_in, RCOLS + 256 * j, 256, 2) for j in range(2 * RW // 256)]
    slabs += [cut(w_in, RCOLS + 2 * RW + 512 * j, 512, 4) for j in range(2)]
    ff1 = np.concatenate([cut(a["w_ff1"][0], 256 * j, 256, 2) for j in range(N_FF1)])

    def blocks(v):
        return np.asarray(v).reshape(-1, P).T

    mu = a["mu_shift"][0]
    inv_freq = np.float32(10000.0) ** (-np.arange(0, HD, 2, dtype=np.float32) / np.float32(HD))
    vecs = np.concatenate([
        blocks(mu[RW:2 * RW]), blocks(mu[0:RW]), blocks(mu[2 * RW:3 * RW]),
        blocks(mu[3 * RW:3 * RW + 2 * P]), blocks(mu[RCOLS - P:RCOLS]),
        blocks(a["rwkv_k_k"][0]), blocks(a["rwkv_k_a"][0]), blocks(a["rwkv_r_k"][0].reshape(-1)),
        blocks(a["rwkv_a0"][0]), blocks(a["rwkv_gn_gain"][0]), blocks(a["rwkv_gn_bias"][0]),
        a["diff_subln_gain"][0].reshape(P, 1),
        np.tile(inv_freq, 4).reshape(P, 1).astype(np.float32),
        np.tile(np.repeat(np.array([-1.0, 1.0], np.float32), 32), 2).reshape(P, 1),
        np.full((P, 1), GN_EPS, np.float32), np.full((P, 1), SUB_EPS, np.float32),
        np.full((P, 1), LN_EPS, np.float32)], axis=1)
    g_up = a["rwkv_g_up"][0]
    gup = np.zeros((P, 2, RW), np.float32)
    gup[:, 0, :] = g_up[0:P]
    gup[P - (LORA_G - P):, 1, :] = g_up[P:LORA_G]
    x = a["x"][0]
    out = {
        "x": x, "xT": x.T.reshape(KT, P, S).transpose(1, 0, 2),
        "positions": a["positions"].astype(np.int32).reshape(1, S),
        "w_in": np.concatenate(slabs), "w_out": a["w_out"][0].reshape(KT, P, D), "w_ff1": ff1,
        "w_ff2": a["w_ff2"][0].reshape(DFF // P, P, D), "vecs": vecs, "consts": shape_constants(),
        "w_up": np.concatenate([a["rwkv_w_up"][0], a["rwkv_w0"]]), "a_up": a["rwkv_a_up"][0], "g_up": gup,
        "lam": np.concatenate([a["diff_lambda_q1"], a["diff_lambda_k1"], a["diff_lambda_q2"], a["diff_lambda_k2"]]),
        "ln1_gain": a["ln1_gain"], "ln1_bias": a["ln1_bias"], "ln2_gain": a["ln2_gain"], "ln2_bias": a["ln2_bias"],
    }
    return {k: np.ascontiguousarray(v) for k, v in out.items()}


def kernel(**inputs):
    import concourse.bacc as bacc
    from concourse.bass_utils import run_bass_kernel_spmd

    nc = bacc.Bacc("TRN2", target_bir_lowering=False, num_devices=1)
    arrays = layout(inputs)
    t = {n: nc.dram_tensor(n, a.shape, mybir.dt.from_np(a.dtype), kind="ExternalInput").ap()
         for n, a in arrays.items()}
    t["out"] = nc.dram_tensor("out", (S, D), F32, kind="ExternalOutput").ap()
    build(nc, t)
    r = run_bass_kernel_spmd(nc, [arrays], core_ids=[0])
    return r.results[0]["out"].reshape(OUT_SHAPE)
```

```python
import math
from contextlib import ExitStack

import numpy as np

import concourse.bass as bass
from concourse import mybir

ALU = mybir.AluOpType
ACT = mybir.ActivationFunctionType
F32 = mybir.dt.float32
F32R = mybir.dt.float32r
I32 = mybir.dt.int32
AX_X = mybir.AxisListType.X

P = 128
D = 2048
S = 256
TT_ = S // P
DFF = 4 * D
RW = D // 2
HD = 64
NB = RW // P
DH = 8
KT = D // P
C = 64
NC = S // C
LORA_W, LORA_A, LORA_G = 64, 64, 160
RCOLS = 3 * RW + LORA_W + LORA_A + LORA_G
ALPHA = 2.0 ** 0.25
LAMBDA_INIT = 0.8 - 0.6 * math.exp(-0.3 * 0)
LN_EPS, GN_EPS, SUB_EPS = 1e-5, 64e-5, 1e-5
DECAY = math.exp(-0.5)
NEG = -1e30
UNITS = 32

SLAB = 2048
G_LORA, N_LORA = 0, 3
G_KRV = G_LORA + N_LORA
N_KRV = 12
G_QK = G_KRV + 2 * N_KRV
N_QK = 8
G_VD = G_QK + 2 * N_QK
G_OUT = G_VD + 8
G_FF1 = G_OUT + KT
N_FF1 = DFF // 256
G_FF2 = G_FF1 + 2 * N_FF1
G_END = G_FF2 + DFF // P
NST, NHL = 4, 2

V_MU, V_KK, V_KA, V_RK, V_A0, V_GG, V_GB, V_SG, V_INVF, V_SIGN, V_GNEPS, V_SUBEPS, V_LNEPS = (
    0, 27, 35, 43, 51, 59, 67, 75, 76, 77, 78, 79, 80)
V_IN = 81
V_OMMU, V_OMKA, V_G08 = 81, 108, 116
V_ALL = 120

C_SU, C_IU, C_SL, C_ID, C_BD, C_ONE = 0, 128, 256, 384, 512, 640
C_SMALL = 768
C_LEV, C_M1T = 768, 768 + 6 * 128
C_ATT = C_M1T + 128
C_ALL = C_ATT + 384


def shape_constants():
    p, q = np.arange(P)[:, None], np.arange(P)[None, :]
    same = p // C == q // C
    out = np.zeros((P, C_ALL), np.float32)
    out[:, C_SU:C_SU + P] = same & (p < q)
    out[:, C_IU:C_IU + P] = same & (p <= q)
    out[:, C_SL:C_SL + P] = same & (q < p)
    out[:, C_ID:C_ID + P] = p == q
    out[:, C_BD:C_BD + P] = same
    out[:, C_ONE:C_ONE + P] = 1.0
    for n in range(6):
        m = 1 << n
        lev = (p // (2 * m) == q // (2 * m)) & (p // m % 2 == 1) & (q // m % 2 == 0)
        out[:, C_LEV + n * P:C_LEV + (n + 1) * P] = lev
        if n == 0:
            out[:, C_M1T:C_M1T + P] = lev.T
    causal = np.where(q > p, NEG, 0.0)
    out[:, C_ATT:C_ATT + P] = causal
    out[:, C_ATT + 2 * P:C_ATT + 3 * P] = causal
    return out


def build(nc, t):
    ctx = ExitStack()
    with ctx:
        BASE, SL_BYTES = 16512, 8192
        SMALL = BASE + 25 * SL_BYTES

        def at(name, slot, shape, dtype=F32, byte=0):
            return nc.alloc_sbuf_tensor_at(name, shape, dtype, offset=BASE + slot * SL_BYTES + byte)

        def small(name, col, shape, dtype=F32):
            return nc.alloc_sbuf_tensor_at(name, shape, dtype, offset=SMALL + 4 * col)

        def sem(name):
            return ctx.enter_context(nc.semaphore(name))

        stage = [at(f"stage{i}", i, [P, SLAB]) for i in range(NST)]
        whi = [at(f"whi{i}", 4 + i, [P, SLAB], F32R) for i in range(NHL)]
        wlo = [at(f"wlo{i}", 6 + i, [P, SLAB], F32R) for i in range(NHL)]
        acthi = at("acthi", 8, [P, KT, S], F32R)
        actlo = at("actlo", 10, [P, KT, S], F32R)
        wup = at("wup", 12, [65, RW])
        aup = at("aup", 12, [P, RW], byte=4096)
        sig = at("sig", 13, [P, TT_, RW])
        kr = at("kr", 14, [P, NB, TT_, 2, P])
        e2 = at("e2", 16, [P, NB, S])
        bt = at("bt", 17, [P, NB, S])
        krv = at("krv", 18, [P, 3 * NB, S])
        ki = at("ki", 21, [P, NB, S])
        qk = at("qk", 22, [P, 2 * DH, S])
        xstage = at("xstage", 22, [P, KT, S])
        vd = at("vd", 24, [P, TT_, RW])
        cosb = at("cosb", 24, [P, S])
        sinb = at("sinb", 24, [P, S], byte=1024)
        angt = [at(f"angt{i}", 24, [P, S], byte=2048 + 1024 * i) for i in range(3)]
        posi = at("posi", 24, [P, S], I32, byte=5120)
        rot = [at(f"rot{i}", 12, [P, 2, S], byte=2048 * i) for i in range(2)]
        sqt = at("sqt", 13, [P, 2, S])
        inv = at("inv", 13, [P, 2, S], byte=2048)
        rkt_ = at("rkt_", 13, [P, 2, S], byte=4096)
        yt = at("yt", 12, [P, KT, S])
        amask = at("amask", 0, [P, 3 * P])
        sm = at("sm", 0, [P, 2, 3 * P], byte=2048)
        pr = at("pr", 0, [P, 2, 3 * P], byte=5120)
        att = at("att", 1, [P, 3 * P])
        attT = at("attT", 1, [P, 3 * P], byte=1536)
        lamv = at("lamv", 1, [P, 4, HD], byte=3072)
        lamt = at("lamt", 1, [P, 2, HD], byte=4096)
        osq = at("osq", 1, [P, S], byte=4608)
        oinv = at("oinv", 1, [P, S], byte=5632)
        levc = at("levc", 3, [P, 7, P])
        AT = at("AT", 8, [P, 16, P])
        TM = at("TM", 9, [P, 16, P])
        XM = at("XM", 10, [P, 16, P])
        TTh = [at("TTh0", 18, [P, 16, P]), at("TTh1", 16, [P, 16, P])]
        kbt = [at(f"kbt{i}", 8, [P, 8, P], byte=4096 * i) for i in range(2)]
        vtm = at("vtm", 9, [P, NB, TT_, P])
        btm = at("btm", 10, [P, NB, TT_, P])
        ktm = at("ktm", 24, [P, NB, TT_, P])
        z1 = at("z1", 22, [P, NB, TT_, P])
        um = at("um", 23, [P, NB, TT_, P])
        st = [None, at("st1", 8, [P, NB, P]), at("st2", 8, [P, NB, P], byte=4096), at("st3", 11, [P, NB, P])]
        gm = [at("gm0", 20, [P, NB, P]), at("gm1", 20, [P, NB, P], byte=4096), at("gm2", 11, [P, NB, P], byte=4096)]
        rbt = at("rbt", 0, [P, UNITS, P])
        rkt = at("rkt", 2, [P, UNITS, P])
        yf = at("yf", 20, [P, NB, S])
        gup = at("gup", 10, [P, 2, RW])
        gsq = at("gsq", 24, [P, NB, S])
        xres = at("xres", 22, [P, TT_, D])
        gain1 = at("gain1", 14, [P, D])
        bias1 = at("bias1", 15, [P, D])
        hid = at("hid", 14, [P, DFF // P, S])
        gain2 = at("gain2", 12, [P, D])
        bias2 = at("bias2", 13, [P, D])
        cst = small("cst", 0, [P, C_SMALL])
        vec = small("vec", 768, [P, V_ALL])
        wt = small("wt", 888, [65, S])
        wa = small("wa", 888 + 256, [P, S])
        sg = [small(f"sg{i}", 888 + 512 + 256 * i, [P, S]) for i in range(2)]
        shi = [small(f"shi{i}", 888 + 256 * i, [P, S], F32R) for i in range(2)]
        slo = [small(f"slo{i}", 888 + 512 + 256 * i, [P, S], F32R) for i in range(2)]
        gam = small("gam", 1912, [P, NB, NC])
        mx = small("mx", 1944, [P, 2, 4])
        nmx = small("nmx", 1952, [P, 2, 4])
        sums = small("sums", 1960, [P, 2, 4])
        coef = small("coef", 1968, [P, 2, 4])
        lam = small("lam", 1976, [P, 4])
        stats = small("stats", 1984, [P, 4, 6])
        moments = small("moments", 2008, [P, 4])
        mv, rstd = moments[:, 0:2], moments[:, 2:3]

        ps = ctx.enter_context(nc.psum_tensor("ps", [P, 8, 512], F32))

        s_stage = [sem(f"stage_loaded{i}") for i in range(NST)]
        s_hi, s_lo, s_used = sem("hi_ready"), sem("lo_ready"), sem("slab_used")
        s_free, s_mix = sem("acc_free"), sem("mix_scaled")
        s_x = [sem(f"x_loaded{i}") for i in range(4)]
        s_xhi, s_xlo = sem("act_hi_ready"), sem("act_lo_ready")
        s_cst, s_pos, s_attc, s_levc, s_gup = (
            sem("consts_loaded"), sem("positions_loaded"), sem("attention_consts_loaded"),
            sem("level_masks_loaded"), sem("gate_up_loaded"))
        s_ln1c, s_ln2c, s_xres, s_out = (
            sem("ln1_vectors_loaded"), sem("ln2_vectors_loaded"), sem("x_reloaded"), sem("output_stored"))
        s_vec, s_lup = sem("vectors_ready"), sem("lora_weights_loaded")
        s_lora, s_z, s_sig = sem("lora_activated"), sem("decay_logits"), sem("decay_sigmoid")
        s_item, s_itemd, s_gam = sem("rate_or_cumsum"), sem("rate_or_cumsum_done"), sem("chunk_decay_kept")
        s_ang, s_sin, s_tab = sem("angle_step"), sem("sines_ready"), sem("rotary_tables_ready")
        s_rotc, s_rotm, s_rotd = sem("rot_copied"), sem("rot_multiplied"), sem("rotary_done")
        s_sq, s_ss, s_nrm = sem("kk_squares"), sem("kk_sums"), sem("kk_norms")
        s_ew = sem("elementwise_step")
        s_rk, s_bon, s_kk, s_pl = sem("bonus_terms"), sem("bonus_sums"), sem("kk_ready"), sem("pool_step")
        s_vdc = sem("v_copied")
        s_lamd = sem("lambda_step")
        s_lame = sem("lambda_exps")
        s_sc, s_smd, s_exp, s_at, s_atc, s_o, s_oc = (
            sem("scores_ready"), sem("masked_scores_ready"), sem("probs_ready"), sem("attention_transposed"),
            sem("attention_T_copied"), sem("head_out"), sem("head_out_copied"))
        s_attn, s_attd = sem("attention_ready"), sem("attention_step")
        s_osq, s_oss, s_ord, s_yd, s_ydn = (
            sem("out_squares"), sem("out_sums"), sem("out_roots"), sem("diff_step"), sem("diff_out_ready"))
        s_init, s_px, s_xm, s_ptx, s_upd = (
            sem("first_level_ready"), sem("level_x"), sem("level_x_masked"), sem("level_products"),
            sem("level_done"))
        s_tr, s_trc = sem("transposed"), sem("transposed_copied")
        s_kb, s_kbm, s_z1p, s_z1 = sem("kb_products"), sem("kb_masked"), sem("z1_products"), sem("z1_ready")
        s_gm = sem("state_decay_masks")
        s_ks, s_zc, s_u, s_uc, s_sp, s_stm, s_st = (
            sem("state_term"), sem("z_ready"), sem("u_products"), sem("u_ready"), sem("state_products"),
            sem("state_sum"), sem("state_ready"))
        s_rb, s_rbm, s_y, s_yc = sem("read_products"), sem("read_masked"), sem("y_products"), sem("y_copied")
        s_mean, s_cen, s_gsq, s_var, s_sd, s_gn, s_gate, s_yg = (
            sem("gn_means"), sem("gn_centred"), sem("gn_squares"), sem("gn_vars"), sem("gn_roots"),
            sem("gn_step"), sem("gate_ready"), sem("rwkv_out_ready"))
        s_ahi, s_alo = sem("moving_hi_ready"), sem("moving_lo_ready")
        s_ln, s_std, s_lnd, s_lnk = sem("ln_moments"), sem("ln_roots"), sem("ln_done"), sem("ln_chain")
        s_xt, s_x1h, s_x1l = sem("x1_transposed"), sem("x1_hi"), sem("x1_lo")
        s_relu, s_ff = sem("relu_ready"), sem("hidden_ready")

        block = ctx.enter_context(nc.Block())

        def col(v, n=0):
            return vec[:, v + n:v + n + 1]

        def vcol(v, blk):
            return vec[:, bass.ds(blk + v, 1)]

        def over(ap, n):
            return ap.unsqueeze(1).broadcast_to([ap.shape[0], n, ap.shape[1]])

        def f(ap):
            return ap.bitcast(F32)

        SU, IU, ID = cst[:, C_SU:C_SU + P], cst[:, C_IU:C_IU + P], cst[:, C_ID:C_ID + P]
        BD, ONE = cst[:, C_BD:C_BD + P], cst[:, C_ONE:C_ONE + P]
        M1, M1T = levc[:, 0, :], levc[:, 6, :]

        def banks(a, n=2, lo=0, hi=512):
            return ps[:, a:a + n, lo:hi]

        def units(g):
            return [(hp * 4 + b2 * 2 + a, hp, 2 * g + b2, a) for hp in range(2) for b2 in range(2) for a in range(TT_)]

        def quad(s):
            return [(4 * s + j, P * j, s % 2, 2 * (s // 2) + j // 2, j % 2) for j in range(4)]

        def TTm(u):
            return TTh[u // 16][:, u % 16, :]

        def unit(b, hp, a):
            return (b // 2) * 8 + hp * 4 + (b % 2) * 2 + a

        STEPS = [(half, lev, s) for half in range(2) for lev in range(6) for s in range(4)]
        PER_HEAD = len(STEPS) // DH

        def setups(n):
            return sum(lev == 0 for _, lev, _ in STEPS[:n + 1])

        def updates(n):
            return n + 1 - setups(n)

        def hr(hp):
            return slice(HD * hp, HD * hp + HD)

        def tok(a):
            return slice(P * a, P * a + P)

        @block.sync
        def _(sp):
            sp.dma_start(cst[:, :], t["consts"][:, 0:C_SMALL]).then_inc(s_cst, 16)
            sp.dma_start(vec[:, 0:V_IN], t["vecs"]).then_inc(s_cst, 16)
            for j in range(4):
                sp.dma_start(xstage[:, 4 * j:4 * j + 4, :], t["xT"][:, 4 * j:4 * j + 4, :]).then_inc(s_x[j], 16)

            def slab(n, k, src):
                if not (isinstance(n, int) and n < NST):
                    sp.wait_ge(s_lo, n - (NST - 1))
                sp.dma_start(stage[k % NST][:, :], src).then_inc(s_stage[k % NST], 16)

            def slabs(base, first, last, src):
                with sp.Fori(first, last) as i:
                    for k in range(4):
                        slab(i * 4 + (base + k), base + k, src[bass.ds(i * 4 + k, 1), :, :])

            for g in range(4):
                slab(g, g, t["w_in"][g])
                if g == 1:
                    sp.dma_start(wup[:, :], t["w_up"]).then_inc(s_lup, 16)
                    sp.dma_start(aup[64:128, :], t["a_up"]).then_inc(s_lup, 16)
                    sp.dma_start(posi[:, :], t["positions"].partition_broadcast(P)).then_inc(s_pos, 16)
            slabs(4, 0, (G_OUT - 4) // 4, t["w_in"][4:, :, :])
            for g in range(G_OUT // 4 * 4, G_OUT):
                slab(g, g, t["w_in"][g])
            sp.wait_ge(s_lo, G_OUT)
            sp.dma_start(amask[:, :], t["consts"][:, C_ATT:C_ATT + 3 * P]).then_inc(s_attc, 16)
            for j in range(4):
                sp.dma_start(lamv[:, j, :], t["lam"][j:j + 1, :].partition_broadcast(P)).then_inc(s_attc, 16)
            sp.dma_start(levc[:, :, :], t["consts"][:, C_LEV:C_LEV + 7 * P].rearrange("p (l q) -> p l q", l=7)
                         ).then_inc(s_levc, 16)
            sp.wait_ge(s_sp, 2 * (NC - 1))
            sp.dma_start(gup[:, :, :], t["g_up"]).then_inc(s_gup, 16)
            sp.wait_ge(s_y, 4)
            for g in range(G_OUT, G_OUT + 4):
                slab(g, g, t["w_out"][g - G_OUT])
            sp.dma_start(xres[:, :, :], t["x"].rearrange("(a p) d -> p a d", p=P)).then_inc(s_xres, 16)
            sp.dma_start(gain1[:, :], t["ln1_gain"].partition_broadcast(P)).then_inc(s_ln1c, 16)
            sp.dma_start(bias1[:, :], t["ln1_bias"].partition_broadcast(P)).then_inc(s_ln1c, 16)
            slabs(G_OUT + 4, 0, KT // 4 - 1, t["w_out"][4:, :, :])
            slabs(G_FF1, 0, N_FF1 // 2, t["w_ff1"])
            sp.dma_start(gain2[:, :], t["ln2_gain"].partition_broadcast(P)).then_inc(s_ln2c, 16)
            sp.dma_start(bias2[:, :], t["ln2_bias"].partition_broadcast(P)).then_inc(s_ln2c, 16)
            slabs(G_FF2, 0, DFF // P // 4, t["w_ff2"])
            for a in range(TT_):
                sp.wait_ge(s_lnd, TT_ + a + 1)
                sp.dma_start(t["out"][a * P:(a + 1) * P, :], xres[:, a, :]).then_inc(s_out, 16)
            sp.wait_ge(s_out, 16 * TT_)

        @block.tensor
        def _(pe):
            def mm(out, lhsT, rhs, start=True, stop=True):
                return pe.matmul(out, lhsT, rhs, start=start, stop=stop, skip_group_check=True)

            def halves_ready(g):
                pe.wait_ge(s_hi, g + 1)
                pe.wait_ge(s_lo, g + 1)

            def chunk(b0, g, k0, width=256, slabs=2):
                kts = SLAB // width
                for s in range(slabs):
                    w = (k0 + s) % NHL
                    halves_ready(g + s)
                    for j in range(kts):
                        k = s * kts + j
                        for fb in range(width // P):
                            acc = ps[:, b0 + fb, 0:S]
                            cols = slice(j * width + fb * P, j * width + fb * P + P)
                            mm(acc, whi[w][:, cols], acthi[:, k, :], start=(k == 0), stop=False)
                            mm(acc, whi[w][:, cols], actlo[:, k, :], start=False, stop=False)
                            last = mm(acc, wlo[w][:, cols], acthi[:, k, :], start=False, stop=(k == KT - 1))
                    last.then_inc(s_used, 1)

            def rows(g, k0, n, first, last_):
                w, h = k0 % NHL, n % 2
                halves_ready(g)
                for a in range(TT_):
                    for q in range(4):
                        acc = ps[:, 4 * a + q, :]
                        cols = slice(512 * q, 512 * q + 512)
                        mm(acc, shi[h][:, tok(a)], whi[w][:, cols], start=first, stop=False)
                        mm(acc, slo[h][:, tok(a)], whi[w][:, cols], start=False, stop=False)
                        last = mm(acc, shi[h][:, tok(a)], wlo[w][:, cols], start=False, stop=last_)
                last.then_inc(s_used, 1)

            pe.wait_ge(s_xlo, 4)
            chunk(0, 0, 0)
            chunk(2, 2, 2, width=128, slabs=1)
            pe.wait_ge(s_cst, 32)
            pe.wait_ge(s_lup, 32)
            pe.wait_ge(s_lora, 1)
            pe.wait_ge(s_vec, 1)
            for a in range(TT_):
                for q in range(2):
                    mm(ps[:, 4 + 2 * a + q, :], wt[:, tok(a)], wup[:, 512 * q:512 * q + 512]).then_inc(s_z, 1)
            for n in range(2 * NB):
                b, bk = n % NB, 4 + n % 4
                if n < 4:
                    pe.wait_ge(s_sig, n + 1)
                else:
                    pe.wait_ge(s_itemd, n - 3)
                if n < NB:
                    mm(ps[:, bk, 0:S], aup[64:128, P * b:P * b + P], wa[64:128, :]).then_inc(s_item, 1)
                else:
                    for a in range(TT_):
                        last = mm(ps[:, bk, 256 * a:256 * a + 256], sig[:, a, P * b:P * b + P],
                                  cst[:, C_SU:C_SU + 2 * P])
                    last.then_inc(s_item, 1)
            with pe.Fori(0, N_KRV // 2) as i:
                for k in range(2):
                    pe.wait_ge(s_free, i * 2 + (k + 1))
                    chunk(2 * k, i * 4 + (G_KRV + 2 * k), G_KRV + 2 * k)
            with pe.Fori(0, N_QK // 2) as i:
                for k in range(2):
                    pe.wait_ge(s_free, i * 2 + (N_KRV + k + 1))
                    chunk(2 * k, i * 4 + (G_QK + 2 * k), G_QK + 2 * k)
                    pe.wait_ge(s_sq, i * 2 + (k + 1))
                    mm(ps[:, 4 + k, 0:S], BD, sqt[:, k, :]).then_inc(s_ss, 1)
                    pe.wait_ge(s_rk, i * 2 + (k + 1))
                    mm(ps[:, 6 + k, 0:S], BD, rkt_[:, k, :]).then_inc(s_bon, 1)
            for m in range(2):
                pe.wait_ge(s_free, 2 + N_KRV + N_QK - 1 + m)
                for s in range(4):
                    g = G_VD + 4 * m + s
                    halves_ready(g)
                    w = g % NHL
                    for j in range(4):
                        k = 4 * s + j
                        for a in range(TT_):
                            acc = ps[:, 2 * m + a, :]
                            cols = slice(512 * j, 512 * j + 512)
                            mm(acc, acthi[:, k, tok(a)], whi[w][:, cols], start=(k == 0), stop=False)
                            mm(acc, actlo[:, k, tok(a)], whi[w][:, cols], start=False, stop=False)
                            last = mm(acc, acthi[:, k, tok(a)], wlo[w][:, cols], start=False, stop=(k == KT - 1))
                    last.then_inc(s_used, 1)

            def attention(h, part):
                if part == 0:
                    if h:
                        pe.wait_ge(s_ord, h)
                    for c in range(2):
                        for a in range(TT_):
                            o = (0, P)[a]
                            last = mm(ps[:, 6 + c, o:o + P * (a + 1)], qk[hr(c), h, tok(a)],
                                      qk[hr(c), DH + h, 0:P * (a + 1)])
                    last.then_inc(s_sc, 1)
                elif part == 3:
                    pe.wait_ge(s_attn, h + 1)
                    for j in range(3):
                        last = pe.transpose(ps[:, 6, P * j:P * j + P], att[:, P * j:P * j + P], ID)
                    last.then_inc(s_at, 1)
                elif part == 4:
                    pe.wait_ge(s_atc, h + 1)
                    mm(ps[:, 7, 0:S], vd[:, 0, P * h:P * h + P], attT[:, 0:S], stop=False)
                    mm(ps[:, 7, P:S], vd[:, 1, P * h:P * h + P], attT[:, S:3 * P], start=False).then_inc(s_o, 1)
                elif part == 5:
                    pe.wait_ge(s_osq, h + 1)
                    mm(ps[:, 6, 0:S], ONE, osq[:, :]).then_inc(s_oss, 1)

            def level_x(n):
                half, lev, s = STEPS[n]
                bk = 2 * (n % 3)
                if n >= 3:
                    if STEPS[n - 3][1]:
                        pe.wait_ge(s_upd, updates(n - 3))
                    else:
                        pe.wait_ge(s_xm, n - 2)
                if lev == 0:
                    for u, o, hp, b, a in quad(4 * half + s):
                        mm(ps[:, bk, o:o + P], kr[hr(hp), b, a, 0, :], bt[hr(hp), b, tok(a)])
                        last = mm(ps[:, bk + 1, o:o + P], bt[hr(hp), b, tok(a)], kr[hr(hp), b, a, 0, :])
                else:
                    if lev == 1:
                        pe.wait_ge(s_init, setups(n - 4))
                    for u, o, hp, b, a in quad(4 * half + s):
                        last = mm(ps[:, bk, o:o + P], AT[:, u % 16, :], TM[:, u % 16, :])
                last.then_inc(s_px, 1)

            def level_t(n):
                half, lev, s = STEPS[n]
                bk = 2 * (n % 3)
                if lev == 0:
                    return
                pe.wait_ge(s_xm, n + 1)
                for u, o, hp, b, a in quad(4 * half + s):
                    if lev < 5:
                        mm(ps[:, bk, o:o + P], TTm(u), XM[:, u % 16, :])
                    last = mm(ps[:, bk + 1, o:o + P], XM[:, u % 16, :], TTm(u))
                last.then_inc(s_ptx, 1)

            pe.wait_ge(s_rotd, N_QK)
            pe.wait_ge(s_vdc, 4)
            pe.wait_ge(s_pl, 4 * NB)
            level_x(0)
            for n in range(len(STEPS)):
                if n + 1 < len(STEPS):
                    level_x(n + 1)
                level_t(n)
                attention(n // PER_HEAD, n % PER_HEAD)
            pe.wait_ge(s_upd, updates(len(STEPS) - 1))
            pe.wait_ge(s_ord, DH)
            for n in range(12):
                src = [lambda b: krv[:, 2 * NB + b, :], lambda b: bt[:, b, :], lambda b: ki[:, b, :]][n // 4]
                if n >= 8:
                    pe.wait_ge(s_trc, n - 7)
                for b2 in range(2):
                    for a in range(TT_):
                        o = P * (2 * b2 + a)
                        last = pe.transpose(ps[:, n % 8, o:o + P], src(2 * (n % 4) + b2)[:, tok(a)], ID)
                last.then_inc(s_tr, 1)
            def kb(g):
                if g >= 2:
                    pe.wait_ge(s_kbm, g - 1)
                for ul, hp, b, a in units(g):
                    o = P * (ul % 4)
                    last = mm(ps[:, 4 * (g % 2) + hp, o:o + P], ki[hr(hp), b, tok(a)], kr[hr(hp), b, a, 0, :])
                last.then_inc(s_kb, 1)

            pe.wait_ge(s_trc, 12)
            kb(0)
            for g in range(4):
                if g + 1 < 4:
                    kb(g + 1)
                pe.wait_ge(s_kbm, g + 1)
                if g >= 2:
                    pe.wait_ge(s_z1, g - 1)
                for ul, hp, b, a in units(g):
                    o = P * (2 * (b % 2) + a) + HD * hp
                    last = mm(ps[:, 4 * (g % 2) + 2, o:o + HD], kbt[g % 2][:, ul, :], vtm[:, b, a, hr(hp)])
                last.then_inc(s_z1p, 1)
            def read(s):
                if s:
                    pe.wait_ge(s_rbm, s)
                for u, o, hp, b, a in quad(s):
                    mm(ps[:, 6, o:o + P], bt[hr(hp), b, tok(a)], kr[hr(hp), b, a, 1, :])
                    last = mm(ps[:, 7, o:o + P], ki[hr(hp), b, tok(a)], kr[hr(hp), b, a, 1, :])
                last.then_inc(s_rb, 1)

            pe.wait_ge(s_z1, 4)
            for c in range(NC):
                a, cb = c // 2, C * (c % 2)
                rw = slice(cb, cb + C)
                if c:
                    for G in range(2):
                        pe.wait_ge(s_st, 2 * (c - 1) + G + 1)
                        for j in range(4):
                            b = 4 * G + j
                            last = mm(ps[rw, 3 * G, P * j:P * j + P], kr[:, b, a, 0, rw], st[c][:, b, :])
                        last.then_inc(s_ks, 1)
                for G in range(2):
                    if c:
                        pe.wait_ge(s_zc, 2 * (c - 1) + G + 1)
                    if c:
                        pe.wait_ge(s_uc, 2 * (c - 1) + G + 1)
                    for j in range(4):
                        b = 4 * G + j
                        for hp in range(2):
                            last = mm(ps[rw, 3 * G + 1, P * j + HD * hp:P * j + HD * hp + HD],
                                      TTm(unit(b, hp, a))[:, rw], z1[:, b, a, hr(hp)])
                    last.then_inc(s_u, 1)
                read(2 * c)
                if c == NC - 1:
                    break
                for G in range(2):
                    pe.wait_ge(s_uc, 2 * c + G + 1)
                    for j in range(4):
                        b = 4 * G + j
                        o = ps[:, 3 * G + 2, P * j:P * j + P]
                        mm(o, ktm[rw, b, a, :], vtm[rw, b, a, :], stop=False)
                        last = mm(o, btm[rw, b, a, :], um[rw, b, a, :], start=False)
                    last.then_inc(s_sp, 1)
                read(2 * c + 1)
            read(2 * NC - 1)
            def read_out(g):
                for b2 in range(2):
                    b = 2 * g + b2
                    for a in range(TT_):
                        o = P * (2 * b2 + a)
                        for hp in range(2):
                            out = ps[hr(hp), 4 + g, o:o + P]
                            u = unit(b, hp, a)
                            mm(out, vtm[:, b, a, hr(hp)], rkt[:, u, :], stop=False)
                            last = mm(out, um[:, b, a, hr(hp)], rbt[:, u, :], start=False)
                        for cc in range(2):
                            c = 2 * a + cc
                            if c:
                                last = mm(ps[:, 4 + g, o + C * cc:o + C * cc + C], st[c][:, b, :],
                                          kr[:, b, a, 1, C * cc:C * cc + C], start=False)
                last.then_inc(s_y, 1)

            def mean(g):
                pe.wait_ge(s_yc, g + 1)
                mm(ps[:, g, :], BD, yf[:, 2 * g:2 * g + 2, :]).then_inc(s_mean, 1)

            def var(g):
                pe.wait_ge(s_gsq, g + 1)
                mm(ps[:, g, :], BD, gsq[:, 2 * g:2 * g + 2, :]).then_inc(s_var, 1)

            def gate(g):
                for j in range(2):
                    b = 2 * g + j
                    for q in range(2):
                        last = mm(ps[:, 4 + g, S * j:S * j + S], gup[:, q, P * b:P * b + P], sg[q][:, :],
                                  start=(q == 0), stop=(q == 1))
                last.then_inc(s_gate, 1)

            pe.wait_ge(s_uc, 2 * NC)
            pe.wait_ge(s_rbm, 2 * NC)
            read_out(0)
            read_out(1)
            mean(0)
            read_out(2)
            mean(1)
            var(0)
            read_out(3)
            mean(2)
            var(1)
            pe.wait_ge(s_gup, 16)
            gate(0)
            mean(3)
            var(2)
            gate(1)
            var(3)
            gate(2)
            gate(3)

            pe.wait_ge(s_yg, 4)
            pe.wait_ge(s_ydn, DH)
            for n in range(4):
                pe.wait_ge(s_ahi, n + 1)
                pe.wait_ge(s_alo, n + 1)
                rows(G_OUT + n, G_OUT + n, n, n == 0, False)
            with pe.Fori(1, KT // 4 - 1) as i:
                for k in range(4):
                    pe.wait_ge(s_ahi, i * 4 + (k + 1))
                    pe.wait_ge(s_alo, i * 4 + (k + 1))
                    rows(i * 4 + (G_OUT + k), G_OUT + k, k, False, False)
            for n in range(KT - 4, KT):
                pe.wait_ge(s_ahi, n + 1)
                pe.wait_ge(s_alo, n + 1)
                rows(G_OUT + n, G_OUT + n, n, False, n == KT - 1)
            for n in range(8):
                a, j = n // 4, n % 4
                pe.wait_ge(s_lnd, a + 1)
                for q in range(4):
                    k = 4 * j + q
                    last = pe.transpose(ps[:, n, P * q:P * q + P], xres[:, a, P * k:P * k + P], ID)
                last.then_inc(s_xt, 1)
            pe.wait_ge(s_x1l, 8)
            for k in range(2):
                chunk(2 * k, G_FF1 + 2 * k, G_FF1 + 2 * k)
            with pe.Fori(1, N_FF1 // 2) as i:
                for k in range(2):
                    pe.wait_ge(s_ff, i * 2 + (k - 1))
                    chunk(2 * k, i * 4 + (G_FF1 + 2 * k), G_FF1 + 2 * k)
            pe.wait_ge(s_ff, N_FF1)
            NF = DFF // P
            for n in range(4):
                pe.wait_ge(s_ahi, KT + n + 1)
                pe.wait_ge(s_alo, KT + n + 1)
                rows(G_FF2 + n, G_FF2 + n, n, n == 0, False)
            with pe.Fori(1, NF // 4 - 1) as i:
                for k in range(4):
                    pe.wait_ge(s_ahi, i * 4 + (KT + k + 1))
                    pe.wait_ge(s_alo, i * 4 + (KT + k + 1))
                    rows(i * 4 + (G_FF2 + k), G_FF2 + k, k, False, False)
            for n in range(NF - 4, NF):
                pe.wait_ge(s_ahi, KT + n + 1)
                pe.wait_ge(s_alo, KT + n + 1)
                rows(G_FF2 + n, G_FF2 + n, n, False, n == NF - 1)

        @block.scalar
        def _(act):
            def A(out, in_, func, **kw):
                return act.activation(out, in_, func, **kw)

            def hi(g, k0):
                act.wait_ge(s_stage[k0 % NST], (g - k0) * 4 + 16 * (k0 // NST + 1))
                if not (isinstance(g, int) and g < 2):
                    act.wait_ge(s_used, g - 1)
                A(whi[k0 % NHL][:, :], stage[k0 % NST][:, :], ACT.Copy).then_inc(s_hi, 1)

            def split(src, g, n, h):
                act.wait_ge(s_used, g - 1)
                A(shi[h][:, :], src, ACT.Copy).then_inc(s_ahi, 1)

            for j in range(4):
                act.wait_ge(s_x[j], 16)
                A(acthi[:, 4 * j:4 * j + 4, :], xstage[:, 4 * j:4 * j + 4, :], ACT.Copy).then_inc(s_xhi, 1)
                if j == 1:
                    hi(0, 0)
            hi(1, 1)
            hi(2, 2)
            act.wait_ge(s_vec, 1)
            act.wait_ge(s_used, 2)
            A(wa[:, :], ps[:, 0, 0:S], ACT.Copy, scale=col(V_OMMU, 24))
            A(sg[0][:, :], ps[:, 1, 0:S], ACT.Copy, scale=col(V_OMMU, 25)).then_inc(s_mix, 1)
            hi(3, 3)
            act.wait_ge(s_free, 1)
            A(wt[0:64, :], wa[0:64, :], ACT.Tanh).then_inc(s_lora, 1)
            act.wait_ge(s_used, 3)
            A(sg[1][:, :], ps[:, 2, 0:S], ACT.Copy, scale=col(V_OMMU, 26)).then_inc(s_mix, 1)
            A(sg[0][:, :], sg[0][:, :], ACT.Sigmoid).then_inc(s_lora, 1)
            act.wait_ge(s_free, 2)
            A(sg[1][:, :], sg[1][:, :], ACT.Sigmoid).then_inc(s_lora, 1)
            for n in range(4):
                act.wait_ge(s_z, n + 1)
                A(sig[:, n // 2, 512 * (n % 2):512 * (n % 2) + 512], ps[:, 4 + n, :], ACT.Sigmoid).then_inc(s_sig, 1)
            for n in range(2 * NB):
                b, bk = n % NB, 4 + n % 4
                act.wait_ge(s_item, n + 1)
                if n < NB:
                    A(bt[:, b, :], ps[:, bk, 0:S], ACT.Sigmoid, bias=col(V_A0, b)).then_inc(s_itemd, 1)
                else:
                    A(kr[:, b, :, :, :].rearrange("p a e q -> p (a e q)"), ps[:, bk, :], ACT.Exp, scale=-DECAY)
                    A(e2[:, b, :].rearrange("p (a q) -> p a q", a=TT_),
                      ps[:, bk, :].rearrange("p (a e q) -> p a e q", a=TT_, e=2)[:, :, 1, :],
                      ACT.Exp, scale=DECAY).then_inc(s_itemd, 1)
            act.wait_ge(s_ang, 9)
            A(sinb[:, :], angt[0][:, :], ACT.Sin).then_inc(s_sin, 1)
            A(cosb[:, :], angt[2][:, :], ACT.Sin).then_inc(s_sin, 1)
            with act.Fori(0, N_KRV // 2) as i:
                for k in range(2):
                    k0 = G_KRV + 2 * k
                    hi(i * 4 + (k0 + 1), k0 + 1)
                    hi(i * 4 + (k0 + 2), k0 + 2)
                    act.wait_ge(s_used, i * 4 + (k0 + 2))
                    for fb in range(2):
                        blk = i * 4 + (2 * k + fb)
                        last = A(krv[:, bass.ds(blk, 1), :].squeeze(1), ps[:, 2 * k + fb, 0:S], ACT.Copy,
                                 scale=vcol(V_OMMU, blk))
                    last.then_inc(s_mix, 1)
            with act.Fori(0, N_QK // 2) as i:
                for k in range(2):
                    k0 = G_QK + 2 * k
                    b = i * 2 + k
                    hi(i * 4 + (k0 + 1), k0 + 1)
                    act.wait_ge(s_free, 2 + N_KRV)
                    A(sqt[:, k, :], krv[:, bass.ds(b, 1), :].squeeze(1), ACT.Square, scale=vcol(V_KK, b)
                      ).then_inc(s_sq, 1)
                    hi(i * 4 + (k0 + 2), k0 + 2)
                    act.wait_ge(s_used, i * 4 + (k0 + 2))
                    for j in range(4):
                        o, s = 32 * j, 32 * (j ^ 1)
                        last = A(rot[k][o:o + 32, :, :], ps[s:s + 32, 2 * k:2 * k + 2, 0:S], ACT.Copy)
                    last.then_inc(s_rotc, 1)
                    act.wait_ge(s_ss, b + 1)
                    A(inv[:, k, :], ps[:, 4 + k, 0:S], ACT.Sqrt).then_inc(s_nrm, 1)
            for m in range(2):
                g = G_VD + 4 * m
                for s in range(1, 5):
                    if g + s < G_OUT:
                        hi(g + s, g + s)
                act.wait_ge(s_used, g + 4)
                act.wait_ge(s_rotd, N_QK)
                for a in range(TT_):
                    A(vd[:, a, 512 * m:512 * m + 512], ps[:, 2 * m + a, :], ACT.Copy).then_inc(s_vdc, 1)
            act.wait_ge(s_lamd, 2)
            A(lam[:, 0:2], lam[:, 0:2], ACT.Exp).then_inc(s_lame, 1)

            for h in range(DH):
                act.wait_ge(s_smd, h + 1)
                for c in range(2):
                    for a in range(TT_):
                        o = (0, P)[a]
                        last = A(pr[:, c, o:o + P * (a + 1)], sm[:, c, o:o + P * (a + 1)], ACT.Exp,
                                 scale=HD ** -0.5, bias=nmx[:, 0, 2 * c + a:2 * c + a + 1],
                                 accum_out=sums[:, 0, 2 * c + a:2 * c + a + 1])
                last.then_inc(s_exp, 1)
                act.wait_ge(s_at, h + 1)
                A(attT[:, :], ps[:, 6, 0:3 * P], ACT.Copy).then_inc(s_atc, 1)
                act.wait_ge(s_o, h + 1)
                A(osq[:, :], ps[:, 7, 0:S], ACT.Square).then_inc(s_osq, 1)
                A(yt[:, NB + h, :], ps[:, 7, 0:S], ACT.Copy).then_inc(s_oc, 1)
                act.wait_ge(s_oss, h + 1)
                if h:
                    act.wait_ge(s_ydn, h)
                A(oinv[:, :], ps[:, 6, 0:S], ACT.Sqrt, scale=1.0 / P, bias=col(V_SUBEPS)).then_inc(s_ord, 1)
            for n in range(12):
                act.wait_ge(s_tr, n + 1)
                dst = (vtm, btm, ktm)[n // 4]
                j = n % 4
                A(dst[:, 2 * j:2 * j + 2, :, :].rearrange("p b a q -> p (b a q)"), ps[:, n % 8, :], ACT.Copy
                  ).then_inc(s_trc, 1)
            for g in range(4):
                act.wait_ge(s_z1p, g + 1)
                A(z1[:, 2 * g:2 * g + 2, :, :].rearrange("p b a q -> p (b a q)"), ps[:, 4 * (g % 2) + 2, :], ACT.Copy
                  ).then_inc(s_z1, 1)
            for c in range(NC):
                a, cb = c // 2, C * (c % 2)
                for G in range(2):
                    act.wait_ge(s_u, 2 * c + G + 1)
                    A(um[cb:cb + C, 4 * G:4 * G + 4, a, :],
                      ps[cb:cb + C, 3 * G + 1, :].rearrange("p (b q) -> p b q", b=4), ACT.Copy).then_inc(s_uc, 1)
            def copied(g):
                act.wait_ge(s_y, g + 1)
                A(yf[:, 2 * g:2 * g + 2, :].rearrange("p b q -> p (b q)"), ps[:, 4 + g, :], ACT.Copy).then_inc(s_yc, 1)

            def squared(g):
                act.wait_ge(s_cen, g + 1)
                A(gsq[:, 2 * g:2 * g + 2, :], yf[:, 2 * g:2 * g + 2, :], ACT.Square).then_inc(s_gsq, 1)

            def rooted(g):
                act.wait_ge(s_var, g + 1)
                A(gsq[:, 2 * g:2 * g + 2, :].rearrange("p b q -> p (b q)"), ps[:, g, :], ACT.Sqrt, scale=1.0 / HD,
                  bias=col(V_GNEPS)).then_inc(s_sd, 1)

            copied(0)
            copied(1)
            squared(0)
            copied(2)
            rooted(0)
            squared(1)
            copied(3)
            rooted(1)
            squared(2)
            squared(3)
            rooted(2)
            rooted(3)
            hi(G_OUT, G_OUT)
            act.wait_ge(s_yg, 4)
            act.wait_ge(s_gate, 4)
            act.wait_ge(s_ydn, DH)
            A(shi[0][:, :], yt[:, 0, :], ACT.Copy).then_inc(s_ahi, 1)
            with act.Fori(0, KT // 4 - 1) as i:
                for k in range(4):
                    hi(i * 4 + (G_OUT + k + 1), G_OUT + k + 1)
                    split(yt[:, bass.ds(i * 4 + (k + 1), 1), :].squeeze(1), i * 4 + (G_OUT + k + 1), None, (k + 1) % 2)
            for k in range(KT - 4, KT):
                hi(G_OUT + k + 1, G_OUT + k + 1)
                if k + 1 < KT:
                    split(yt[:, k + 1, :], G_OUT + k + 1, None, (k + 1) % 2)

            def roots(n):
                act.wait_ge(s_ln, n + 1)
                A(rstd[:, :], mv[:, 1:2], ACT.Sqrt, bias=col(V_LNEPS)).then_inc(s_std, 1)

            roots(0)
            roots(1)
            for n in range(8):
                act.wait_ge(s_xt, n + 1)
                a, j = n // 4, n % 4
                A(acthi[:, 4 * j:4 * j + 4, tok(a)], ps[:, n, :].rearrange("p (k q) -> p k q", k=4), ACT.Copy
                  ).then_inc(s_x1h, 1)
            with act.Fori(0, N_FF1 // 2) as i:
                for k in range(2):
                    k0 = G_FF1 + 2 * k
                    hi(i * 4 + (k0 + 1), k0 + 1)
                    hi(i * 4 + (k0 + 2), k0 + 2)
                    act.wait_ge(s_used, i * 4 + (k0 + 2))
                    A(hid[:, bass.ds(i * 4 + 2 * k, 2), :], ps[:, 2 * k:2 * k + 2, 0:S], ACT.Relu).then_inc(s_relu, 1)
            act.wait_ge(s_ff, 1)
            A(shi[0][:, :], hid[:, 0, :], ACT.Copy).then_inc(s_ahi, 1)
            NF = DFF // P
            act.wait_ge(s_ff, N_FF1)
            with act.Fori(0, NF // 4 - 1) as i:
                for k in range(4):
                    hi(i * 4 + (G_FF2 + k + 1), G_FF2 + k + 1)
                    split(hid[:, bass.ds(i * 4 + (k + 1), 1), :].squeeze(1), i * 4 + (G_FF2 + k + 1), None, (k + 1) % 2)
            for k in range(NF - 4, NF - 1):
                hi(G_FF2 + k + 1, G_FF2 + k + 1)
                split(hid[:, k + 1, :], G_FF2 + k + 1, None, (k + 1) % 2)
            roots(2)
            roots(3)

        @block.vector
        def _(dve):
            TTn, TS, STT = dve.tensor_tensor, dve.tensor_scalar, dve.scalar_tensor_tensor

            def lo(g, k0):
                dve.wait_ge(s_hi, g + 1)
                if not (isinstance(g, int) and g < 2):
                    dve.wait_ge(s_used, g - 1)
                TTn(wlo[k0 % NHL][:, :], stage[k0 % NST][:, :], f(whi[k0 % NHL][:, :]), ALU.subtract
                    ).then_inc(s_lo, 1)

            def mix(out, acc, mu):
                return STT(out[:, 1:S], acc[:, 0:S - 1], mu, out[:, 1:S], ALU.mult, ALU.add)

            dve.wait_ge(s_cst, 32)
            dve.memset(wt[64:65, :], 1.0)
            TS(vec[:, V_OMMU:V_OMMU + 27], vec[:, V_MU:V_MU + 27], -1.0, 1.0, ALU.mult, ALU.add)
            TS(vec[:, V_OMKA:V_OMKA + 8], vec[:, V_KA:V_KA + 8], -1.0, 1.0, ALU.mult, ALU.add)
            TS(vec[:, V_G08:V_G08 + 1], vec[:, V_SG:V_SG + 1], 1.0 - LAMBDA_INIT, None, ALU.mult).then_inc(s_vec, 1)
            for j in range(4):
                dve.wait_ge(s_xhi, j + 1)
                TTn(actlo[:, 4 * j:4 * j + 4, :], xstage[:, 4 * j:4 * j + 4, :], f(acthi[:, 4 * j:4 * j + 4, :]),
                    ALU.subtract).then_inc(s_xlo, 1)
            for g in range(3):
                lo(g, g)
            dve.wait_ge(s_mix, 1)
            mix(wa, ps[:, 0, :], col(V_MU, 24))
            mix(sg[0], ps[:, 1, :], col(V_MU, 25)).then_inc(s_free, 1)
            lo(3, 3)
            dve.wait_ge(s_mix, 2)
            mix(sg[1], ps[:, 2, :], col(V_MU, 26)).then_inc(s_free, 1)
            dve.wait_ge(s_pos, 16)
            MAGIC = 1.5 * 2 ** 23
            n = 0

            def ang(ins):
                nonlocal n
                n += 1
                ins.then_inc(s_ang, 1)
                dve.wait_ge(s_ang, n)

            ang(dve.tensor_copy(angt[0][:, :], posi[:, :]))
            ang(TS(angt[0][:, :], angt[0][:, :], col(V_INVF), None, ALU.mult))
            ang(TS(angt[1][:, :], angt[0][:, :], 1.0 / (2.0 * math.pi), MAGIC, ALU.mult, ALU.add))
            ang(TS(angt[1][:, :], angt[1][:, :], MAGIC, None, ALU.subtract))
            for part in (6.28125, 2029.0 / 2 ** 20, 2.0 * math.pi - 6.28125 - 2029.0 / 2 ** 20):
                ang(STT(angt[0][:, :], angt[1][:, :], -part, angt[0][:, :], ALU.mult, ALU.add))
            ang(TS(angt[0][:, :], angt[0][:, :], 3.1415925, -3.1415925, ALU.min, ALU.max))
            dve.wait_ge(s_ang, 8)
            STT(angt[2][:, :], angt[0][:, :], -1.0, angt[0][:, :], ALU.mult, ALU.max).then_inc(s_tab, 1)
            dve.wait_ge(s_tab, 1)
            TS(angt[2][:, :], angt[2][:, :], -1.0, math.pi / 2, ALU.mult, ALU.add).then_inc(s_ang, 1)
            dve.wait_ge(s_sin, 1)
            TS(sinb[:, :], sinb[:, :], col(V_SIGN), None, ALU.mult).then_inc(s_tab, 1)
            dve.wait_ge(s_itemd, 16)
            dve.tensor_copy(gam[:, :, :].rearrange("p b c -> p (b c)").rearrange("p (m c) -> p m c", c=2),
                            kr[:, :, :, 1, C - 1::C].rearrange("p b a c -> p (b a) c")).then_inc(s_gam, 1)
            with dve.Fori(0, N_KRV // 2) as i:
                for k in range(2):
                    k0 = G_KRV + 2 * k
                    lo(i * 4 + (k0 + 1), k0 + 1)
                    lo(i * 4 + (k0 + 2), k0 + 2)
                    dve.wait_ge(s_mix, i * 2 + (k + 3))
                    for fb in range(2):
                        blk = i * 4 + (2 * k + fb)
                        out = krv[:, bass.ds(blk, 1), 1:S].squeeze(1)
                        last = STT(out, ps[:, 2 * k + fb, 0:S - 1], vcol(V_MU, blk), out, ALU.mult, ALU.add)
                    last.then_inc(s_free, 1)
            dve.wait_ge(s_tab, 2)
            dve.wait_ge(s_sin, 2)
            dve.wait_ge(s_gam, 1)
            dve.wait_ge(s_free, 2 + N_KRV)
            with dve.Fori(0, N_QK // 2) as i:
                for k in range(2):
                    k0 = G_QK + 2 * k
                    b = i * 2 + k

                    def at_b(x, o=0):
                        return x[:, bass.ds(b + o, 1), :].squeeze(1)

                    K, R, V = at_b(krv), at_b(krv, NB), at_b(krv, 2 * NB)
                    lo(i * 4 + (k0 + 1), k0 + 1)
                    E = i * 10 + 5 * k
                    TS(at_b(ki), at_b(bt), vcol(V_KA, b), vcol(V_OMKA, b), ALU.mult, ALU.add).then_inc(s_ew, 1)
                    dve.wait_ge(s_ew, E + 1)
                    TTn(at_b(ki), K, at_b(ki), ALU.mult).then_inc(s_ew, 1)
                    dve.wait_ge(s_ew, E + 2)
                    STT(rkt_[:, k, :], R, vcol(V_RK, b), at_b(ki), ALU.mult, ALU.mult).then_inc(s_rk, 1)
                    rt = kr[:, bass.ds(b, 1), :, 1, :].squeeze(1)
                    TTn(rt, rt, R.rearrange("p (a q) -> p a q", a=TT_), ALU.mult).then_inc(s_ew, 1)
                    lo(i * 4 + (k0 + 2), k0 + 2)
                    dve.wait_ge(s_rotc, b + 1)
                    TTn(rot[k][:, :, :], rot[k][:, :, :], over(sinb[:, :], 2), ALU.mult).then_inc(s_rotm, 1)
                    out = qk[:, bass.ds(b * 2, 2), :]
                    TTn(out, ps[:, 2 * k:2 * k + 2, 0:S], over(cosb[:, :], 2), ALU.mult).then_inc(s_free, 1)
                    dve.wait_ge(s_rotm, b + 1)
                    dve.wait_ge(s_free, b + (2 + N_KRV + 1))
                    TTn(out, out, rot[k][:, :, :], ALU.add).then_inc(s_rotd, 1)
                    dve.wait_ge(s_nrm, b + 1)
                    TS(inv[:, k, :], inv[:, k, :], 1e-12, None, ALU.max).then_inc(s_ew, 1)
                    dve.wait_ge(s_ew, E + 4)
                    dve.reciprocal(inv[:, k, :], inv[:, k, :]).then_inc(s_ew, 1)
                    dve.wait_ge(s_ew, E + 5)
                    STT(K, K, vcol(V_KK, b), inv[:, k, :], ALU.mult, ALU.mult).then_inc(s_kk, 1)
                    dve.wait_ge(s_bon, b + 1)
                    TTn(R, V, ps[:, 6 + k, 0:S], ALU.mult).then_inc(s_kk, 1)
            for g in range(G_VD + 1, G_OUT):
                lo(g, g)
            dve.wait_ge(s_attc, 80)
            for j in range(2):
                dve.tensor_tensor_reduce(lamt[:, j, :], lamv[:, 2 * j, :], lamv[:, 2 * j + 1, :], 1.0, 0.0,
                                         ALU.mult, ALU.add, lam[:, j:j + 1]).then_inc(s_lamd, 1)
            dve.wait_ge(s_lame, 1)
            TTn(lam[:, 2:3], lam[:, 1:2], lam[:, 0:1], ALU.subtract).then_inc(s_lamd, 1)
            dve.wait_ge(s_lamd, 3)
            TS(lam[:, 3:4], lam[:, 2:3], LAMBDA_INIT, None, ALU.subtract).then_inc(s_lamd, 1)
            dve.wait_ge(s_lamd, 4)

            ad = 0

            def attention(h, part):
                nonlocal ad

                def link(ins):
                    nonlocal ad
                    ad += 1
                    ins.then_inc(s_attd, 1)
                    dve.wait_ge(s_attd, ad)

                if part == 0:
                    dve.wait_ge(s_sc, h + 1)
                    for c in range(2):
                        for a in range(TT_):
                            o = (0, P)[a]
                            last = dve.tensor_tensor_reduce(
                                sm[:, c, o:o + P * (a + 1)], ps[:, 6 + c, o:o + P * (a + 1)],
                                amask[:, o:o + P * (a + 1)], 1.0, -3e38, ALU.add, ALU.max,
                                mx[:, 0, 2 * c + a:2 * c + a + 1])
                    link(last)
                    TS(nmx[:, 0, :], mx[:, 0, :], -HD ** -0.5, None, ALU.mult).then_inc(s_smd, 1)
                elif part == 2:
                    dve.wait_ge(s_exp, h + 1)
                    link(dve.reciprocal(coef[:, 0, :], sums[:, 0, :]))
                    TS(coef[:, 0, 2:4], coef[:, 0, 2:4], lam[:, 3:4], None, ALU.mult)
                    for a in range(TT_):
                        o = (0, P)[a]
                        last = TS(att[:, o:o + P * (a + 1)], pr[:, 0, o:o + P * (a + 1)], coef[:, 0, a:a + 1], None,
                                  ALU.mult)
                    link(last)
                    for a in range(TT_):
                        o = (0, P)[a]
                        last = STT(att[:, o:o + P * (a + 1)], pr[:, 1, o:o + P * (a + 1)],
                                   coef[:, 0, 2 + a:3 + a], att[:, o:o + P * (a + 1)], ALU.mult, ALU.add)
                    last.then_inc(s_attn, 1)
                elif part == 5:
                    dve.wait_ge(s_ord, h + 1)
                    link(dve.reciprocal(oinv[:, :], oinv[:, :]))
                    STT(yt[:, NB + h, :], yt[:, NB + h, :], col(V_G08), oinv[:, :], ALU.mult, ALU.mult
                        ).then_inc(s_ydn, 1)

            def level_x(n):
                half, lev, s = STEPS[n]
                bk, u, uh = 2 * (n % 3), slice(4 * s, 4 * s + 4), TTh[half]
                ab = ps[:, bk, :].rearrange("p (u q) -> p u q", q=P)
                bb = ps[:, bk + 1, :].rearrange("p (u q) -> p u q", q=P)
                dve.wait_ge(s_px, n + 1)
                if lev == 0:
                    STT(TM[:, u, :], ab, -1.0, over(M1, 4), ALU.mult, ALU.mult)
                    STT(uh[:, u, :], bb, -1.0, over(M1T, 4), ALU.mult, ALU.mult)
                    TTn(AT[:, u, :], bb, over(SU, 4), ALU.mult).then_inc(s_xm, 1)
                else:
                    TTn(XM[:, u, :], ab, over(levc[:, lev, :], 4), ALU.mult).then_inc(s_xm, 1)

            def level_t(n):
                half, lev, s = STEPS[n]
                if lev == 0:
                    return
                bk, u = 2 * (n % 3), slice(4 * s, 4 * s + 4)
                ab = ps[:, bk, :].rearrange("p (u q) -> p u q", q=P)
                bb = ps[:, bk + 1, :].rearrange("p (u q) -> p u q", q=P)
                tm, tt = TM[:, u, :], TTh[half][:, u, :]
                dve.wait_ge(s_ptx, updates(n))
                if lev < 5:
                    TTn(tm, tm, ab, ALU.subtract)
                    TTn(tt, tt, bb, ALU.subtract).then_inc(s_upd, 1)
                else:
                    TTn(tt, bb, tt, ALU.subtract).then_inc(s_upd, 1)

            dve.wait_ge(s_levc, 16)
            level_x(0)
            for n in range(len(STEPS)):
                if n + 1 < len(STEPS):
                    level_x(n + 1)
                level_t(n)
                attention(n // PER_HEAD, n % PER_HEAD)
            for g in range(4):
                dve.wait_ge(s_kb, g + 1)
                if g >= 2:
                    dve.wait_ge(s_z1p, g - 1)
                TTn(kbt[g % 2][:, :, :], banks(4 * (g % 2)).rearrange("p h (u q) -> p (h u) q", q=P), over(SU, 8),
                    ALU.mult).then_inc(s_kbm, 1)
            def read(s):
                dve.wait_ge(s_rb, s + 1)
                u = slice(4 * s, 4 * s + 4)
                TTn(rbt[:, u, :], ps[:, 6, :].rearrange("p (u q) -> p u q", q=P), over(IU, 4), ALU.mult)
                TTn(rkt[:, u, :], ps[:, 7, :].rearrange("p (u q) -> p u q", q=P), over(IU, 4), ALU.mult
                    ).then_inc(s_rbm, 1)

            dve.wait_ge(s_gm, 3)
            dve.wait_ge(s_z1, 4)
            for c in range(NC):
                a, cb = c // 2, C * (c % 2)
                if c:
                    for G in range(2):
                        dve.wait_ge(s_ks, 2 * (c - 1) + G + 1)
                        z = z1[cb:cb + C, 4 * G:4 * G + 4, a, :]
                        TTn(z, ps[cb:cb + C, 3 * G, :].rearrange("p (b q) -> p b q", b=4), z, ALU.add
                            ).then_inc(s_zc, 1)
                read(2 * c)
                if c == NC - 1:
                    break
                for G in range(2):
                    dve.wait_ge(s_sp, 2 * c + G + 1)
                    bs = slice(4 * G, 4 * G + 4)
                    pp = ps[:, 3 * G + 2, :].rearrange("p (b q) -> p b q", b=4)
                    if c == 0:
                        TTn(st[1][:, bs, :], pp, gm[0][:, bs, :], ALU.mult).then_inc(s_st, 1)
                    else:
                        TTn(st[c + 1][:, bs, :], pp, st[c][:, bs, :], ALU.add).then_inc(s_stm, 1)
                        dve.wait_ge(s_stm, 2 * (c - 1) + G + 1)
                        TTn(st[c + 1][:, bs, :], st[c + 1][:, bs, :], gm[c][:, bs, :], ALU.mult).then_inc(s_st, 1)
                read(2 * c + 1)
            read(2 * NC - 1)
            def centred(g):
                y512 = yf[:, 2 * g:2 * g + 2, :].rearrange("p b q -> p (b q)")
                dve.wait_ge(s_mean, g + 1)
                STT(y512, ps[:, g, :], -1.0 / HD, y512, ALU.mult, ALU.add).then_inc(s_cen, 1)

            def finished(g):
                bl = slice(2 * g, 2 * g + 2)
                dve.wait_ge(s_sd, g + 1)
                dve.reciprocal(gsq[:, bl, :], gsq[:, bl, :]).then_inc(s_gn, 1)
                dve.wait_ge(s_gn, 3 * g + 1)
                TTn(yf[:, bl, :], yf[:, bl, :], gsq[:, bl, :], ALU.mult).then_inc(s_gn, 1)
                dve.wait_ge(s_gn, 3 * g + 2)
                for b in range(2 * g, 2 * g + 2):
                    last = STT(yf[:, b, :], yf[:, b, :], col(V_GG, b), krv[:, NB + b, :], ALU.mult, ALU.add)
                last.then_inc(s_gn, 1)
                dve.wait_ge(s_gn, 3 * g + 3)
                dve.wait_ge(s_gate, g + 1)
                for j in range(2):
                    b = 2 * g + j
                    last = STT(yt[:, b, :], yf[:, b, :], col(V_GB, b), ps[:, 4 + g, S * j:S * j + S], ALU.add, ALU.mult)
                last.then_inc(s_yg, 1)

            for g in range(3):
                centred(g)
            finished(0)
            centred(3)
            finished(1)
            finished(2)
            lo(G_OUT, G_OUT)
            finished(3)

            def split(src, n, h, used):
                dve.wait_ge(s_ahi, n + 1)
                if used is not None:
                    dve.wait_ge(s_used, used)
                TTn(slo[h][:, :], src, f(shi[h][:, :]), ALU.subtract).then_inc(s_alo, 1)

            split(yt[:, 0, :], 0, 0, None)
            with dve.Fori(0, KT // 4 - 1) as i:
                for k in range(4):
                    lo(i * 4 + (G_OUT + k + 1), G_OUT + k + 1)
                    split(yt[:, bass.ds(i * 4 + (k + 1), 1), :].squeeze(1), i * 4 + (k + 1), (k + 1) % 2,
                          i * 4 + (G_OUT + k))
            for k in range(KT - 4, KT):
                lo(G_OUT + k + 1, G_OUT + k + 1)
                if k + 1 < KT:
                    split(yt[:, k + 1, :], k + 1, (k + 1) % 2, G_OUT + k)

            chain = 0

            def layer_norm(n, gain, bias):
                nonlocal chain

                def link(ins):
                    nonlocal chain
                    chain += 1
                    ins.then_inc(s_lnk, 1)
                    dve.wait_ge(s_lnk, chain)

                for a in range(TT_):
                    for q in range(4):
                        x = xres[:, a, 512 * q:512 * q + 512]
                        last = STT(x, x, ALPHA, ps[:, 4 * a + q, :], ALU.mult, ALU.add)
                    link(last)
                for a in range(TT_):
                    for q in range(4):
                        last = dve.bn_stats(stats[:, q, :], xres[:, a, 512 * q:512 * q + 512])
                    link(last)
                    dve.bn_aggr(mv[:, :], stats[:, :, :]).then_inc(s_ln, 1)
                    dve.wait_ge(s_std, 2 * n + a + 1)
                    link(dve.reciprocal(rstd[:, :], rstd[:, :]))
                    x = xres[:, a, :]
                    link(TS(x, x, mv[:, 0:1], rstd[:, 0:1], ALU.subtract, ALU.mult))
                    link(TTn(x, x, gain[:, :], ALU.mult))
                    TTn(x, x, bias[:, :], ALU.add).then_inc(s_lnd, 1)

            dve.wait_ge(s_used, G_FF1)
            dve.wait_ge(s_xres, 16)
            dve.wait_ge(s_ln1c, 32)
            layer_norm(0, gain1, bias1)
            for n in range(8):
                dve.wait_ge(s_x1h, n + 1)
                a, j = n // 4, n % 4
                TTn(actlo[:, 4 * j:4 * j + 4, tok(a)], ps[:, n, :].rearrange("p (k q) -> p k q", k=4),
                    f(acthi[:, 4 * j:4 * j + 4, tok(a)]), ALU.subtract).then_inc(s_x1l, 1)
            with dve.Fori(0, N_FF1 // 2) as i:
                for k in range(2):
                    k0 = G_FF1 + 2 * k
                    lo(i * 4 + (k0 + 1), k0 + 1)
                    lo(i * 4 + (k0 + 2), k0 + 2)
                    dve.wait_ge(s_relu, i * 2 + (k + 1))
                    h2 = hid[:, bass.ds(i * 4 + 2 * k, 2), :]
                    TTn(h2, ps[:, 2 * k:2 * k + 2, 0:S], h2, ALU.mult).then_inc(s_ff, 1)
            NF = DFF // P
            split(hid[:, 0, :], KT, 0, None)
            with dve.Fori(0, NF // 4 - 1) as i:
                for k in range(4):
                    lo(i * 4 + (G_FF2 + k + 1), G_FF2 + k + 1)
                    split(hid[:, bass.ds(i * 4 + (k + 1), 1), :].squeeze(1), i * 4 + (KT + k + 1), (k + 1) % 2,
                          i * 4 + (G_FF2 + k))
            for k in range(NF - 4, NF - 1):
                lo(G_FF2 + k + 1, G_FF2 + k + 1)
                split(hid[:, k + 1, :], KT + k + 1, (k + 1) % 2, G_FF2 + k)
            dve.wait_ge(s_used, G_END)
            dve.wait_ge(s_ln2c, 32)
            layer_norm(1, gain2, bias2)

        @block.gpsimd
        def _(pool):
            PT = pool.tensor_tensor
            with pool.Fori(0, NB) as b:
                def at_b(x):
                    return x[:, bass.ds(b, 1), :].squeeze(1)

                kk, bb, kb_, e = at_b(krv), at_b(bt), at_b(ki), at_b(e2)
                kt = kr[:, bass.ds(b, 1), :, 0, :].squeeze(1)
                pool.wait_ge(s_kk, b * 2 + 1)
                PT(kt, kt, kk.rearrange("p (a q) -> p a q", a=TT_), ALU.mult).then_inc(s_pl, 1)
                PT(bb, bb, kk, ALU.mult).then_inc(s_pl, 1)
                pool.wait_ge(s_pl, b * 4 + 2)
                PT(bb, bb, e, ALU.mult).then_inc(s_pl, 1)
                PT(kb_, kb_, e, ALU.mult).then_inc(s_pl, 1)
            for q in range(8):
                u = slice(4 * (q % 4), 4 * (q % 4) + 4)
                n = STEPS.index((q // 4, 0, q % 4))
                pool.wait_ge(s_xm, n + 1)
                PT(TM[:, u, :], TM[:, u, :], over(ID, 4), ALU.add)
                tt = TTh[q // 4][:, u, :]
                PT(tt, tt, over(ID, 4), ALU.add).then_inc(s_init, 1)
            for c in range(3):
                if c == 0:
                    pool.wait_ge(s_tr, 4)
                if c == 2:
                    pool.wait_ge(s_upd, updates(len(STEPS) - 1))
                PT(gm[c][:, :, :], over(BD, NB), gam[:, :, c:c + 1].broadcast_to([P, NB, P]), ALU.mult
                   ).then_inc(s_gm, 1)


OUT_SHAPE = (1, S, D)


def layout(inputs):
    a = {k: np.asarray(v) for k, v in inputs.items()}
    w_in = a["w_in"][0]

    def cut(w, c0, width, slabs):
        piece = w[:, c0:c0 + width].reshape(slabs, KT // slabs, P, width)
        return piece.transpose(0, 2, 1, 3).reshape(slabs, P, -1)

    slabs = [cut(w_in, 3 * RW, 256, 2), cut(w_in, RCOLS - P, P, 1)]
    for base in (RW, 0, 2 * RW):
        slabs += [cut(w_in, base + 256 * j, 256, 2) for j in range(RW // 256)]
    slabs += [cut(w_in, RCOLS + 256 * j, 256, 2) for j in range(2 * RW // 256)]
    slabs += [cut(w_in, RCOLS + 2 * RW + 512 * j, 512, 4) for j in range(2)]
    ff1 = np.concatenate([cut(a["w_ff1"][0], 256 * j, 256, 2) for j in range(N_FF1)])

    def blocks(v):
        return np.asarray(v).reshape(-1, P).T

    mu = a["mu_shift"][0]
    inv_freq = np.float32(10000.0) ** (-np.arange(0, HD, 2, dtype=np.float32) / np.float32(HD))
    vecs = np.concatenate([
        blocks(mu[RW:2 * RW]), blocks(mu[0:RW]), blocks(mu[2 * RW:3 * RW]),
        blocks(mu[3 * RW:3 * RW + 2 * P]), blocks(mu[RCOLS - P:RCOLS]),
        blocks(a["rwkv_k_k"][0]), blocks(a["rwkv_k_a"][0]), blocks(a["rwkv_r_k"][0].reshape(-1)),
        blocks(a["rwkv_a0"][0]), blocks(a["rwkv_gn_gain"][0]), blocks(a["rwkv_gn_bias"][0]),
        a["diff_subln_gain"][0].reshape(P, 1),
        np.tile(inv_freq, 4).reshape(P, 1).astype(np.float32),
        np.tile(np.repeat(np.array([-1.0, 1.0], np.float32), 32), 2).reshape(P, 1),
        np.full((P, 1), GN_EPS, np.float32), np.full((P, 1), SUB_EPS, np.float32),
        np.full((P, 1), LN_EPS, np.float32)], axis=1)
    g_up = a["rwkv_g_up"][0]
    gup = np.zeros((P, 2, RW), np.float32)
    gup[:, 0, :] = g_up[0:P]
    gup[P - (LORA_G - P):, 1, :] = g_up[P:LORA_G]
    x = a["x"][0]
    out = {
        "x": x, "xT": x.T.reshape(KT, P, S).transpose(1, 0, 2),
        "positions": a["positions"].astype(np.int32).reshape(1, S),
        "w_in": np.concatenate(slabs), "w_out": a["w_out"][0].reshape(KT, P, D), "w_ff1": ff1,
        "w_ff2": a["w_ff2"][0].reshape(DFF // P, P, D), "vecs": vecs, "consts": shape_constants(),
        "w_up": np.concatenate([a["rwkv_w_up"][0], a["rwkv_w0"]]), "a_up": a["rwkv_a_up"][0], "g_up": gup,
        "lam": np.concatenate([a["diff_lambda_q1"], a["diff_lambda_k1"], a["diff_lambda_q2"], a["diff_lambda_k2"]]),
        "ln1_gain": a["ln1_gain"], "ln1_bias": a["ln1_bias"], "ln2_gain": a["ln2_gain"], "ln2_bias": a["ln2_bias"],
    }
    return {k: np.ascontiguousarray(v) for k, v in out.items()}


def kernel(**inputs):
    import concourse.bacc as bacc
    from concourse.bass_utils import run_bass_kernel_spmd

    nc = bacc.Bacc("TRN2", target_bir_lowering=False, num_devices=1)
    arrays = layout(inputs)
    t = {n: nc.dram_tensor(n, a.shape, mybir.dt.from_np(a.dtype), kind="ExternalInput").ap()
         for n, a in arrays.items()}
    t["out"] = nc.dram_tensor("out", (S, D), F32, kind="ExternalOutput").ap()
    build(nc, t)
    r = run_bass_kernel_spmd(nc, [arrays], core_ids=[0])
    return r.results[0]["out"].reshape(OUT_SHAPE)
```

```python
import math
from contextlib import ExitStack

import numpy as np

import concourse.bass as bass
from concourse import mybir

ALU = mybir.AluOpType
ACT = mybir.ActivationFunctionType
F32 = mybir.dt.float32
F32R = mybir.dt.float32r
I32 = mybir.dt.int32
AX_X = mybir.AxisListType.X

P = 128
D = 2048
S = 256
TT_ = S // P
DFF = 4 * D
RW = D // 2
HD = 64
NB = RW // P
DH = 8
KT = D // P
C = 64
NC = S // C
LORA_W, LORA_A, LORA_G = 64, 64, 160
RCOLS = 3 * RW + LORA_W + LORA_A + LORA_G
ALPHA = 2.0 ** 0.25
LAMBDA_INIT = 0.8 - 0.6 * math.exp(-0.3 * 0)
LN_EPS, GN_EPS, SUB_EPS = 1e-5, 64e-5, 1e-5
DECAY = math.exp(-0.5)
NEG = -1e30
UNITS = 32

SLAB = 2048
G_LORA, N_LORA = 0, 3
G_MIX = G_LORA + N_LORA
N_QK = 8
N_MIX = 3 * RW // 256 + N_QK
PER = 5
G_VD = G_MIX + 2 * N_MIX
G_OUT = G_VD + 8
G_FF1 = G_OUT + KT
N_FF1 = DFF // 256
G_FF2 = G_FF1 + 2 * N_FF1
G_END = G_FF2 + DFF // P
NST, NHL = 4, 2

V_MU, V_KK, V_KA, V_RK, V_A0, V_GG, V_GB, V_SG, V_INVF, V_SIGN, V_GNEPS, V_SUBEPS, V_LNEPS = (
    0, 27, 35, 43, 51, 59, 67, 75, 76, 77, 78, 79, 80)
V_IN = 81
V_OMMU, V_OMKA, V_G08 = 81, 108, 116
V_ALL = 120

C_SU, C_IU, C_ID, C_BD = 0, P, 2 * P, 3 * P
C_SMALL = 4 * P
C_LEV, C_M1T = C_SMALL, C_SMALL + 6 * P
C_ATT = C_M1T + 128
C_SUMW = C_ATT + 384
C_SEL = C_SUMW + 48
C_ALL = C_SEL + 2 * NB * P


def shape_constants():
    p, q = np.arange(P)[:, None], np.arange(P)[None, :]
    same = p // C == q // C
    out = np.zeros((P, C_ALL), np.float32)
    out[:, C_SU:C_SU + P] = same & (p < q)
    out[:, C_IU:C_IU + P] = same & (p <= q)
    out[:, C_ID:C_ID + P] = p == q
    out[:, C_BD:C_BD + P] = same
    for n in range(6):
        m = 1 << n
        lev = (p // (2 * m) == q // (2 * m)) & (p // m % 2 == 1) & (q // m % 2 == 0)
        out[:, C_LEV + n * P:C_LEV + (n + 1) * P] = lev
        if n == 0:
            out[:, C_M1T:C_M1T + P] = lev.T
    causal = np.where(q > p, NEG, 0.0)
    out[:, C_ATT:C_ATT + P] = causal
    out[:, C_ATT + 2 * P:C_ATT + 3 * P] = causal
    out[:C, C_SUMW + 14] = 1.0
    out[C:, C_SUMW + 15] = 1.0
    out[:, C_SUMW + 30 + 7] = 1.0
    for b in range(NB):
        at = C_SEL + b * P
        out[2 * b, at:at + C] = 1.0
        out[2 * b + 1, at + C:at + P] = 1.0
        out[b, at + NB * P:at + NB * P + P] = 1.0
    return out


def build(nc, t):
    ctx = ExitStack()
    with ctx:
        BASE, SL_BYTES = 16512, 8192
        SMALL = BASE + 25 * SL_BYTES

        def at(name, slot, shape, dtype=F32, byte=0):
            return nc.alloc_sbuf_tensor_at(name, shape, dtype, offset=BASE + slot * SL_BYTES + byte)

        def small(name, col, shape, dtype=F32):
            return nc.alloc_sbuf_tensor_at(name, shape, dtype, offset=SMALL + 4 * col)

        def sem(name):
            return ctx.enter_context(nc.semaphore(name))

        stage = [at(f"stage{i}", i, [P, SLAB]) for i in range(NST)]
        whi = [at(f"whi{i}", 4 + i, [P, SLAB], F32R) for i in range(NHL)]
        wlo = [at(f"wlo{i}", 6 + i, [P, SLAB], F32R) for i in range(NHL)]
        acthi = at("acthi", 8, [P, KT, S], F32R)
        actlo = at("actlo", 10, [P, KT, S], F32R)
        wup = at("wup", 12, [65, RW])
        aup = at("aup", 12, [P, RW], byte=4096)
        sig = at("sig", 13, [P, TT_, RW])
        kr = at("kr", 14, [P, NB, TT_, 2, P])
        e2 = at("e2", 16, [P, NB, S])
        bt = at("bt", 17, [P, NB, S])
        krv = at("krv", 18, [P, 3 * NB, S])
        ki = at("ki", 21, [P, NB, S])
        qk = at("qk", 22, [P, 2 * DH, S])
        xstage = at("xstage", 22, [P, KT, S])
        vd = at("vd", 24, [P, TT_, RW])
        cosb = at("cosb", 24, [P, S])
        sinb = at("sinb", 24, [P, S], byte=1024)
        angt = [at(f"angt{i}", 24, [P, S], byte=2048 + 1024 * i) for i in range(3)]
        posi = at("posi", 24, [P, S], I32, byte=5120)
        rot = at("rot", 12, [P, 2, S])
        sqt = at("sqt", 13, [P, 2, S])
        inv = at("inv", 13, [P, 2, S], byte=2048)
        rkt_ = at("rkt_", 13, [P, 2, S], byte=4096)
        yt = at("yt", 12, [P, KT, S])
        amask = at("amask", 0, [P, 3 * P])
        sm = at("sm", 0, [P, 2, 3 * P], byte=2048)
        pr = at("pr", 0, [P, 2, 3 * P], byte=5120)
        att = at("att", 1, [P, 3 * P])
        attT = at("attT", 1, [P, 3 * P], byte=1536)
        lamv = at("lamv", 1, [P, 4, HD], byte=3072)
        lamt = at("lamt", 1, [P, 2, HD], byte=4096)
        osq = at("osq", 2, [P, DH, S])
        oinv = at("oinv", 1, [DH, S], byte=4608)
        levc = at("levc", 3, [P, 7, P])
        sumw = at("sumw", 3, [P, 48], byte=3584)
        sel8 = at("sel8", 3, [DH, DH, P], byte=4096)
        AT = at("AT", 8, [P, 16, P])
        TM = at("TM", 9, [P, 16, P])
        XM = at("XM", 10, [P, 16, P])
        TTh = [at("TTh0", 18, [P, 16, P]), at("TTh1", 16, [P, 16, P])]
        kbt = [at(f"kbt{i}", 8, [P, 8, P], byte=4096 * i) for i in range(2)]
        vtm = at("vtm", 9, [P, NB, TT_, P])
        btm = at("btm", 10, [P, NB, TT_, P])
        ktm = at("ktm", 24, [P, NB, TT_, P])
        z1 = at("z1", 22, [P, NB, TT_, P])
        um = at("um", 23, [P, NB, TT_, P])
        st = [None, at("st1", 8, [P, NB, P]), at("st2", 8, [P, NB, P], byte=4096), at("st3", 11, [P, NB, P])]
        gm = [at("gm0", 20, [P, NB, P]), at("gm1", 20, [P, NB, P], byte=4096), at("gm2", 11, [P, NB, P], byte=4096)]
        rbt = at("rbt", 4, [P, UNITS, P])
        rkt = at("rkt", 6, [P, UNITS, P])
        sel16 = at("sel16", 21, [2 * NB, NB, P])
        ginv = at("ginv", 21, [2 * NB, S], byte=4096)
        sumg = at("sumg", 21, [P, 32], byte=5120)
        yf = at("yf", 20, [P, NB, S])
        gup = at("gup", 10, [P, 2, RW])
        gsq = at("gsq", 24, [P, NB, S])
        xres = at("xres", 22, [P, TT_, D])
        gain1 = at("gain1", 14, [P, D])
        bias1 = at("bias1", 15, [P, D])
        hid = at("hid", 14, [P, DFF // P, S])
        gain2 = at("gain2", 12, [P, D])
        bias2 = at("bias2", 13, [P, D])
        cst = small("cst", 0, [P, C_SMALL])
        vec = small("vec", 768, [P, V_ALL])
        wt = small("wt", 888, [65, S])
        wa = small("wa", 888 + 256, [P, S])
        sg = [small(f"sg{i}", 888 + 512 + 256 * i, [P, S]) for i in range(2)]
        shi = [small(f"shi{i}", 888 + 256 * i, [P, S], F32R) for i in range(2)]
        slo = [small(f"slo{i}", 888 + 512 + 256 * i, [P, S], F32R) for i in range(2)]
        gam = small("gam", 1912, [P, NB, NC])
        mx = small("mx", 1944, [P, 2, 4])
        nmx = small("nmx", 1952, [P, 2, 4])
        sums = small("sums", 1960, [P, 2, 4])
        coef = small("coef", 1968, [P, 2, 4])
        lam = small("lam", 1976, [P, 4])
        stats = [small("stats0", 1984, [P, 4, 6]), small("stats1", 1944, [P, 4, 6])]
        moments = [small("moments0", 2008, [P, 4]), small("moments1", 1968, [P, 4])]

        ps = ctx.enter_context(nc.psum_tensor("ps", [P, 8, 512], F32))

        s_stage = [sem(f"stage_loaded{i}") for i in range(NST)]
        s_hi, s_lo, s_used = sem("hi_ready"), sem("lo_ready"), sem("slab_used")
        s_free, s_mix = sem("acc_free"), sem("mix_scaled")
        s_x = [sem(f"x_loaded{i}") for i in range(4)]
        s_xhi, s_xlo = sem("act_hi_ready"), sem("act_lo_ready")
        s_cst, s_pos, s_attc, s_levc, s_gup = (
            sem("consts_loaded"), sem("positions_loaded"), sem("attention_consts_loaded"),
            sem("level_masks_loaded"), sem("gate_up_loaded"))
        s_ln1c, s_ln2c, s_xres, s_out = (
            sem("ln1_vectors_loaded"), sem("ln2_vectors_loaded"), sem("x_reloaded"), sem("output_stored"))
        s_vecl = sem("vectors_loaded")
        s_vec, s_lup = sem("vectors_ready"), sem("lora_weights_loaded")
        s_lora, s_z, s_sig = sem("lora_activated"), sem("decay_logits"), sem("decay_sigmoid")
        s_item, s_itemd, s_gam = sem("rate_or_cumsum"), sem("rate_or_cumsum_done"), sem("chunk_decay_kept")
        s_ang, s_sin, s_tab = sem("angle_step"), sem("sines_ready"), sem("rotary_tables_ready")
        s_rotc, s_rotm, s_rotd = sem("rot_copied"), sem("rot_multiplied"), sem("rotary_done")
        s_sq, s_ss, s_nrm = sem("kk_squares"), sem("kk_sums"), sem("kk_norms")
        s_ew = sem("elementwise_step")
        s_rk, s_bon, s_kk, s_pl = sem("bonus_terms"), sem("bonus_sums"), sem("kk_ready"), sem("pool_step")
        s_bonv = sem("bonus_ready")
        s_vdc = sem("v_copied")
        s_lamd = sem("lambda_step")
        s_lame = sem("lambda_exps")
        s_sc, s_smd, s_exp, s_at, s_atc, s_o, s_oc = (
            sem("scores_ready"), sem("masked_scores_ready"), sem("probs_ready"), sem("attention_transposed"),
            sem("attention_T_copied"), sem("head_out"), sem("head_out_copied"))
        s_attn, s_attd = sem("attention_ready"), sem("attention_step")
        s_osq, s_oss, s_ord, s_ydn = (
            sem("out_squares"), sem("out_sums"), sem("out_inverses"), sem("diff_out_ready"))
        s_init, s_px, s_xm, s_ptx, s_upd = (
            sem("first_level_ready"), sem("level_x"), sem("level_x_masked"), sem("level_products"),
            sem("level_done"))
        s_tr, s_trc = sem("transposed"), sem("transposed_copied")
        s_kb, s_kbm, s_z1p, s_z1 = sem("kb_products"), sem("kb_masked"), sem("z1_products"), sem("z1_ready")
        s_gm = sem("state_decay_masks")
        s_ks, s_zc, s_u, s_uc, s_sp, s_stm, s_st = (
            sem("state_term"), sem("z_ready"), sem("u_products"), sem("u_ready"), sem("state_products"),
            sem("state_sum"), sem("state_ready"))
        s_y, s_yc = sem("y_products"), sem("y_copied")
        s_sumg, s_sumw, s_sel8, s_sel16, s_oss_read, s_spr, s_ginv, s_bc = (
            sem("norm_windows_loaded"), sem("sum_windows_loaded"), sem("head_rows_loaded"), sem("norm_rows_loaded"), sem("out_sums_read"),
            sem("heads_spread"), sem("gn_inverses"), sem("gn_spread"))
        s_mean, s_cen, s_gsq, s_var, s_sd, s_gn, s_gate, s_yg = (
            sem("gn_means"), sem("gn_centred"), sem("gn_squares"), sem("gn_vars"), sem("gn_roots"),
            sem("gn_step"), sem("gate_ready"), sem("rwkv_out_ready"))
        s_ahi, s_alo = sem("moving_hi_ready"), sem("moving_lo_ready")
        s_row, s_ln, s_std, s_rs, s_nrmq, s_gq, s_lnd, s_lnp, s_lnk = (
            sem("row_sums_ready"), sem("ln_moments"), sem("ln_roots"), sem("ln_scales"), sem("ln_normalised"),
            sem("ln_gained"), sem("ln_done_vector"), sem("ln_done_pool"), sem("ln_chain"))
        s_pg = sem("ln_gained_pool")
        s_xt, s_x1h, s_x1l = sem("x1_transposed"), sem("x1_hi"), sem("x1_lo")
        s_relu, s_ff = sem("relu_ready"), sem("hidden_ready")

        block = ctx.enter_context(nc.Block())

        def col(v, n=0):
            return vec[:, v + n:v + n + 1]

        def vcol(v, blk):
            return vec[:, bass.ds(blk + v, 1)]

        def over(ap, n):
            return ap.unsqueeze(1).broadcast_to([ap.shape[0], n, ap.shape[1]])

        def f(ap):
            return ap.bitcast(F32)

        SU, IU, ID = cst[:, C_SU:C_SU + P], cst[:, C_IU:C_IU + P], cst[:, C_ID:C_ID + P]
        BD = cst[:, C_BD:C_BD + P]
        M1, M1T = levc[:, 0, :], levc[:, 6, :]

        def banks(a, n=2, lo=0, hi=512):
            return ps[:, a:a + n, lo:hi]

        def units(g):
            return [(hp * 4 + b2 * 2 + a, hp, 2 * g + b2, a) for hp in range(2) for b2 in range(2) for a in range(TT_)]

        def quad(s):
            return [(4 * s + j, P * j, s % 2, 2 * (s // 2) + j // 2, j % 2) for j in range(4)]

        def TTm(u):
            return TTh[u // 16][:, u % 16, :]

        def unit(b, hp, a):
            return (b // 2) * 8 + hp * 4 + (b % 2) * 2 + a

        READ = 6
        STEPS = [(half, lev, s) for half in range(2) for lv in range(6)
                 for lev, s in [(lv, q) for q in range(4)] + ([(READ, lv - 1)] if 1 <= lv <= 4 else [])]
        PER_HEAD = len(STEPS) // DH

        def setups(n):
            return sum(lev == 0 for _, lev, _ in STEPS[:n + 1])

        def updates(n):
            return sum(lev not in (0, READ) for _, lev, _ in STEPS[:n + 1])

        def ln_done(eng, n, a, q):
            eng.wait_ge((s_lnp, s_lnd)[a], 4 * n + q + 1)

        def hr(hp):
            return slice(HD * hp, HD * hp + HD)

        def tok(a):
            return slice(P * a, P * a + P)

        @block.sync
        def _(sp):
            def slab(n, k, src):
                if not (isinstance(n, int) and n < NST):
                    sp.wait_ge(s_lo, n - (NST - 1))
                sp.dma_start(stage[k % NST][:, :], src).then_inc(s_stage[k % NST], 16)

            def slabs(base, first, last, src):
                with sp.Fori(first, last) as i:
                    for k in range(4):
                        slab(i * 4 + (base + k), base + k, src[bass.ds(i * 4 + k, 1), :, :])

            def x_piece(j):
                sp.dma_start(xstage[:, 4 * j:4 * j + 4, :], t["xT"][:, 4 * j:4 * j + 4, :]).then_inc(s_x[j], 16)

            x_piece(0)
            slab(0, 0, t["w_in"][0])
            for j in range(1, 4):
                x_piece(j)
            slab(1, 1, t["w_in"][1])
            sp.dma_start(vec[:, 0:V_IN], t["vecs"]).then_inc(s_vecl, 16)
            slab(2, 2, t["w_in"][2])
            sp.dma_start(wup[:, :], t["w_up"]).then_inc(s_lup, 16)
            sp.dma_start(aup[64:128, :], t["a_up"]).then_inc(s_lup, 16)
            sp.dma_start(cst[:, :], t["consts"][:, 0:C_SMALL]).then_inc(s_cst, 16)
            slab(3, 3, t["w_in"][3])
            sp.dma_start(posi[:, :], t["positions"].partition_broadcast(P)).then_inc(s_pos, 16)
            slabs(4, 0, (G_OUT - 4) // 4, t["w_in"][4:, :, :])
            for g in range(G_OUT // 4 * 4, G_OUT):
                slab(g, g, t["w_in"][g])
            sp.wait_ge(s_lo, G_OUT)
            sp.dma_start(amask[:, :], t["consts"][:, C_ATT:C_ATT + 3 * P]).then_inc(s_attc, 16)
            for j in range(4):
                sp.dma_start(lamv[:, j, :], t["lam"][j:j + 1, :].partition_broadcast(P)).then_inc(s_attc, 16)
            sp.dma_start(levc[:, :, :], t["consts"][:, C_LEV:C_LEV + 7 * P].rearrange("p (l q) -> p l q", l=7)
                         ).then_inc(s_levc, 16)
            sp.dma_start(sel8[:, :, :], t["consts"][0:DH, C_SEL + NB * P:C_SEL + 2 * NB * P]
                         .rearrange("p (h q) -> p h q", q=P)).then_inc(s_sel8, 16)
            sp.dma_start(sumw[:, :], t["consts"][:, C_SUMW:C_SUMW + 48]).then_inc(s_sumw, 16)
            sp.wait_ge(s_kb, 4)
            sp.dma_start(sel16[:, :, :], t["consts"][0:2 * NB, C_SEL:C_SEL + NB * P]
                         .rearrange("p (h q) -> p h q", q=P)).then_inc(s_sel16, 16)
            sp.dma_start(sumg[:, :], t["consts"][:, C_SUMW:C_SUMW + 32]).then_inc(s_sumg, 16)
            sp.wait_ge(s_sp, 2 * (NC - 1))
            sp.dma_start(gup[:, :, :], t["g_up"]).then_inc(s_gup, 16)
            sp.wait_ge(s_ydn, 4)
            for g in range(G_OUT, G_OUT + 4):
                slab(g, g, t["w_out"][g - G_OUT])
            sp.wait_ge(s_y, 4)
            sp.dma_start(xres[:, :, :], t["x"].rearrange("(a p) d -> p a d", p=P)).then_inc(s_xres, 16)
            sp.dma_start(gain1[:, :], t["ln1_gain"].partition_broadcast(P)).then_inc(s_ln1c, 16)
            sp.dma_start(bias1[:, :], t["ln1_bias"].partition_broadcast(P)).then_inc(s_ln1c, 16)
            slabs(G_OUT + 4, 0, KT // 4 - 1, t["w_out"][4:, :, :])
            slabs(G_FF1, 0, N_FF1 // 2, t["w_ff1"])
            sp.dma_start(gain2[:, :], t["ln2_gain"].partition_broadcast(P)).then_inc(s_ln2c, 16)
            sp.dma_start(bias2[:, :], t["ln2_bias"].partition_broadcast(P)).then_inc(s_ln2c, 16)
            slabs(G_FF2, 0, DFF // P // 4, t["w_ff2"])
            for a in range(TT_):
                for q in range(4):
                    ln_done(sp, 1, a, q)
                    cols = slice(512 * q, 512 * q + 512)
                    sp.dma_start(t["out"][tok(a), cols], xres[:, a, cols]).then_inc(s_out, 16)
            sp.wait_ge(s_out, 16 * 4 * TT_)

        @block.tensor
        def _(pe):
            def mm(out, lhsT, rhs, start=True, stop=True):
                return pe.matmul(out, lhsT, rhs, start=start, stop=stop, skip_group_check=True)

            def halves_ready(g):
                pe.wait_ge(s_hi, g + 1)
                pe.wait_ge(s_lo, g + 1)

            def chunk(b0, g, k0, width=256, slabs=2, ready=None):
                kts = SLAB // width
                for s in range(slabs):
                    w = (k0 + s) % NHL
                    halves_ready(g + s)
                    for j in range(kts):
                        k = s * kts + j
                        if ready and k % 4 == 0:
                            pe.wait_ge(ready[0], ready[1] + k // 4)
                        for fb in range(width // P):
                            acc = ps[:, b0 + fb, 0:S]
                            cols = slice(j * width + fb * P, j * width + fb * P + P)
                            mm(acc, whi[w][:, cols], acthi[:, k, :], start=(k == 0), stop=False)
                            mm(acc, whi[w][:, cols], actlo[:, k, :], start=False, stop=False)
                            last = mm(acc, wlo[w][:, cols], acthi[:, k, :], start=False, stop=(k == KT - 1))
                    last.then_inc(s_used, 1)

            def rows(g, k0, n, first, last_, each=False):
                w, h = k0 % NHL, n % 2
                halves_ready(g)
                outs = [(a, q) for a in range(TT_) for q in range(4)]
                if isinstance(g, int) and g == G_OUT:
                    outs = [(a, q) for q in range(4) for a in range(TT_)]
                for a, q in outs:
                    if isinstance(g, int) and g == G_OUT:
                        pe.wait_ge(s_yg, q + 1)
                    acc = ps[:, 4 * a + q, :]
                    cols = slice(512 * q, 512 * q + 512)
                    mm(acc, shi[h][:, tok(a)], whi[w][:, cols], start=first, stop=False)
                    mm(acc, slo[h][:, tok(a)], whi[w][:, cols], start=False, stop=False)
                    last = mm(acc, shi[h][:, tok(a)], wlo[w][:, cols], start=False, stop=last_)
                    if each and (a, q) != (TT_ - 1, 3):
                        last.then_inc(s_row, 1)
                last.then_inc(s_used, 1)

            chunk(0, 0, 0, ready=(s_xlo, 1))
            chunk(2, 2, 2, width=128, slabs=1)
            pe.wait_ge(s_cst, 16)
            pe.wait_ge(s_lup, 32)
            pe.wait_ge(s_lora, 1)
            pe.wait_ge(s_vec, 1)
            for a in range(TT_):
                for q in range(2):
                    mm(ps[:, 4 + 2 * a + q, :], wt[:, tok(a)], wup[:, 512 * q:512 * q + 512]).then_inc(s_z, 1)
            for n in range(2 * NB):
                b, bk = n % NB, 4 + n % 4
                if n < 4:
                    pe.wait_ge(s_sig, n + 1)
                else:
                    pe.wait_ge(s_itemd, n - 3)
                if n < NB:
                    mm(ps[:, bk, 0:S], aup[64:128, P * b:P * b + P], wa[64:128, :]).then_inc(s_item, 1)
                else:
                    for a in range(TT_):
                        last = mm(ps[:, bk, 256 * a:256 * a + 256], sig[:, a, P * b:P * b + P],
                                  cst[:, C_SU:C_SU + 2 * P])
                    last.then_inc(s_item, 1)
            with pe.Fori(0, NB // 4) as i:
                for jj in range(2):
                    for c in range(PER):
                        m, k0 = PER * jj + c, G_MIX + 2 * (PER * jj + c)
                        pe.wait_ge(s_free, i * (2 * PER) + (m + 1))
                        chunk(2 * (m % 2), i * (4 * PER) + k0, k0)
                        if c == 1:
                            pe.wait_ge(s_sq, i * 2 + (jj + 1))
                            mm(ps[:, 4 + jj, :], BD, sqt[:, :, :]).then_inc(s_ss, 1)
                        if c == 2:
                            pe.wait_ge(s_rk, i * 2 + (jj + 1))
                            mm(ps[:, 6 + jj, :], BD, rkt_[:, :, :]).then_inc(s_bon, 1)
            for m in range(2):
                pe.wait_ge(s_free, 2 + N_MIX - 1 + m)
                for s in range(4):
                    g = G_VD + 4 * m + s
                    halves_ready(g)
                    w = g % NHL
                    for j in range(4):
                        k = 4 * s + j
                        for a in range(TT_):
                            acc = ps[:, 2 * m + a, :]
                            cols = slice(512 * j, 512 * j + 512)
                            mm(acc, acthi[:, k, tok(a)], whi[w][:, cols], start=(k == 0), stop=False)
                            mm(acc, actlo[:, k, tok(a)], whi[w][:, cols], start=False, stop=False)
                            last = mm(acc, acthi[:, k, tok(a)], wlo[w][:, cols], start=False, stop=(k == KT - 1))
                    last.then_inc(s_used, 1)

            def attention(h, part):
                if part == 0:
                    if h:
                        pe.wait_ge(s_osq, h)
                    for c in range(2):
                        for a in range(TT_):
                            o = (0, P)[a]
                            last = mm(ps[:, 6 + c, o:o + P * (a + 1)], qk[hr(c), h, tok(a)],
                                      qk[hr(c), DH + h, 0:P * (a + 1)])
                    last.then_inc(s_sc, 1)
                elif part == 4:
                    pe.wait_ge(s_attn, h + 1)
                    for j in range(3):
                        last = pe.transpose(ps[:, 6, P * j:P * j + P], att[:, P * j:P * j + P], ID)
                    last.then_inc(s_at, 1)
                elif part == 5:
                    pe.wait_ge(s_atc, h + 1)
                    mm(ps[:, 7, 0:S], vd[:, 0, P * h:P * h + P], attT[:, 0:S], stop=False)
                    mm(ps[:, 7, P:S], vd[:, 1, P * h:P * h + P], attT[:, S:3 * P], start=False).then_inc(s_o, 1)

            def level_x(n):
                half, lev, s = STEPS[n]
                bk = 2 * (n % 3)
                if n >= 3:
                    if STEPS[n - 3][1] not in (0, READ):
                        pe.wait_ge(s_upd, updates(n - 3))
                    else:
                        pe.wait_ge(s_xm, n - 2)
                if lev == 0:
                    for u, o, hp, b, a in quad(4 * half + s):
                        mm(ps[:, bk, o:o + P], kr[hr(hp), b, a, 0, :], bt[hr(hp), b, tok(a)])
                        last = mm(ps[:, bk + 1, o:o + P], bt[hr(hp), b, tok(a)], kr[hr(hp), b, a, 0, :])
                elif lev == READ:
                    for u, o, hp, b, a in quad(4 * half + s):
                        mm(ps[:, bk, o:o + P], bt[hr(hp), b, tok(a)], kr[hr(hp), b, a, 1, :])
                        last = mm(ps[:, bk + 1, o:o + P], ki[hr(hp), b, tok(a)], kr[hr(hp), b, a, 1, :])
                else:
                    if lev == 1:
                        pe.wait_ge(s_init, 4 * half + s + 1)
                    for u, o, hp, b, a in quad(4 * half + s):
                        last = mm(ps[:, bk, o:o + P], AT[:, u % 16, :], TM[:, u % 16, :])
                last.then_inc(s_px, 1)

            def level_t(n):
                half, lev, s = STEPS[n]
                bk = 2 * (n % 3)
                if lev in (0, READ):
                    return
                pe.wait_ge(s_xm, n + 1)
                for u, o, hp, b, a in quad(4 * half + s):
                    if lev < 5:
                        mm(ps[:, bk, o:o + P], TTm(u), XM[:, u % 16, :])
                    last = mm(ps[:, bk + 1, o:o + P], XM[:, u % 16, :], TTm(u))
                last.then_inc(s_ptx, 1)

            def head_sums():
                pe.wait_ge(s_osq, DH)
                pe.wait_ge(s_sumw, 16)
                for h in range(DH):
                    last = mm(ps[0:DH, 6, 0:S], sumw[:, 37 - h:45 - h], osq[:, h, :], start=(h == 0), stop=(h == DH - 1))
                last.then_inc(s_oss, 1)

            def head_spread(p):
                if p == 0:
                    pe.wait_ge(s_sel8, 16)
                    pe.wait_ge(s_ord, 1)
                if p >= 2:
                    pe.wait_ge(s_ydn, p - 1)
                for j in range(2):
                    last = mm(ps[:, 6 + p % 2, S * j:S * j + S], sel8[:, 2 * p + j, :], oinv[:, :])
                last.then_inc(s_spr, 1)

            pe.wait_ge(s_rotd, N_QK)
            pe.wait_ge(s_vdc, 4)
            pe.wait_ge(s_pl, 4 * NB // 2)
            level_x(0)
            for n in range(len(STEPS)):
                if n + 1 < len(STEPS):
                    level_x(n + 1)
                level_t(n)
                attention(n // PER_HEAD, n % PER_HEAD)
            head_sums()
            pe.wait_ge(s_upd, updates(len(STEPS) - 1))
            for n in range(12):
                src = [lambda b: krv[:, 2 * NB + b, :], lambda b: bt[:, b, :], lambda b: ki[:, b, :]][n // 4]
                if n >= 6:
                    pe.wait_ge(s_trc, n - 5)
                for b2 in range(2):
                    for a in range(TT_):
                        o = P * (2 * b2 + a)
                        last = pe.transpose(ps[:, n % 6, o:o + P], src(2 * (n % 4) + b2)[:, tok(a)], ID)
                last.then_inc(s_tr, 1)
            def kb(g):
                if g >= 2:
                    pe.wait_ge(s_kbm, g - 1)
                for ul, hp, b, a in units(g):
                    o = P * (ul % 4)
                    last = mm(ps[:, 4 * (g % 2) + hp, o:o + P], ki[hr(hp), b, tok(a)], kr[hr(hp), b, a, 0, :])
                last.then_inc(s_kb, 1)

            pe.wait_ge(s_trc, 12)
            pe.wait_ge(s_oss_read, 1)
            kb(0)
            for g in range(4):
                if g + 1 < 4:
                    kb(g + 1)
                pe.wait_ge(s_kbm, g + 1)
                if g >= 2:
                    pe.wait_ge(s_z1, g - 1)
                for ul, hp, b, a in units(g):
                    o = P * (2 * (b % 2) + a) + HD * hp
                    last = mm(ps[:, 4 * (g % 2) + 2, o:o + HD], kbt[g % 2][:, ul, :], vtm[:, b, a, hr(hp)])
                last.then_inc(s_z1p, 1)
            pe.wait_ge(s_z1, 4)
            for c in range(NC):
                a, cb = c // 2, C * (c % 2)
                rw = slice(cb, cb + C)
                if c:
                    for G in range(2):
                        pe.wait_ge(s_st, 2 * (c - 1) + G + 1)
                        for j in range(4):
                            b = 4 * G + j
                            last = mm(ps[rw, 3 * G, P * j:P * j + P], kr[:, b, a, 0, rw], st[c][:, b, :])
                        last.then_inc(s_ks, 1)
                for G in range(2):
                    if c:
                        pe.wait_ge(s_zc, 2 * (c - 1) + G + 1)
                    if c:
                        pe.wait_ge(s_uc, 2 * (c - 1) + G + 1)
                    for j in range(4):
                        b = 4 * G + j
                        for hp in range(2):
                            last = mm(ps[rw, 3 * G + 1, P * j + HD * hp:P * j + HD * hp + HD],
                                      TTm(unit(b, hp, a))[:, rw], z1[:, b, a, hr(hp)])
                    last.then_inc(s_u, 1)
                head_spread(c)
                if c == NC - 1:
                    break
                for G in range(2):
                    pe.wait_ge(s_uc, 2 * c + G + 1)
                    for j in range(4):
                        b = 4 * G + j
                        o = ps[:, 3 * G + 2, P * j:P * j + P]
                        mm(o, ktm[rw, b, a, :], vtm[rw, b, a, :], stop=False)
                        last = mm(o, btm[rw, b, a, :], um[rw, b, a, :], start=False)
                    last.then_inc(s_sp, 1)
            def read_out(g):
                if g >= 2:
                    pe.wait_ge(s_ydn, g + 1)
                for b2 in range(2):
                    b = 2 * g + b2
                    for a in range(TT_):
                        o = P * (2 * b2 + a)
                        for hp in range(2):
                            out = ps[hr(hp), 4 + g, o:o + P]
                            u = unit(b, hp, a)
                            mm(out, vtm[:, b, a, hr(hp)], rkt[:, u, :], stop=False)
                            last = mm(out, um[:, b, a, hr(hp)], rbt[:, u, :], start=False)
                        for cc in range(2):
                            c = 2 * a + cc
                            if c:
                                last = mm(ps[:, 4 + g, o + C * cc:o + C * cc + C], st[c][:, b, :],
                                          kr[:, b, a, 1, C * cc:C * cc + C], start=False)
                last.then_inc(s_y, 1)

            def mean(g):
                pe.wait_ge(s_yc, g + 1)
                mm(ps[:, g, :], BD, yf[:, 2 * g:2 * g + 2, :]).then_inc(s_mean, 1)

            def square_sums(g):
                if g == 0:
                    pe.wait_ge(s_sumg, 16)
                pe.wait_ge(s_gsq, g + 1)
                for b in (2 * g, 2 * g + 1):
                    last = mm(ps[0:2 * NB, 0, 0:S], sumg[:, 14 - 2 * b:30 - 2 * b], gsq[:, b, :],
                              start=(b == 0), stop=(b == NB - 1))
                if g == 3:
                    last.then_inc(s_var, 1)

            def spread(g):
                for j in range(2):
                    last = mm(ps[:, g, S * j:S * j + S], sel16[:, 2 * g + j, :], ginv[:, :])
                last.then_inc(s_bc, 1)

            def gate(g):
                for j in range(2):
                    b = 2 * g + j
                    for q in range(2):
                        last = mm(ps[:, 4 + g, S * j:S * j + S], gup[:, q, P * b:P * b + P], sg[q][:, :],
                                  start=(q == 0), stop=(q == 1))
                last.then_inc(s_gate, 1)

            pe.wait_ge(s_uc, 2 * NC)
            read_out(0)
            read_out(1)
            mean(0)
            read_out(2)
            mean(1)
            read_out(3)
            mean(2)
            square_sums(0)
            pe.wait_ge(s_gup, 16)
            gate(0)
            mean(3)
            square_sums(1)
            gate(1)
            square_sums(2)
            square_sums(3)
            gate(2)
            gate(3)
            pe.wait_ge(s_sel16, 16)
            pe.wait_ge(s_ginv, 1)
            for g in range(4):
                spread(g)

            for n in range(4):
                pe.wait_ge(s_ahi, n + 1)
                pe.wait_ge(s_alo, n + 1)
                rows(G_OUT + n, G_OUT + n, n, n == 0, False)
            with pe.Fori(1, KT // 4 - 1) as i:
                for k in range(4):
                    pe.wait_ge(s_ahi, i * 4 + (k + 1))
                    pe.wait_ge(s_alo, i * 4 + (k + 1))
                    rows(i * 4 + (G_OUT + k), G_OUT + k, k, False, False)
            for n in range(KT - 4, KT):
                pe.wait_ge(s_ahi, n + 1)
                pe.wait_ge(s_alo, n + 1)
                rows(G_OUT + n, G_OUT + n, n, False, n == KT - 1, each=(n == KT - 1))
            for n in range(8):
                a, j = n // 4, n % 4
                ln_done(pe, 0, a, j)
                for q in range(4):
                    k = 4 * j + q
                    last = pe.transpose(ps[:, n, P * q:P * q + P], xres[:, a, P * k:P * k + P], ID)
                last.then_inc(s_xt, 1)
            pe.wait_ge(s_x1h, 4)
            chunk(0, G_FF1, G_FF1, ready=(s_x1l, 5))
            chunk(2, G_FF1 + 2, G_FF1 + 2)
            with pe.Fori(1, N_FF1 // 2) as i:
                for k in range(2):
                    pe.wait_ge(s_ff, i * 2 + (k - 1))
                    chunk(2 * k, i * 4 + (G_FF1 + 2 * k), G_FF1 + 2 * k)
            pe.wait_ge(s_ff, N_FF1)
            NF = DFF // P
            for n in range(4):
                pe.wait_ge(s_ahi, KT + n + 1)
                pe.wait_ge(s_alo, KT + n + 1)
                rows(G_FF2 + n, G_FF2 + n, n, n == 0, False)
            with pe.Fori(1, NF // 4 - 1) as i:
                for k in range(4):
                    pe.wait_ge(s_ahi, i * 4 + (KT + k + 1))
                    pe.wait_ge(s_alo, i * 4 + (KT + k + 1))
                    rows(i * 4 + (G_FF2 + k), G_FF2 + k, k, False, False)
            for n in range(NF - 4, NF):
                pe.wait_ge(s_ahi, KT + n + 1)
                pe.wait_ge(s_alo, KT + n + 1)
                rows(G_FF2 + n, G_FF2 + n, n, False, n == NF - 1, each=(n == NF - 1))

        @block.scalar
        def _(act):
            def A(out, in_, func, **kw):
                return act.activation(out, in_, func, **kw)

            def hi(g, k0):
                act.wait_ge(s_stage[k0 % NST], (g - k0) * 4 + 16 * (k0 // NST + 1))
                if not (isinstance(g, int) and g < 2):
                    act.wait_ge(s_used, g - 1)
                A(whi[k0 % NHL][:, :], stage[k0 % NST][:, :], ACT.Copy).then_inc(s_hi, 1)

            def split(src, g, n, h):
                act.wait_ge(s_used, g - 1)
                A(shi[h][:, :], src, ACT.Copy).then_inc(s_ahi, 1)

            def x_hi(j):
                act.wait_ge(s_x[j], 16)
                A(acthi[:, 4 * j:4 * j + 4, :], xstage[:, 4 * j:4 * j + 4, :], ACT.Copy).then_inc(s_xhi, 1)

            x_hi(0)
            hi(0, 0)
            for j in range(1, 4):
                x_hi(j)
            hi(1, 1)
            hi(2, 2)
            act.wait_ge(s_vec, 1)
            act.wait_ge(s_used, 2)
            A(wa[:, :], ps[:, 0, 0:S], ACT.Copy, scale=col(V_OMMU, 24))
            A(sg[0][:, :], ps[:, 1, 0:S], ACT.Copy, scale=col(V_OMMU, 25)).then_inc(s_mix, 1)
            hi(3, 3)
            act.wait_ge(s_free, 1)
            A(wt[0:64, :], wa[0:64, :], ACT.Tanh).then_inc(s_lora, 1)
            act.wait_ge(s_used, 3)
            A(sg[1][:, :], ps[:, 2, 0:S], ACT.Copy, scale=col(V_OMMU, 26)).then_inc(s_mix, 1)
            A(sg[0][:, :], sg[0][:, :], ACT.Sigmoid).then_inc(s_lora, 1)
            act.wait_ge(s_free, 2)
            A(sg[1][:, :], sg[1][:, :], ACT.Sigmoid).then_inc(s_lora, 1)
            for n in range(4):
                act.wait_ge(s_z, n + 1)
                A(sig[:, n // 2, 512 * (n % 2):512 * (n % 2) + 512], ps[:, 4 + n, :], ACT.Sigmoid).then_inc(s_sig, 1)
            for n in range(2 * NB):
                b, bk = n % NB, 4 + n % 4
                act.wait_ge(s_item, n + 1)
                if n < NB:
                    A(bt[:, b, :], ps[:, bk, 0:S], ACT.Sigmoid, bias=col(V_A0, b)).then_inc(s_itemd, 1)
                else:
                    A(kr[:, b, :, :, :].rearrange("p a e q -> p (a e q)"), ps[:, bk, :], ACT.Exp, scale=-DECAY)
                    A(e2[:, b, :].rearrange("p (a q) -> p a q", a=TT_),
                      ps[:, bk, :].rearrange("p (a e q) -> p a e q", a=TT_, e=2)[:, :, 1, :],
                      ACT.Exp, scale=DECAY).then_inc(s_itemd, 1)
            act.wait_ge(s_ang, 9)
            A(sinb[:, :], angt[0][:, :], ACT.Sin).then_inc(s_sin, 1)
            A(cosb[:, :], angt[2][:, :], ACT.Sin).then_inc(s_sin, 1)
            hi(G_MIX + 1, G_MIX + 1)
            with act.Fori(0, NB // 4) as i:
                for jj in range(2):
                    for c in range(PER):
                        m, k0 = PER * jj + c, G_MIX + 2 * (PER * jj + c)
                        p0 = 2 * (m % 2)
                        hi(i * (4 * PER) + (k0 + 2), k0 + 2)
                        if c == 1:
                            act.wait_ge(s_free, i * (2 * PER) + (PER * jj + 3))
                            for fb in range(2):
                                b = i * 4 + (2 * jj + fb)
                                last = A(sqt[:, fb, :], krv[:, bass.ds(b, 1), :].squeeze(1), ACT.Square,
                                         scale=vcol(V_KK, b))
                            last.then_inc(s_sq, 1)
                        if c == 2:
                            act.wait_ge(s_ss, i * 2 + (jj + 1))
                            A(inv[:, :, :].rearrange("p b q -> p (b q)"), ps[:, 4 + jj, :], ACT.Sqrt).then_inc(s_nrm, 1)
                        hi(i * (4 * PER) + (k0 + 3), k0 + 3)
                        act.wait_ge(s_used, i * (4 * PER) + (k0 + 2))
                        if c < 3:
                            for fb in range(2):
                                blk = i * 4 + (NB * c + 2 * jj + fb)
                                last = A(krv[:, bass.ds(blk, 1), :].squeeze(1), ps[:, p0 + fb, 0:S], ACT.Copy,
                                         scale=vcol(V_OMMU, blk))
                            last.then_inc(s_mix, 1)
                        else:
                            n = 2 * jj + c - 3
                            if n:
                                act.wait_ge(s_rotd, i * 4 + n)
                            for j in range(4):
                                o, s = 32 * j, 32 * (j ^ 1)
                                last = A(rot[o:o + 32, :, :], ps[s:s + 32, p0:p0 + 2, 0:S], ACT.Copy)
                            last.then_inc(s_rotc, 1)
            for m in range(2):
                g = G_VD + 4 * m
                for s in range(2, 6):
                    if g + s < G_OUT:
                        hi(g + s, g + s)
                act.wait_ge(s_used, g + 4)
                act.wait_ge(s_rotd, N_QK)
                for a in range(TT_):
                    A(vd[:, a, 512 * m:512 * m + 512], ps[:, 2 * m + a, :], ACT.Copy).then_inc(s_vdc, 1)
            act.wait_ge(s_lamd, 2)
            A(lam[:, 0:2], lam[:, 0:2], ACT.Exp).then_inc(s_lame, 1)

            for h in range(DH):
                act.wait_ge(s_smd, h + 1)
                for c in range(2):
                    for a in range(TT_):
                        o = (0, P)[a]
                        last = A(pr[:, c, o:o + P * (a + 1)], sm[:, c, o:o + P * (a + 1)], ACT.Exp,
                                 scale=HD ** -0.5, bias=nmx[:, 0, 2 * c + a:2 * c + a + 1],
                                 accum_out=sums[:, 0, 2 * c + a:2 * c + a + 1])
                last.then_inc(s_exp, 1)
                act.wait_ge(s_at, h + 1)
                A(attT[:, :], ps[:, 6, 0:3 * P], ACT.Copy).then_inc(s_atc, 1)
                act.wait_ge(s_o, h + 1)
                A(yt[:, h, :], ps[:, 7, 0:S], ACT.Copy).then_inc(s_oc, 1)
                A(osq[:, h, :], ps[:, 7, 0:S], ACT.Square).then_inc(s_osq, 1)
            act.wait_ge(s_oss, 1)
            A(oinv[:, :], ps[0:DH, 6, 0:S], ACT.Sqrt, scale=1.0 / P, bias=vec[0:DH, V_SUBEPS:V_SUBEPS + 1]
              ).then_inc(s_oss_read, 1)
            for n in range(12):
                act.wait_ge(s_tr, n + 1)
                dst = (vtm, btm, ktm)[n // 4]
                j = n % 4
                A(dst[:, 2 * j:2 * j + 2, :, :].rearrange("p b a q -> p (b a q)"), ps[:, n % 6, :], ACT.Copy
                  ).then_inc(s_trc, 1)
            for g in range(4):
                act.wait_ge(s_z1p, g + 1)
                A(z1[:, 2 * g:2 * g + 2, :, :].rearrange("p b a q -> p (b a q)"), ps[:, 4 * (g % 2) + 2, :], ACT.Copy
                  ).then_inc(s_z1, 1)
            for c in range(NC):
                a, cb = c // 2, C * (c % 2)
                for G in range(2):
                    act.wait_ge(s_u, 2 * c + G + 1)
                    A(um[cb:cb + C, 4 * G:4 * G + 4, a, :],
                      ps[cb:cb + C, 3 * G + 1, :].rearrange("p (b q) -> p b q", b=4), ACT.Copy).then_inc(s_uc, 1)
            def copied(g):
                act.wait_ge(s_y, g + 1)
                A(yf[:, 2 * g:2 * g + 2, :].rearrange("p b q -> p (b q)"), ps[:, 4 + g, :], ACT.Copy).then_inc(s_yc, 1)

            def squared(g):
                act.wait_ge(s_cen, g + 1)
                A(gsq[:, 2 * g:2 * g + 2, :], yf[:, 2 * g:2 * g + 2, :], ACT.Square).then_inc(s_gsq, 1)

            copied(0)
            copied(1)
            squared(0)
            copied(2)
            squared(1)
            copied(3)
            squared(2)
            hi(G_OUT, G_OUT)
            squared(3)
            act.wait_ge(s_var, 1)
            A(ginv[:, :], ps[0:2 * NB, 0, 0:S], ACT.Sqrt, scale=1.0 / HD, bias=vec[0:2 * NB, V_GNEPS:V_GNEPS + 1]
              ).then_inc(s_sd, 1)
            act.wait_ge(s_ydn, 4)
            A(shi[0][:, :], yt[:, 0, :], ACT.Copy).then_inc(s_ahi, 1)
            with act.Fori(0, KT // 4 - 1) as i:
                for k in range(4):
                    hi(i * 4 + (G_OUT + k + 1), G_OUT + k + 1)
                    split(yt[:, bass.ds(i * 4 + (k + 1), 1), :].squeeze(1), i * 4 + (G_OUT + k + 1), None, (k + 1) % 2)
            for k in range(KT - 4, KT - 1):
                hi(G_OUT + k + 1, G_OUT + k + 1)
                split(yt[:, k + 1, :], G_OUT + k + 1, None, (k + 1) % 2)

            def root(n, a):
                act.wait_ge(s_ln, TT_ * n + a + 1)
                A(moments[a][:, 2:3], moments[a][:, 1:2], ACT.Sqrt, bias=col(V_LNEPS)).then_inc(s_std, 1)

            def normalise(n, a):
                act.wait_ge(s_rs, TT_ * n + a + 1)
                for q in range(4):
                    x = xres[:, a, 512 * q:512 * q + 512]
                    A(x, x, ACT.Identity, scale=moments[a][:, 2:3], bias=moments[a][:, 3:4]).then_inc(s_nrmq, 1)

            hi(G_FF1, G_FF1)
            root(0, 0)
            normalise(0, 0)
            root(0, 1)
            normalise(0, 1)
            for n in range(8):
                act.wait_ge(s_xt, n + 1)
                a, j = n // 4, n % 4
                A(acthi[:, 4 * j:4 * j + 4, tok(a)], ps[:, n, :].rearrange("p (k q) -> p k q", k=4), ACT.Copy
                  ).then_inc(s_x1h, 1)
            hi(G_FF1 + 1, G_FF1 + 1)
            def ff1(i, k, last=False):
                k0 = G_FF1 + 2 * k
                hi(i * 4 + (k0 + 2), k0 + 2)
                if not last:
                    hi(i * 4 + (k0 + 3), k0 + 3)
                act.wait_ge(s_used, i * 4 + (k0 + 2))
                A(hid[:, bass.ds(i * 4 + 2 * k, 2), :], ps[:, 2 * k:2 * k + 2, 0:S], ACT.Relu).then_inc(s_relu, 1)

            with act.Fori(0, N_FF1 // 2 - 1) as i:
                for k in range(2):
                    ff1(i, k)
            for k in range(2):
                ff1(N_FF1 // 2 - 1, k, k == 1)
            act.wait_ge(s_ff, 1)
            A(shi[0][:, :], hid[:, 0, :], ACT.Copy).then_inc(s_ahi, 1)
            NF = DFF // P
            act.wait_ge(s_ff, N_FF1)
            with act.Fori(0, NF // 4 - 1) as i:
                for k in range(4):
                    hi(i * 4 + (G_FF2 + k + 1), G_FF2 + k + 1)
                    split(hid[:, bass.ds(i * 4 + (k + 1), 1), :].squeeze(1), i * 4 + (G_FF2 + k + 1), None, (k + 1) % 2)
            for k in range(NF - 4, NF - 1):
                hi(G_FF2 + k + 1, G_FF2 + k + 1)
                split(hid[:, k + 1, :], G_FF2 + k + 1, None, (k + 1) % 2)
            for a in range(TT_):
                root(1, a)
                normalise(1, a)

        @block.vector
        def _(dve):
            TTn, TS, STT = dve.tensor_tensor, dve.tensor_scalar, dve.scalar_tensor_tensor

            def lo(g, k0):
                dve.wait_ge(s_hi, g + 1)
                if not (isinstance(g, int) and g < 2):
                    dve.wait_ge(s_used, g - 1)
                TTn(wlo[k0 % NHL][:, :], stage[k0 % NST][:, :], f(whi[k0 % NHL][:, :]), ALU.subtract
                    ).then_inc(s_lo, 1)

            def mix(out, acc, mu):
                return STT(out[:, 1:S], acc[:, 0:S - 1], mu, out[:, 1:S], ALU.mult, ALU.add)

            def x_lo(j):
                dve.wait_ge(s_xhi, j + 1)
                TTn(actlo[:, 4 * j:4 * j + 4, :], xstage[:, 4 * j:4 * j + 4, :], f(acthi[:, 4 * j:4 * j + 4, :]),
                    ALU.subtract).then_inc(s_xlo, 1)

            dve.memset(wt[64:65, :], 1.0)
            x_lo(0)
            lo(0, 0)
            for j in range(1, 4):
                x_lo(j)
            lo(1, 1)
            dve.wait_ge(s_vecl, 16)
            TS(vec[:, V_OMMU:V_OMMU + 27], vec[:, V_MU:V_MU + 27], -1.0, 1.0, ALU.mult, ALU.add)
            TS(vec[:, V_OMKA:V_OMKA + 8], vec[:, V_KA:V_KA + 8], -1.0, 1.0, ALU.mult, ALU.add)
            TS(vec[:, V_G08:V_G08 + 1], vec[:, V_SG:V_SG + 1], 1.0 - LAMBDA_INIT, None, ALU.mult).then_inc(s_vec, 1)
            lo(2, 2)
            dve.wait_ge(s_mix, 1)
            mix(wa, ps[:, 0, :], col(V_MU, 24))
            mix(sg[0], ps[:, 1, :], col(V_MU, 25)).then_inc(s_free, 1)
            lo(3, 3)
            dve.wait_ge(s_mix, 2)
            mix(sg[1], ps[:, 2, :], col(V_MU, 26)).then_inc(s_free, 1)
            dve.wait_ge(s_pos, 16)
            MAGIC = 1.5 * 2 ** 23
            n = 0

            def ang(ins):
                nonlocal n
                n += 1
                ins.then_inc(s_ang, 1)
                dve.wait_ge(s_ang, n)

            ang(dve.tensor_copy(angt[0][:, :], posi[:, :]))
            ang(TS(angt[0][:, :], angt[0][:, :], col(V_INVF), None, ALU.mult))
            ang(TS(angt[1][:, :], angt[0][:, :], 1.0 / (2.0 * math.pi), MAGIC, ALU.mult, ALU.add))
            ang(TS(angt[1][:, :], angt[1][:, :], MAGIC, None, ALU.subtract))
            for part in (6.28125, 2029.0 / 2 ** 20, 2.0 * math.pi - 6.28125 - 2029.0 / 2 ** 20):
                ang(STT(angt[0][:, :], angt[1][:, :], -part, angt[0][:, :], ALU.mult, ALU.add))
            ang(TS(angt[0][:, :], angt[0][:, :], 3.1415925, -3.1415925, ALU.min, ALU.max))
            dve.wait_ge(s_ang, 8)
            STT(angt[2][:, :], angt[0][:, :], -1.0, angt[0][:, :], ALU.mult, ALU.max).then_inc(s_tab, 1)
            dve.wait_ge(s_tab, 1)
            TS(angt[2][:, :], angt[2][:, :], -1.0, math.pi / 2, ALU.mult, ALU.add).then_inc(s_ang, 1)
            dve.wait_ge(s_sin, 1)
            TS(sinb[:, :], sinb[:, :], col(V_SIGN), None, ALU.mult).then_inc(s_tab, 1)
            dve.wait_ge(s_itemd, 16)
            dve.tensor_copy(gam[:, :, :].rearrange("p b c -> p (b c)").rearrange("p (m c) -> p m c", c=2),
                            kr[:, :, :, 1, C - 1::C].rearrange("p b a c -> p (b a) c")).then_inc(s_gam, 1)
            dve.wait_ge(s_tab, 2)
            dve.wait_ge(s_sin, 2)
            dve.wait_ge(s_gam, 1)
            lo(G_MIX + 1, G_MIX + 1)
            with dve.Fori(0, NB // 4) as i:
                for jj in range(2):
                    def pair(x, o=0):
                        return x[:, bass.ds(i * 4 + (2 * jj + o), 2), :]

                    def one(x, fb, o=0):
                        return x[:, bass.ds(i * 4 + (2 * jj + fb + o), 1), :].squeeze(1)

                    K, R, V, E = pair(krv), pair(krv, NB), pair(krv, 2 * NB), i * 10 + 5 * jj
                    for c in range(PER):
                        m, k0 = PER * jj + c, G_MIX + 2 * (PER * jj + c)
                        p0 = 2 * (m % 2)
                        if c == 1:
                            for fb in range(2):
                                b = i * 4 + (2 * jj + fb)
                                last = TS(one(ki, fb), one(bt, fb), vcol(V_KA, b), vcol(V_OMKA, b), ALU.mult, ALU.add)
                            last.then_inc(s_ew, 1)
                            dve.wait_ge(s_ew, E + 1)
                            dve.wait_ge(s_free, i * (2 * PER) + (PER * jj + 3))
                            TTn(pair(ki), K, pair(ki), ALU.mult).then_inc(s_ew, 1)
                        if c == 2:
                            dve.wait_ge(s_ew, E + 2)
                            dve.wait_ge(s_free, i * (2 * PER) + (PER * jj + 4))
                            for fb in range(2):
                                last = STT(rkt_[:, fb, :], one(krv, fb, NB), vcol(V_RK, i * 4 + (2 * jj + fb)),
                                           one(ki, fb), ALU.mult, ALU.mult)
                            last.then_inc(s_rk, 1)
                            rt = kr[:, bass.ds(i * 4 + 2 * jj, 2), :, 1, :]
                            TTn(rt, rt, R.rearrange("p b (a q) -> p b a q", a=TT_), ALU.mult)
                        lo(i * (4 * PER) + (k0 + 2), k0 + 2)
                        if c == 2:
                            dve.wait_ge(s_nrm, i * 2 + (jj + 1))
                            TS(inv[:, :, :], inv[:, :, :], 1e-12, None, ALU.max).then_inc(s_ew, 1)
                            dve.wait_ge(s_ew, E + 3)
                            dve.reciprocal(inv[:, 0, :], inv[:, 0, :]).then_inc(s_ew, 1)
                        if c == 3:
                            dve.reciprocal(inv[:, 1, :], inv[:, 1, :]).then_inc(s_ew, 1)
                            dve.wait_ge(s_ew, E + 5)
                            for fb in range(2):
                                last = STT(one(krv, fb), one(krv, fb), vcol(V_KK, i * 4 + (2 * jj + fb)),
                                           inv[:, fb, :], ALU.mult, ALU.mult)
                            last.then_inc(s_kk, 1)
                        if c == 4:
                            dve.wait_ge(s_bon, i * 2 + (jj + 1))
                            dve.wait_ge(s_free, i * (2 * PER) + (PER * jj + 5))
                            TTn(R, V, ps[:, 6 + jj, :].rearrange("p (b q) -> p b q", b=2), ALU.mult).then_inc(s_bonv, 1)
                        lo(i * (4 * PER) + (k0 + 3), k0 + 3)
                        if c < 3:
                            dve.wait_ge(s_mix, i * 6 + (3 * jj + c + 3))
                            for fb in range(2):
                                blk = i * 4 + (NB * c + 2 * jj + fb)
                                out = krv[:, bass.ds(blk, 1), 1:S].squeeze(1)
                                last = STT(out, ps[:, p0 + fb, 0:S - 1], vcol(V_MU, blk), out, ALU.mult, ALU.add)
                            last.then_inc(s_free, 1)
                        else:
                            n = 2 * jj + c - 3
                            dve.wait_ge(s_rotc, i * 4 + (n + 1))
                            out = qk[:, bass.ds(i * 8 + 2 * n, 2), :]
                            TTn(out, ps[:, p0:p0 + 2, 0:S], over(cosb[:, :], 2), ALU.mult).then_inc(s_free, 1)
                            TTn(rot[:, :, :], rot[:, :, :], over(sinb[:, :], 2), ALU.mult).then_inc(s_rotm, 1)
                            dve.wait_ge(s_rotm, i * 4 + (n + 1))
                            dve.wait_ge(s_free, i * (2 * PER) + (m + 3))
                            TTn(out, out, rot[:, :, :], ALU.add).then_inc(s_rotd, 1)
            for g in range(G_VD + 2, G_OUT):
                lo(g, g)
            dve.wait_ge(s_attc, 80)
            for j in range(2):
                dve.tensor_tensor_reduce(lamt[:, j, :], lamv[:, 2 * j, :], lamv[:, 2 * j + 1, :], 1.0, 0.0,
                                         ALU.mult, ALU.add, lam[:, j:j + 1]).then_inc(s_lamd, 1)
            dve.wait_ge(s_lame, 1)
            TTn(lam[:, 2:3], lam[:, 1:2], lam[:, 0:1], ALU.subtract).then_inc(s_lamd, 1)
            dve.wait_ge(s_lamd, 3)
            TS(lam[:, 3:4], lam[:, 2:3], LAMBDA_INIT, None, ALU.subtract).then_inc(s_lamd, 1)
            dve.wait_ge(s_lamd, 4)

            ad = 0

            def attention(h, part):
                nonlocal ad

                def link(ins):
                    nonlocal ad
                    ad += 1
                    ins.then_inc(s_attd, 1)
                    dve.wait_ge(s_attd, ad)

                if part == 0:
                    dve.wait_ge(s_sc, h + 1)
                    for c in range(2):
                        for a in range(TT_):
                            o = (0, P)[a]
                            last = dve.tensor_tensor_reduce(
                                sm[:, c, o:o + P * (a + 1)], ps[:, 6 + c, o:o + P * (a + 1)],
                                amask[:, o:o + P * (a + 1)], 1.0, -3e38, ALU.add, ALU.max,
                                mx[:, 0, 2 * c + a:2 * c + a + 1])
                    link(last)
                    TS(nmx[:, 0, :], mx[:, 0, :], -HD ** -0.5, None, ALU.mult).then_inc(s_smd, 1)
                elif part == 3:
                    dve.wait_ge(s_exp, h + 1)
                    link(dve.reciprocal(coef[:, 0, :], sums[:, 0, :]))
                    TS(coef[:, 0, 2:4], coef[:, 0, 2:4], lam[:, 3:4], None, ALU.mult)
                    for a in range(TT_):
                        o = (0, P)[a]
                        last = TS(att[:, o:o + P * (a + 1)], pr[:, 0, o:o + P * (a + 1)], coef[:, 0, a:a + 1], None,
                                  ALU.mult)
                    link(last)
                    for a in range(TT_):
                        o = (0, P)[a]
                        last = STT(att[:, o:o + P * (a + 1)], pr[:, 1, o:o + P * (a + 1)],
                                   coef[:, 0, 2 + a:3 + a], att[:, o:o + P * (a + 1)], ALU.mult, ALU.add)
                    last.then_inc(s_attn, 1)

            def level_x(n):
                half, lev, s = STEPS[n]
                bk, u, uh = 2 * (n % 3), slice(4 * s, 4 * s + 4), TTh[half]
                ab = ps[:, bk, :].rearrange("p (u q) -> p u q", q=P)
                bb = ps[:, bk + 1, :].rearrange("p (u q) -> p u q", q=P)
                dve.wait_ge(s_px, n + 1)
                if lev == 0:
                    STT(TM[:, u, :], ab, -1.0, over(M1, 4), ALU.mult, ALU.mult)
                    STT(uh[:, u, :], bb, -1.0, over(M1T, 4), ALU.mult, ALU.mult)
                    TTn(AT[:, u, :], bb, over(SU, 4), ALU.mult).then_inc(s_xm, 1)
                elif lev == READ:
                    ur = slice(16 * half + 4 * s, 16 * half + 4 * s + 4)
                    TTn(rbt[:, ur, :], ab, over(IU, 4), ALU.mult)
                    TTn(rkt[:, ur, :], bb, over(IU, 4), ALU.mult).then_inc(s_xm, 1)
                else:
                    TTn(XM[:, u, :], ab, over(levc[:, lev, :], 4), ALU.mult).then_inc(s_xm, 1)

            def level_t(n):
                half, lev, s = STEPS[n]
                if lev in (0, READ):
                    return
                bk, u = 2 * (n % 3), slice(4 * s, 4 * s + 4)
                ab = ps[:, bk, :].rearrange("p (u q) -> p u q", q=P)
                bb = ps[:, bk + 1, :].rearrange("p (u q) -> p u q", q=P)
                tm, tt = TM[:, u, :], TTh[half][:, u, :]
                dve.wait_ge(s_ptx, updates(n))
                if lev < 5:
                    TTn(tm, tm, ab, ALU.subtract)
                    TTn(tt, tt, bb, ALU.subtract).then_inc(s_upd, 1)
                else:
                    TTn(tt, bb, tt, ALU.subtract).then_inc(s_upd, 1)

            dve.wait_ge(s_levc, 16)
            level_x(0)
            for n in range(len(STEPS)):
                if n + 1 < len(STEPS):
                    level_x(n + 1)
                level_t(n)
                attention(n // PER_HEAD, n % PER_HEAD)
            for g in range(4):
                dve.wait_ge(s_kb, g + 1)
                if g >= 2:
                    dve.wait_ge(s_z1p, g - 1)
                TTn(kbt[g % 2][:, :, :], banks(4 * (g % 2)).rearrange("p h (u q) -> p (h u) q", q=P), over(SU, 8),
                    ALU.mult).then_inc(s_kbm, 1)
            dve.wait_ge(s_oss_read, 1)
            dve.reciprocal(oinv[:, :], oinv[:, :]).then_inc(s_ord, 1)

            def head_norm(p):
                dve.wait_ge(s_spr, p + 1)
                y = yt[:, 2 * p:2 * p + 2, :]
                STT(y, y, col(V_G08), ps[:, 6 + p % 2, :].rearrange("p (h q) -> p h q", h=2), ALU.mult, ALU.mult
                    ).then_inc(s_ydn, 1)

            dve.wait_ge(s_gm, 3)
            dve.wait_ge(s_z1, 4)
            for c in range(NC):
                a, cb = c // 2, C * (c % 2)
                if c:
                    for G in range(2):
                        dve.wait_ge(s_ks, 2 * (c - 1) + G + 1)
                        z = z1[cb:cb + C, 4 * G:4 * G + 4, a, :]
                        TTn(z, ps[cb:cb + C, 3 * G, :].rearrange("p (b q) -> p b q", b=4), z, ALU.add
                            ).then_inc(s_zc, 1)
                head_norm(c)
                if c == NC - 1:
                    break
                for G in range(2):
                    dve.wait_ge(s_sp, 2 * c + G + 1)
                    bs = slice(4 * G, 4 * G + 4)
                    pp = ps[:, 3 * G + 2, :].rearrange("p (b q) -> p b q", b=4)
                    if c == 0:
                        TTn(st[1][:, bs, :], pp, gm[0][:, bs, :], ALU.mult).then_inc(s_st, 1)
                    else:
                        TTn(st[c + 1][:, bs, :], pp, st[c][:, bs, :], ALU.add).then_inc(s_stm, 1)
                        dve.wait_ge(s_stm, 2 * (c - 1) + G + 1)
                        TTn(st[c + 1][:, bs, :], st[c + 1][:, bs, :], gm[c][:, bs, :], ALU.mult).then_inc(s_st, 1)
            def centred(g):
                y512 = yf[:, 2 * g:2 * g + 2, :].rearrange("p b q -> p (b q)")
                dve.wait_ge(s_mean, g + 1)
                STT(y512, ps[:, g, :], -1.0 / HD, y512, ALU.mult, ALU.add).then_inc(s_cen, 1)

            def finished(g):
                bl = slice(2 * g, 2 * g + 2)
                dve.wait_ge(s_bc, g + 1)
                TTn(yf[:, bl, :], yf[:, bl, :], ps[:, g, :].rearrange("p (b q) -> p b q", b=2), ALU.mult).then_inc(s_gn, 1)
                dve.wait_ge(s_gn, 2 * g + 1)
                for b in range(2 * g, 2 * g + 2):
                    last = STT(yf[:, b, :], yf[:, b, :], col(V_GG, b), krv[:, NB + b, :], ALU.mult, ALU.add)
                last.then_inc(s_gn, 1)
                dve.wait_ge(s_gn, 2 * g + 2)
                dve.wait_ge(s_gate, g + 1)
                for j in range(2):
                    b = 2 * g + j
                    last = STT(yt[:, DH + b, :], yf[:, b, :], col(V_GB, b), ps[:, 4 + g, S * j:S * j + S], ALU.add,
                               ALU.mult)
                last.then_inc(s_yg, 1)

            for g in range(4):
                centred(g)
            dve.wait_ge(s_sd, 1)
            dve.reciprocal(ginv[:, :], ginv[:, :]).then_inc(s_ginv, 1)

            def split(src, n, h, used):
                dve.wait_ge(s_ahi, n + 1)
                if used is not None:
                    dve.wait_ge(s_used, used)
                TTn(slo[h][:, :], src, f(shi[h][:, :]), ALU.subtract).then_inc(s_alo, 1)

            dve.wait_ge(s_gate, 4)
            split(yt[:, 0, :], 0, 0, None)
            for g in range(4):
                finished(g)
            dve.wait_ge(s_lo, G_OUT + 1)
            with dve.Fori(0, KT // 4 - 1) as i:
                for k in range(4):
                    lo(i * 4 + (G_OUT + k + 1), G_OUT + k + 1)
                    split(yt[:, bass.ds(i * 4 + (k + 1), 1), :].squeeze(1), i * 4 + (k + 1), (k + 1) % 2,
                          i * 4 + (G_OUT + k))
            for k in range(KT - 4, KT - 1):
                lo(G_OUT + k + 1, G_OUT + k + 1)
                split(yt[:, k + 1, :], k + 1, (k + 1) % 2, G_OUT + k)

            chain = 0

            def link(ins):
                nonlocal chain
                chain += 1
                ins.then_inc(s_lnk, 1)
                dve.wait_ge(s_lnk, chain)

            def add_and_measure(n, a, q):
                if (a, q) == (TT_ - 1, 3):
                    dve.wait_ge(s_used, (G_FF1, G_END)[n])
                else:
                    dve.wait_ge(s_row, 7 * n + 4 * a + q + 1)
                x = xres[:, a, 512 * q:512 * q + 512]
                link(STT(x, x, ALPHA, ps[:, 4 * a + q, :], ALU.mult, ALU.add))
                return dve.bn_stats(stats[a][:, q, :], x)

            def scales(n, a, last):
                m = moments[a]
                link(last)
                dve.bn_aggr(m[:, 0:2], stats[a][:, :, :]).then_inc(s_ln, 1)
                dve.wait_ge(s_std, TT_ * n + a + 1)
                link(dve.reciprocal(m[:, 2:3], m[:, 2:3]))
                STT(m[:, 3:4], m[:, 0:1], -1.0, m[:, 2:3], ALU.mult, ALU.mult).then_inc(s_rs, 1)

            def gained(n, q, gain, bias):
                x, cols = xres[:, 1, 512 * q:512 * q + 512], slice(512 * q, 512 * q + 512)
                dve.wait_ge(s_nrmq, 8 * n + 4 + q + 1)
                TTn(x, x, gain[:, cols], ALU.mult).then_inc(s_gq, 1)
                dve.wait_ge(s_gq, 4 * n + q + 1)
                TTn(x, x, bias[:, cols], ALU.add).then_inc(s_lnd, 1)

            def layer_norm(n, gain, bias):
                for a in range(TT_):
                    for q in range(4):
                        last = add_and_measure(n, a, q)
                    scales(n, a, last)
                for q in range(4):
                    gained(n, q, gain, bias)

            def x1_low(n):
                dve.wait_ge(s_x1h, n + 1)
                a, j = n // 4, n % 4
                TTn(actlo[:, 4 * j:4 * j + 4, tok(a)], ps[:, n, :].rearrange("p (k q) -> p k q", k=4),
                    f(acthi[:, 4 * j:4 * j + 4, tok(a)]), ALU.subtract).then_inc(s_x1l, 1)

            dve.wait_ge(s_xres, 16)
            dve.wait_ge(s_ln1c, 32)
            layer_norm(0, gain1, bias1)
            for n in range(8):
                x1_low(n)
            dve.wait_ge(s_lo, G_FF1 + 1)
            lo(G_FF1 + 1, G_FF1 + 1)
            def ff1(i, k, last=False):
                k0 = G_FF1 + 2 * k
                lo(i * 4 + (k0 + 2), k0 + 2)
                if not last:
                    lo(i * 4 + (k0 + 3), k0 + 3)
                dve.wait_ge(s_relu, i * 2 + (k + 1))
                h2 = hid[:, bass.ds(i * 4 + 2 * k, 2), :]
                TTn(h2, ps[:, 2 * k:2 * k + 2, 0:S], h2, ALU.mult).then_inc(s_ff, 1)

            with dve.Fori(0, N_FF1 // 2 - 1) as i:
                for k in range(2):
                    ff1(i, k)
            for k in range(2):
                ff1(N_FF1 // 2 - 1, k, k == 1)
            NF = DFF // P
            split(hid[:, 0, :], KT, 0, None)
            with dve.Fori(0, NF // 4 - 1) as i:
                for k in range(4):
                    lo(i * 4 + (G_FF2 + k + 1), G_FF2 + k + 1)
                    split(hid[:, bass.ds(i * 4 + (k + 1), 1), :].squeeze(1), i * 4 + (KT + k + 1), (k + 1) % 2,
                          i * 4 + (G_FF2 + k))
            for k in range(NF - 4, NF - 1):
                lo(G_FF2 + k + 1, G_FF2 + k + 1)
                split(hid[:, k + 1, :], KT + k + 1, (k + 1) % 2, G_FF2 + k)
            dve.wait_ge(s_ln2c, 32)
            layer_norm(1, gain2, bias2)

        @block.gpsimd
        def _(pool):
            PT = pool.tensor_tensor
            with pool.Fori(0, NB // 2) as j:
                def pair(x):
                    return x[:, bass.ds(j * 2, 2), :]

                kk, bb, kb_, e = pair(krv), pair(bt), pair(ki), pair(e2)
                kt = kr[:, bass.ds(j * 2, 2), :, 0, :]
                pool.wait_ge(s_kk, j + 1)
                PT(bb, bb, kk, ALU.mult).then_inc(s_pl, 1)
                PT(kt, kt, kk.rearrange("p b (a q) -> p b a q", a=TT_), ALU.mult).then_inc(s_pl, 1)
                pool.wait_ge(s_pl, j * 4 + 2)
                PT(bb, bb, e, ALU.mult).then_inc(s_pl, 1)
                PT(kb_, kb_, e, ALU.mult).then_inc(s_pl, 1)
            for q in range(8):
                u = slice(4 * (q % 4), 4 * (q % 4) + 4)
                n = STEPS.index((q // 4, 0, q % 4))
                pool.wait_ge(s_xm, n + 1)
                PT(TM[:, u, :], TM[:, u, :], over(ID, 4), ALU.add)
                tt = TTh[q // 4][:, u, :]
                PT(tt, tt, over(ID, 4), ALU.add).then_inc(s_init, 1)
            for c in range(3):
                if c == 0:
                    pool.wait_ge(s_tr, 4)
                if c == 2:
                    pool.wait_ge(s_upd, updates(len(STEPS) - 1))
                PT(gm[c][:, :, :], over(BD, NB), gam[:, :, c:c + 1].broadcast_to([P, NB, P]), ALU.mult
                   ).then_inc(s_gm, 1)

            pool.wait_ge(s_hi, G_OUT + 1)
            PT(wlo[G_OUT % NHL][:, :], stage[G_OUT % NST][:, :], f(whi[G_OUT % NHL][:, :]), ALU.subtract
               ).then_inc(s_lo, 1)
            pool.wait_ge(s_hi, G_FF1 + 1)
            pool.wait_ge(s_stage[(G_FF1 + 3) % NST], 16 * ((G_FF1 + 3) // NST + 1))
            PT(wlo[G_FF1 % NHL][:, :], stage[G_FF1 % NST][:, :], f(whi[G_FF1 % NHL][:, :]), ALU.subtract
               ).then_inc(s_lo, 1)

            def gained(n, gain, bias):
                for q in range(4):
                    x, cols = xres[:, 0, 512 * q:512 * q + 512], slice(512 * q, 512 * q + 512)
                    pool.wait_ge(s_nrmq, 8 * n + q + 1)
                    PT(x, x, gain[:, cols], ALU.mult).then_inc(s_pg, 1)
                    pool.wait_ge(s_pg, 4 * n + q + 1)
                    PT(x, x, bias[:, cols], ALU.add).then_inc(s_lnp, 1)

            pool.wait_ge(s_ln1c, 32)
            gained(0, gain1, bias1)
            pool.wait_ge(s_ln2c, 32)
            gained(1, gain2, bias2)

OUT_SHAPE = (1, S, D)


def layout(inputs):
    a = {k: np.asarray(v) for k, v in inputs.items()}
    w_in = a["w_in"][0]

    def cut(w, c0, width, slabs):
        piece = w[:, c0:c0 + width].reshape(slabs, KT // slabs, P, width)
        return piece.transpose(0, 2, 1, 3).reshape(slabs, P, -1)

    slabs = [cut(w_in, 3 * RW, 256, 2), cut(w_in, RCOLS - P, P, 1)]
    for j in range(RW // 256):
        slabs += [cut(w_in, base + 256 * j, 256, 2) for base in (RW, 0, 2 * RW)]
        slabs += [cut(w_in, RCOLS + 256 * n, 256, 2) for n in (2 * j, 2 * j + 1)]
    slabs += [cut(w_in, RCOLS + 2 * RW + 512 * j, 512, 4) for j in range(2)]
    ff1 = np.concatenate([cut(a["w_ff1"][0], 256 * j, 256, 2) for j in range(N_FF1)])

    def blocks(v):
        return np.asarray(v).reshape(-1, P).T

    mu = a["mu_shift"][0]
    inv_freq = np.float32(10000.0) ** (-np.arange(0, HD, 2, dtype=np.float32) / np.float32(HD))
    vecs = np.concatenate([
        blocks(mu[RW:2 * RW]), blocks(mu[0:RW]), blocks(mu[2 * RW:3 * RW]),
        blocks(mu[3 * RW:3 * RW + 2 * P]), blocks(mu[RCOLS - P:RCOLS]),
        blocks(a["rwkv_k_k"][0]), blocks(a["rwkv_k_a"][0]), blocks(a["rwkv_r_k"][0].reshape(-1)),
        blocks(a["rwkv_a0"][0]), blocks(a["rwkv_gn_gain"][0]), blocks(a["rwkv_gn_bias"][0]),
        a["diff_subln_gain"][0].reshape(P, 1),
        np.tile(inv_freq, 4).reshape(P, 1).astype(np.float32),
        np.tile(np.repeat(np.array([-1.0, 1.0], np.float32), 32), 2).reshape(P, 1),
        np.full((P, 1), GN_EPS, np.float32), np.full((P, 1), SUB_EPS, np.float32),
        np.full((P, 1), LN_EPS, np.float32)], axis=1)
    g_up = a["rwkv_g_up"][0]
    gup = np.zeros((P, 2, RW), np.float32)
    gup[:, 0, :] = g_up[0:P]
    gup[P - (LORA_G - P):, 1, :] = g_up[P:LORA_G]
    x = a["x"][0]
    out = {
        "x": x, "xT": x.T.reshape(KT, P, S).transpose(1, 0, 2),
        "positions": a["positions"].astype(np.int32).reshape(1, S),
        "w_in": np.concatenate(slabs), "w_out": np.roll(a["w_out"][0].reshape(KT, P, D), DH, axis=0), "w_ff1": ff1,
        "w_ff2": a["w_ff2"][0].reshape(DFF // P, P, D), "vecs": vecs, "consts": shape_constants(),
        "w_up": np.concatenate([a["rwkv_w_up"][0], a["rwkv_w0"]]), "a_up": a["rwkv_a_up"][0], "g_up": gup,
        "lam": np.concatenate([a["diff_lambda_q1"], a["diff_lambda_k1"], a["diff_lambda_q2"], a["diff_lambda_k2"]]),
        "ln1_gain": a["ln1_gain"], "ln1_bias": a["ln1_bias"], "ln2_gain": a["ln2_gain"], "ln2_bias": a["ln2_bias"],
    }
    return {k: np.ascontiguousarray(v) for k, v in out.items()}


def kernel(**inputs):
    import concourse.bacc as bacc
    from concourse.bass_utils import run_bass_kernel_spmd

    nc = bacc.Bacc("TRN2", target_bir_lowering=False, num_devices=1)
    arrays = layout(inputs)
    t = {n: nc.dram_tensor(n, a.shape, mybir.dt.from_np(a.dtype), kind="ExternalInput").ap()
         for n, a in arrays.items()}
    t["out"] = nc.dram_tensor("out", (S, D), F32, kind="ExternalOutput").ap()
    build(nc, t)
    r = run_bass_kernel_spmd(nc, [arrays], core_ids=[0])
    return r.results[0]["out"].reshape(OUT_SHAPE)
```
